# Optimizing a Trainium2 kernel written in Bass

```python
import math
import jax, jax.numpy as jnp
from jax import lax
import numpy as np

D_MODEL = 1024
BATCH = 1
SEQ = 512
DEPTH = 2

GDN_HEADS = 8
GDN_HEAD_DIM = 64
GDN_WIDTH = GDN_HEADS * GDN_HEAD_DIM
GDN_CONV = 4
GDN_CHUNK = 64
MLA_HEADS = 8
MLA_Q_RANK = 256
MLA_KV_RANK = 128
MLA_NOPE = 64
MLA_ROPE = 32
MLA_QK = MLA_NOPE + MLA_ROPE
MLA_V = 64
MLA_WIDTH = MLA_HEADS * MLA_V
ROPE_THETA = 10000.0
Q_BLOCK = 128
NEG_INF = -1e30
IN_SPLITS = (GDN_WIDTH, GDN_WIDTH, GDN_WIDTH, GDN_WIDTH, GDN_HEADS, GDN_HEADS, MLA_Q_RANK, MLA_KV_RANK, MLA_ROPE)
IN_COLS = sum(IN_SPLITS)
MIX_WIDTH = GDN_WIDTH + MLA_WIDTH
RWKV_HEADS = 16
RWKV_HEAD_DIM = 64
DECAY_LORA = 64
AAA_LORA = 64
GATE_LORA = 160
RWKV_GN_EPS = 64e-5
D_FF = 4 * D_MODEL
EPS = 1e-6

kernel_name = "hybrid_gdn_mla_rwkv7_adaln"

def rms_norm(t):
    tf = t.astype(jnp.float32)
    return (tf * lax.rsqrt(jnp.mean(tf * tf, axis=-1, keepdims=True) + EPS)).astype(t.dtype)

def l2_normalize(t):
    tf = t.astype(jnp.float32)
    return (tf * lax.rsqrt(jnp.sum(tf * tf, axis=-1, keepdims=True) + 1e-12)).astype(t.dtype)

def adaln(t, shift, scale):
    return rms_norm(t) * (1 + scale[:, None, :]) + shift[:, None, :]

def split_columns(t, sizes):
    offsets = []
    total = 0
    for s in sizes[:-1]:
        total += s
        offsets.append(total)
    return jnp.split(t, offsets, axis=-1)

def causal_depthwise_conv(t, w):
    K = w.shape[0]
    S = t.shape[1]
    tp = jnp.pad(t, ((0, 0), (K - 1, 0), (0, 0)))
    out = tp[:, 0:S] * w[0]
    for j in range(1, K):
        out = out + tp[:, j:j + S] * w[j]
    return out

def rope_tables(positions):
    inv_freq = ROPE_THETA ** (-jnp.arange(0, MLA_ROPE, 2, dtype=jnp.float32) / MLA_ROPE)
    ang = positions.astype(jnp.float32)[..., None] * inv_freq
    return jnp.cos(ang)[:, :, None, :], jnp.sin(ang)[:, :, None, :]

def apply_rope_tail(t, cos, sin):
    t_pass, t_rot = t[..., :MLA_NOPE], t[..., MLA_NOPE:]
    x1, x2 = jnp.split(t_rot.astype(jnp.float32), 2, axis=-1)
    rot = jnp.concatenate([x1 * cos - x2 * sin, x2 * cos + x1 * sin], axis=-1).astype(t.dtype)
    return jnp.concatenate([t_pass, rot], axis=-1)

def chunked_gated_delta_rule(q, k, v, g, beta):
    B, S, H, Dk = q.shape
    Dv = v.shape[-1]
    C = GDN_CHUNK
    N = S // C
    f32 = jnp.float32

    def to_chunks(t):
        t = t.astype(f32).reshape((B, N, C, H) + t.shape[3:])
        return jnp.moveaxis(t, 3, 1)

    q = to_chunks(q) * (Dk ** -0.5)
    k = to_chunks(k)
    v = to_chunks(v)
    beta = to_chunks(beta)
    g = jnp.cumsum(to_chunks(g), axis=-1)
    causal = jnp.tril(jnp.ones((C, C), dtype=bool))
    strict = jnp.tril(jnp.ones((C, C), dtype=bool), -1)
    gdiff = g[..., :, None] - g[..., None, :]
    decay = jnp.where(causal, jnp.exp(jnp.where(causal, gdiff, 0.0)), 0.0)
    k_beta = k * beta[..., None]
    L = jnp.where(strict, jnp.einsum('bhnid,bhnjd->bhnij', k_beta, k) * decay, 0.0)
    eye = jnp.eye(C, dtype=f32)
    T = lax.linalg.triangular_solve(eye + L, jnp.broadcast_to(eye, L.shape),
                                    left_side=True, lower=True, unit_diagonal=True)
    u = T @ (v * beta[..., None])
    w = T @ (k_beta * jnp.exp(g)[..., None])
    qk = jnp.where(causal, jnp.einsum('bhnid,bhnjd->bhnij', q, k) * decay, 0.0)
    g_last = g[..., -1]
    q_dec = q * jnp.exp(g)[..., None]
    k_dec = k * jnp.exp(g_last[..., None] - g)[..., None]

    def step(state, inp):
        q_i, k_i, w_i, u_i, qk_i, gl_i = inp
        v_new = u_i - w_i @ state
        o_i = q_i @ state + qk_i @ v_new
        state = state * jnp.exp(gl_i)[..., None, None] + jnp.swapaxes(k_i, -1, -2) @ v_new
        return state, o_i

    xs = tuple(jnp.moveaxis(t, 2, 0) for t in (q_dec, k_dec, w, u, qk, g_last))
    state0 = jnp.zeros((B, H, Dk, Dv), f32)
    _, o = lax.scan(step, state0, xs)
    return o.transpose(1, 0, 3, 2, 4).reshape(B, S, H, Dv)

def causal_block_attention(q, k, v):
    B, S, H, Dqk = q.shape
    Dv = v.shape[-1]
    nb = S // Q_BLOCK
    q_blocks = jnp.moveaxis(q.reshape(B, nb, Q_BLOCK, H, Dqk), 1, 0)
    key_pos = jnp.arange(S)
    scale = Dqk ** -0.5

    def one_block(args):
        q_blk, blk = args
        s = jnp.einsum('bqhd,bkhd->bhqk', q_blk, k, preferred_element_type=jnp.float32) * scale
        query_pos = blk * Q_BLOCK + jnp.arange(Q_BLOCK)
        s = jnp.where(key_pos[None, :] <= query_pos[:, None], s, NEG_INF)
        p = jax.nn.softmax(s, axis=-1).astype(v.dtype)
        return jnp.einsum('bhqk,bkhd->bqhd', p, v)

    o = lax.map(one_block, (q_blocks, jnp.arange(nb)))
    return jnp.moveaxis(o, 0, 1).reshape(B, S, H, Dv)

def gdn_mla_mixer(h, cos, sin, w_in, conv_w, a_log, dt_bias, gdn_gain, q_norm_gain, kv_norm_gain,
                  w_uq, w_ukv, q_head_gain, k_head_gain, w_out):
    B, S, _ = h.shape
    proj = h @ w_in
    q, k, v, z, a, b, dq, dkv, k_rope = split_columns(proj, IN_SPLITS)
    qkv = jax.nn.silu(causal_depthwise_conv(jnp.concatenate([q, k, v], axis=-1), conv_w))
    q, k, v = jnp.split(qkv, 3, axis=-1)
    gshape = (B, S, GDN_HEADS, GDN_HEAD_DIM)
    q = l2_normalize(q.reshape(gshape))
    k = l2_normalize(k.reshape(gshape))
    v = v.reshape(gshape)
    beta = jax.nn.sigmoid(b.astype(jnp.float32))
    g = -jnp.exp(a_log.astype(jnp.float32)) * jax.nn.softplus(a.astype(jnp.float32) + dt_bias)
    o = chunked_gated_delta_rule(q, k, v, g, beta).astype(h.dtype)
    o_gdn = (rms_norm(o) * gdn_gain * jax.nn.silu(z.reshape(gshape))).reshape(B, S, GDN_WIDTH)
    q_lat = rms_norm(dq) * q_norm_gain
    qm = (q_lat @ w_uq).reshape(B, S, MLA_HEADS, MLA_QK)
    kv_lat = rms_norm(dkv) * kv_norm_gain
    kv = (kv_lat @ w_ukv).reshape(B, S, MLA_HEADS, MLA_NOPE + MLA_V)
    k_nope, vm = kv[..., :MLA_NOPE], kv[..., MLA_NOPE:]
    k_rope_h = jnp.broadcast_to(k_rope[:, :, None, :], (B, S, MLA_HEADS, MLA_ROPE))
    km = jnp.concatenate([k_nope, k_rope_h], axis=-1)
    qm = apply_rope_tail(rms_norm(qm) * q_head_gain, cos, sin)
    km = apply_rope_tail(rms_norm(km) * k_head_gain, cos, sin)
    o_mla = causal_block_attention(qm, km, vm).reshape(B, S, MLA_WIDTH)
    return jnp.concatenate([o_gdn, o_mla], axis=-1) @ w_out

def rwkv7_recurrence(r, w, k, v, a, b):
    B, S, H, N = r.shape

    def step(state, inp):
        r_t, w_t, k_t, v_t, a_t, b_t = inp
        sa = jnp.einsum('bhvk,bhk->bhv', state, a_t)
        state = (state * w_t[:, :, None, :] + sa[..., None] * b_t[:, :, None, :]
                 + v_t[..., None] * k_t[:, :, None, :])
        return state, jnp.einsum('bhvk,bhk->bhv', state, r_t)

    xs = tuple(jnp.moveaxis(t.astype(jnp.float32), 1, 0) for t in (r, w, k, v, a, b))
    _, y = lax.scan(step, jnp.zeros((B, H, N, N), jnp.float32), xs)
    return jnp.moveaxis(y, 0, 1)

def rwkv7_time_mix(h, mu, w_r, w_k, w_v, w_o, w0, w1, w2, a0, a1, a2, g1, g2,
                   k_k, k_a, r_k, ln_gain, ln_bias):
    B, S, D = h.shape
    hshape = (B, S, RWKV_HEADS, RWKV_HEAD_DIM)
    xx = jnp.pad(h[:, :-1], ((0, 0), (1, 0), (0, 0))) - h
    xr, xw, xk, xv, xa, xg = [h + xx * mu[j] for j in range(6)]
    r = xr @ w_r
    k = xk @ w_k
    v = xv @ w_v
    w_log = -jax.nn.softplus(-(w0 + jnp.tanh(xw @ w1) @ w2).astype(jnp.float32)) - 0.5
    decay = jnp.exp(-jnp.exp(w_log))
    a = jax.nn.sigmoid(a0 + (xa @ a1) @ a2)
    g = jax.nn.sigmoid(xg @ g1) @ g2
    kk = l2_normalize((k * k_k).reshape(hshape))
    k = k * (1 + (a - 1) * k_a)
    r_h, k_h, v_h, a_h = r.reshape(hshape), k.reshape(hshape), v.reshape(hshape), a.reshape(hshape)
    y = rwkv7_recurrence(r_h, decay.reshape(hshape), k_h, v_h, -kk, kk * a_h)
    mean = jnp.mean(y, axis=-1, keepdims=True)
    var = jnp.mean(jnp.square(y - mean), axis=-1, keepdims=True)
    y = ((y - mean) * lax.rsqrt(var + RWKV_GN_EPS)).reshape(B, S, D) * ln_gain + ln_bias
    bonus = jnp.sum((r_h * k_h * r_k).astype(jnp.float32), axis=-1, keepdims=True) * v_h
    y = (y + bonus.reshape(B, S, D)) * g
    return y.astype(h.dtype) @ w_o

def squared_relu_mlp(h, w_up, w_down):
    return jnp.square(jax.nn.relu(h @ w_up)) @ w_down

def setup_inputs(seed: int = 0) -> dict:
    key = jax.random.key(seed)
    keys = iter(jax.random.split(key, 48))
    f32 = jnp.float32
    n_even = (DEPTH + 1) // 2
    n_odd = DEPTH // 2

    def nrm(shape, s):
        return jax.random.normal(next(keys), shape, f32) * s

    def uni(shape, lo, hi):
        return jax.random.uniform(next(keys), shape, f32, minval=lo, maxval=hi)

    x = nrm((BATCH, SEQ, D_MODEL), 1.0)
    c = nrm((BATCH, D_MODEL), 1.0)
    positions = (jnp.arange(SEQ, dtype=jnp.int32)[None, :]
                 + jax.random.randint(next(keys), (BATCH, 1), 0, 4096, dtype=jnp.int32))
    dt = jnp.exp(uni((n_even, GDN_HEADS), math.log(1e-3), math.log(1e-1)))
    return {
        "x": x,
        "c": c,
        "positions": positions,
        "w_mod": nrm((DEPTH, D_MODEL, 6 * D_MODEL), D_MODEL ** -0.5),
        "b_mod": nrm((DEPTH, 6 * D_MODEL), 0.01),
        "w_in0": nrm((n_even, D_MODEL, IN_COLS), D_MODEL ** -0.5),
        "gdn_conv_w": nrm((n_even, GDN_CONV, 3 * GDN_WIDTH), GDN_CONV ** -0.5),
        "gdn_a_log": jnp.log(uni((n_even, GDN_HEADS), 1.0, 16.0)),
        "gdn_dt_bias": dt + jnp.log(-jnp.expm1(-dt)),
        "gdn_norm_gain": 1.0 + nrm((n_even, GDN_HEAD_DIM), 0.02),
        "mla_q_norm_gain": 1.0 + nrm((n_even, MLA_Q_RANK), 0.02),
        "mla_kv_norm_gain": 1.0 + nrm((n_even, MLA_KV_RANK), 0.02),
        "mla_w_uq": nrm((n_even, MLA_Q_RANK, MLA_HEADS * MLA_QK), MLA_Q_RANK ** -0.5),
        "mla_w_ukv": nrm((n_even, MLA_KV_RANK, MLA_HEADS * (MLA_NOPE + MLA_V)), MLA_KV_RANK ** -0.5),
        "mla_q_head_gain": 1.0 + nrm((n_even, MLA_QK), 0.02),
        "mla_k_head_gain": 1.0 + nrm((n_even, MLA_QK), 0.02),
        "w_out0": nrm((n_even, MIX_WIDTH, D_MODEL), MIX_WIDTH ** -0.5),
        "rwkv_mu": uni((n_odd, 6, D_MODEL), 0.0, 1.0),
        "rwkv_w_r": nrm((n_odd, D_MODEL, D_MODEL), D_MODEL ** -0.5),
        "rwkv_w_k": nrm((n_odd, D_MODEL, D_MODEL), D_MODEL ** -0.5),
        "rwkv_w_v": nrm((n_odd, D_MODEL, D_MODEL), D_MODEL ** -0.5),
        "rwkv_w_o": nrm((n_odd, D_MODEL, D_MODEL), D_MODEL ** -0.5),
        "rwkv_w0": uni((n_odd, D_MODEL), -6.0, -1.0),
        "rwkv_w1": nrm((n_odd, D_MODEL, DECAY_LORA), 0.1 * D_MODEL ** -0.5),
        "rwkv_w2": nrm((n_odd, DECAY_LORA, D_MODEL), 0.1 * DECAY_LORA ** -0.5),
        "rwkv_a0": nrm((n_odd, D_MODEL), 0.1),
        "rwkv_a1": nrm((n_odd, D_MODEL, AAA_LORA), 0.1 * D_MODEL ** -0.5),
        "rwkv_a2": nrm((n_odd, AAA_LORA, D_MODEL), 0.1 * AAA_LORA ** -0.5),
        "rwkv_g1": nrm((n_odd, D_MODEL, GATE_LORA), D_MODEL ** -0.5),
        "rwkv_g2": nrm((n_odd, GATE_LORA, D_MODEL), GATE_LORA ** -0.5),
        "rwkv_k_k": 0.85 + nrm((n_odd, D_MODEL), 0.02),
        "rwkv_k_a": 1.0 + nrm((n_odd, D_MODEL), 0.02),
        "rwkv_r_k": nrm((n_odd, RWKV_HEADS, RWKV_HEAD_DIM), 0.1),
        "rwkv_ln_gain": 1.0 + nrm((n_odd, D_MODEL), 0.02),
        "rwkv_ln_bias": nrm((n_odd, D_MODEL), 0.01),
        "w_up": nrm((DEPTH, D_MODEL, D_FF), D_MODEL ** -0.5),
        "w_down": nrm((DEPTH, D_FF, D_MODEL), D_FF ** -0.5),
    }

def reference(x, c, positions, w_mod, b_mod, w_in0, gdn_conv_w, gdn_a_log, gdn_dt_bias, gdn_norm_gain,
              mla_q_norm_gain, mla_kv_norm_gain, mla_w_uq, mla_w_ukv, mla_q_head_gain, mla_k_head_gain, w_out0,
              rwkv_mu, rwkv_w_r, rwkv_w_k, rwkv_w_v, rwkv_w_o, rwkv_w0, rwkv_w1, rwkv_w2,
              rwkv_a0, rwkv_a1, rwkv_a2, rwkv_g1, rwkv_g2, rwkv_k_k, rwkv_k_a, rwkv_r_k,
              rwkv_ln_gain, rwkv_ln_bias, w_up, w_down):
    cond = jax.nn.silu(c)
    cos, sin = rope_tables(positions)
    for layer in range(DEPTH):
        mod = cond @ w_mod[layer] + b_mod[layer]
        shift1, scale1, gate1, shift2, scale2, gate2 = jnp.split(mod, 6, axis=-1)
        h = adaln(x, shift1, scale1)
        i = layer // 2
        if layer % 2 == 0:
            y = gdn_mla_mixer(h, cos, sin, w_in0[i], gdn_conv_w[i], gdn_a_log[i], gdn_dt_bias[i],
                              gdn_norm_gain[i], mla_q_norm_gain[i], mla_kv_norm_gain[i], mla_w_uq[i],
                              mla_w_ukv[i], mla_q_head_gain[i], mla_k_head_gain[i], w_out0[i])
        else:
            y = rwkv7_time_mix(h, rwkv_mu[i], rwkv_w_r[i], rwkv_w_k[i], rwkv_w_v[i], rwkv_w_o[i],
                               rwkv_w0[i], rwkv_w1[i], rwkv_w2[i], rwkv_a0[i], rwkv_a1[i], rwkv_a2[i],
                               rwkv_g1[i], rwkv_g2[i], rwkv_k_k[i], rwkv_k_a[i], rwkv_r_k[i],
                               rwkv_ln_gain[i], rwkv_ln_bias[i])
        x = x + gate1[:, None, :] * y
        h = adaln(x, shift2, scale2)
        x = x + gate2[:, None, :] * squared_relu_mlp(h, w_up[layer], w_down[layer])
    return x


_drawn_inputs = setup_inputs


def setup_inputs(seed=0):
    import zlib

    import numpy as np

    out = dict(_drawn_inputs(seed))
    spreads = {}
    factors = {'gdn_norm_gain': 7.237,
     'mla_q_norm_gain': 8.0,
     'mla_kv_norm_gain': 8.0,
     'mla_q_head_gain': 8.0,
     'mla_k_head_gain': 8.0,
     'rwkv_w1': 8.0,
     'rwkv_w2': 8.0,
     'rwkv_a0': 5.499,
     'rwkv_a1': 8.0,
     'rwkv_a2': 8.0,
     'rwkv_ln_gain': 8.0,
     'rwkv_ln_bias': 8.0}
    for name, (base, spread) in spreads.items():
        noise = np.random.default_rng([zlib.crc32(name.encode()), seed]).standard_normal(out[name].shape)
        drawn = base * np.exp(spread * noise) if base else spread * noise
        out[name] = __import__('jax').numpy.asarray(drawn.astype(out[name].dtype))
    for name, factor in factors.items():
        out[name] = (out[name] * factor).astype(out[name].dtype)
    return out
```

```python
from contextlib import ExitStack

import concourse.bass as bass
from concourse import mybir

F32 = mybir.dt.float32
I32 = mybir.dt.int32
ALU = mybir.AluOpType
ACT = mybir.ActivationFunctionType
AX = mybir.AxisListType

P = 128
S = 512
D = 1024
KT = D // P
TT = S // P
C = 64
NCH = S // C
FF = 4096
FT = FF // P
GDN_W = 512
GDN_PAIRS = 4
RWKV_PAIRS = 8
GDN_STEPS, GDN_ACT_STEPS, RWKV_STEPS, RWKV_ACT_STEPS = 32, 24, 31, 28
GATE_COL = 2048
DQ_COL, DKV_COL, KROPE_COL = 2064, 2320, 2448
REST = 2480 - GATE_COL
QK = 96
NOPE, ROPE, HALF = 64, 32, 16
LEVELS = 6
EPS, L2_EPS, GN_EPS = 1e-6, 1e-12, 64e-5
DECAY = 0.6065306597126334

CONST_COLS = {}
_at = 0
for _name, _n in (("ident", P), ("ones", P), ("blk", P), ("istack", C), ("strictT", C), ("inclT", C),
                  ("level", LEVELS * C), ("level1T", C), ("causal", P), ("reset", S), ("invfreq", HALF),
                  ("headsel", GDN_PAIRS * P), ("eps", 4)):
    CONST_COLS[_name] = (_at, _n)
    _at += _n
NCONST = _at

T1 = {"mu": 0, "w0": 48, "a0": 56, "k_k": 64, "k_a": 72, "r_k": 80, "ln_g": 88, "ln_b": 96}
T1_ROWS = 104
T2 = {"conv": 0, "c": 48, "qng": 56, "kvng": 58, "gdng": 59}
T2_ROWS = 60


def build(nc, I, out):
    with ExitStack() as ctx:
        def sb(name, shape, dt=F32):
            return ctx.enter_context(nc.sbuf_tensor(name, shape, dt))

        def sem(name):
            return ctx.enter_context(nc.semaphore(name))

        PS = ctx.enter_context(nc.psum_tensor("PS", [P, 8, S], F32))
        cst = sb("cst", [P, NCONST])

        def cc(name):
            at, n = CONST_COLS[name]
            return cst[:, at:at + n]

        ident, ones, blk, istack = cc("ident"), cc("ones"), cc("blk"), cc("istack")
        strictT, inclT, level1T, causal, reset = cc("strictT"), cc("inclT"), cc("level1T"), cc("causal"), cc("reset")
        eps6, eps12, epsgn = (cc("eps")[:, j:j + 1] for j in range(3))

        def level(n):
            return cc("level")[:, (n - 1) * C:n * C]

        def over_chunks(mask, n=NCH):
            return mask.unsqueeze(1).broadcast_to([P, n, C])

        def chunks(x):
            return x.rearrange("p (c t) -> p c t", c=NCH)

        def tokens(x):
            return x.rearrange("p c t -> p (c t)")

        def bank(j):
            return PS[:, j, :].rearrange("p (c t) -> p c t", c=NCH)

        def blocks2(j):
            return PS[:, j:j + 2, :].rearrange("p b (c t) -> p (b c) t", c=4)

        xT = sb("xT", [P, KT, S])
        hT = sb("hT", [P, KT, S])
        bmodT = sb("bmodT", [P, 96])
        t1T = sb("t1T", [P, T1_ROWS])
        t2T = sb("t2T", [P, T2_ROWS])
        modT = sb("modT", [P, 48])
        cond = sb("cond", [P, KT])
        cond_t = sb("cond_t", [P, 2, KT])
        sq = sb("sq", [P, 2, S])
        rs = sb("rs", [P, 2, S])
        ones1 = sb("ones1", [P, 1])
        ARENA = 40300
        arena = sb("arena", [P, ARENA])
        cursor = [0]

        def region(*shape):
            n = 1
            for x in shape:
                n *= x
            a = arena[:, cursor[0]:cursor[0] + n]
            cursor[0] += n
            assert cursor[0] <= ARENA, (cursor[0], shape)
            if len(shape) == 2:
                a = a.rearrange("p (a b) -> p a b", a=shape[0])
            if len(shape) == 3:
                a = a.rearrange("p (a b c) -> p a b c", a=shape[0], b=shape[1])
            return a

        xtok = region(TT, D)
        tabs = region(3, P)
        pos_i = region(P).bitcast(I32)
        pos_f = region(P)
        mwring = region(2, KT, 256)
        macc = region(6 * D)
        mblk = region(2, 256)
        cursor[0] = 0
        mix0 = region(KT, S)
        pc = region(16)
        pw = region(4, KT, P)
        FB_AT = cursor[0]
        FB = [region(NCH, P) for _ in range(4)]
        TOK_AT = cursor[0]
        btok, ktok, atok, Vbd = (region(NCH, P) for _ in range(4))
        LTbd, AKbd, XTbd, Pbd = FB
        WTbd, Hbd, ubd = Pbd, XTbd, AKbd
        R1 = region(NCH, 2, C)
        RB, RK, LTs, XTs, Xs, Pst, Vs, AKV, U, KVe = (region(NCH, C) for _ in range(10))
        AKs = Pst
        Hs = region(NCH + 1, C)
        te = region(2, C)
        egC = region(NCH)
        S1, S2, S3, RT, qf, kf, vf, zf, th, tmp, post = (region(S) for _ in range(11))
        PAIR_END = cursor[0]
        Grow, Brow = region(GDN_PAIRS, S), region(GDN_PAIRS, S)
        Gp, Bp = region(S), region(S)
        cb = region(3, S + 3)
        gcol, bcol, glast = region(NCH), region(NCH), region(NCH)
        gatew = region(KT, 16)
        cursor[0] = PAIR_END
        xr, xk = region(KT, S), region(KT, S)
        lora = region(4, S)
        lw = region(4, P)
        xv = mix0
        xx = arena[:, FB_AT:FB_AT + KT * S].rearrange("p (k s) -> p k s", k=KT)
        lw1 = arena[:, TOK_AT:TOK_AT + KT * 288].rearrange("p (k f) -> p k f", k=KT)
        cursor[0] = KT * S
        mlaw = region(KT, 416)
        uq = region(2, 768)
        ukv = region(D)
        dq, dkv = region(2, S), region(S)
        grow = region(2, QK)
        gains = region(2, QK)
        krope = region(TT, ROPE)
        ang, rot, trig = region(TT, 2, HALF), region(TT, 2, HALF), region(TT, 2, HALF)
        qall, kall = region(TT, 8, QK), region(TT, 8, QK)
        vall = region(TT, 8, C)
        sqh = region(8, QK)
        ropet = region(4, 8, HALF)
        ssh = region(2, 8)
        qh, kh, vh = region(TT, QK), region(TT, QK), region(TT, C)
        qhT, khT = region(S), region(S)
        prob = region(TT, S)
        probT = region(TT, S)
        negm, den, rden = region(TT), region(TT), region(TT)
        MOD2 = cursor[0]
        mwring2 = region(2, KT, 256)
        macc2 = region(4 * D)
        mblk2 = region(2, 256)
        cursor[0] = 0
        hid = region(FT, S)
        wring = region(2, KT, 256)
        mwring1 = region(2, KT, 256)
        macc1 = region(6 * D)
        mblk1 = region(2, 256)
        xout = region(2, D)

        tabs_landed, x_landed, cst_landed = sem("tabs_landed"), sem("x_landed"), sem("cst_landed")
        tabs_T, tabs_ready, x_T, x_ready = sem("tabs_T"), sem("tabs_ready"), sem("x_T"), sem("x_ready")
        cond_tanh, cond_ready = sem("cond_tanh"), sem("cond_ready")
        mw_landed = [sem("mw0_landed"), sem("mw1_landed")]
        pmw_landed = [sem("pmw0_landed"), sem("pmw1_landed")]
        lw1_landed = sem("lw1_landed")
        mw_used = sem("mw_used")
        macc_ready, mod_summed, mod_ready = sem("macc_ready"), sem("mod_summed"), sem("mod_ready")
        vec, act_, pool_ = sem("vec_steps"), sem("act_steps"), sem("pool_steps")
        sq_ready, sq_used, ss_ready, rstd_ready, h_ready = (
            sem("sq_ready"), sem("sq_used"), sem("ss_ready"), sem("rstd_ready"), sem("h_ready"))
        w_landed = [sem("w0_landed"), sem("w1_landed")]
        w_used, tile_out, tile_taken = sem("w_used"), sem("tile_out"), sem("tile_taken")
        zeroed = sem("zeroed")
        gw_landed, rows_out, rows_t, rows_e, rows_l, rows_done, rows_bc, gates_ready = (
            sem("gw_landed"), sem("rows_out"), sem("rows_t"), sem("rows_e"), sem("rows_l"), sem("rows_done"),
            sem("rows_bc"), sem("gates_ready"))
        pw_landed = [sem(f"pw{j}_landed") for j in range(4)]
        lw_landed, proj_out, proj_act, proj_vec = sem("lw_landed"), sem("proj_out"), sem("proj_act"), sem("proj_vec")
        head_sq, head_ss, head_rs = sem("head_sq"), sem("head_ss"), sem("head_rs")
        d_in, d_exp, fm_ready = sem("d_in"), sem("d_exp"), sem("fm_ready")
        fb_act, fb_pool, r1_ready = sem("fb_act"), sem("fb_pool"), sem("r1_ready")
        a_out, tok_out, tok_taken, lts_ready, lt_bd, aks_ready = (
            sem("a_out"), sem("tok_out"), sem("tok_taken"), sem("lts_ready"), sem("lt_bd"), sem("aks_ready"))
        vs_out, vs_ready, vbd_ready = sem("vs_out"), sem("vs_ready"), sem("vbd_ready")
        at_out, xs_ready, xt_ready, xtbd_ready = sem("at_out"), sem("xs_ready"), sem("xt_ready"), sem("xtbd_ready")
        p_out, ps_ready, pbd_ready, q_out = sem("p_out"), sem("ps_ready"), sem("pbd_ready"), sem("q_out")
        akv_out, akv_ready, kv_ready, u0_out, u0_ready, wt_ready = (
            sem("akv_out"), sem("akv_ready"), sem("kv_ready"), sem("u0_out"), sem("u0_ready"), sem("wt_ready"))
        dh_out, hs_ready, w_out, us_ready, hu_bd, y_out = (
            sem("dh_out"), sem("hs_ready"), sem("w_out"), sem("us_ready"), sem("hu_bd"), sem("y_out"))
        post_a, post_b, post_c, mix_ready = sem("post_a"), sem("post_b"), sem("post_c"), sem("mix_ready")
        mla_landed, lat_out, lat_taken, lat_sq, lat_ss, lat_rs, lat_ready = (
            sem("mla_landed"), sem("lat_out"), sem("lat_taken"), sem("lat_sq"), sem("lat_ss"), sem("lat_rs"),
            sem("lat_ready"))
        ang_ready, trig_ready, gains_bc, tok_proj, tok_copied, ssh_ready, rsh_ready, heads_ready = (
            sem("ang_ready"), sem("trig_ready"), sem("gains_bc"), sem("tok_proj"), sem("tok_copied"),
            sem("ssh_ready"), sem("rsh_ready"), sem("heads_ready"))
        hslice, qkT_out, qkT_ready, score_out, max_ready, exp_ready, prob_ready = (
            sem("hslice"), sem("qkT_out"), sem("qkT_ready"), sem("score_out"), sem("max_ready"), sem("exp_ready"),
            sem("prob_ready"))
        pT_out, pT_ready, o_out, o_ready = sem("pT_out"), sem("pT_ready"), sem("o_out"), sem("o_ready")
        xmix_ready, lora_out, lora_ready, xx_ready = sem("xmix_ready"), sem("lora_out"), sem("lora_ready"), sem("xx_ready")
        xo_T, xo_ready, out_landed = sem("xo_T"), sem("xo_ready"), [sem("out0_landed"), sem("out1_landed")]
        cb_zeroed = sem("cb_zeroed")
        class Steps:

            def __init__(self, eng, sem_):
                self.eng, self.sem, self.n, self.off = eng, sem_, 0, 0

            def __call__(self, ins):
                self.n += 1
                ins.then_inc(self.sem, 1)
                self.eng.wait_ge(self.sem, self.off + self.n)

            def tell(self, ins, sem_, value):
                ins.then_inc(sem_, 1)
                self.eng.wait_ge(sem_, value)

            def loop(self, count, steps, body):
                start = self.n
                with self.eng.Fori(0, count) as i:
                    self.off = i * steps
                    body(i)
                assert self.n - start == steps, f"the loop has {self.n - start} steps"
                self.off, self.n = 0, start + count * steps

        small8 = sb("small8", [8, 4])
        posT = sb("posT", [P, TT])
        gate_cols = sb("gate_cols", [P, KT])
        tmp_r = sq
        one = cc("eps")[:, 3:4]

        BLK = {"o0": 0, "up0": 4, "down0": 20, "o1": 36, "up1": 40, "down1": 56}
        TIL = {"o0": 0, "up0": 8, "down0": 40, "o1": 48, "up1": 56, "down1": 88}
        X_DONE = [None, 4 + 8, 4 + 48, 4 + 56]
        SHIFT, SCALE, GATE = (0, 24), (8, 32), (16, 40)

        block = ctx.enter_context(nc.Block())

        @block.sync
        def _(sp):
            sp.dma_start(cst[:], I["const"][:, :]).then_inc(cst_landed, 16)

            def table(dst, src):
                sp.dma_start(dst, src).then_inc(tabs_landed, 16)
            table(tabs[0:96, 0, :], I["b_mod"].rearrange("l (r f) -> (l r) f", f=P))
            table(tabs[0:48, 1, :], I["rwkv_mu"].rearrange("a j (r f) -> (a j r) f", f=P))
            for name in ("w0", "a0", "k_k", "k_a", "ln_g", "ln_b"):
                src = {"ln_g": "rwkv_ln_gain", "ln_b": "rwkv_ln_bias"}.get(name, "rwkv_" + name)
                table(tabs[T1[name]:T1[name] + KT, 1, :], I[src].rearrange("a (r f) -> (a r) f", f=P))
            table(tabs[T1["r_k"]:T1["r_k"] + KT, 1, :], I["rwkv_r_k"].rearrange("a (r h) d -> (a r) (h d)", h=2))
            table(tabs[0:48, 2, :], I["gdn_conv_w"].rearrange("a j (r f) -> (a j r) f", f=P))
            table(tabs[48:56, 2, :], I["c"].rearrange("a (r f) -> (a r) f", f=P))
            table(tabs[56:58, 2, :], I["mla_q_norm_gain"].rearrange("a (r f) -> (a r) f", f=P))
            table(tabs[58:59, 2, :], I["mla_kv_norm_gain"])
            table(tabs[59:60, 2, 0:C], I["gdn_norm_gain"])
            table(tabs[59:60, 2, C:P], I["gdn_norm_gain"])
            table(pos_i[0:TT, :], I["positions"].rearrange("a (t p) -> (a t) p", p=P))
            table(small8[:, 0:1], I["gdn_dt_bias"].rearrange("a h -> h a"))
            table(small8[:, 1:2], I["gdn_a_log"].rearrange("a h -> h a"))
            sp.dma_start(xtok, I["x"][0].rearrange("(t p) d -> p t d", p=P)).then_inc(x_landed, 16)

            wm = I["w_mod"][0].rearrange("(k p) n -> p k n", p=P)
            with sp.Fori(0, 4) as i:
                for s in range(2):
                    sp.wait_ge(mw_used, i * 2 + s + 1)
                    sp.dma_start(mwring[:, s], wm[:, :, bass.ds(i * 512 + s * 256, 256)]).then_inc(mw_landed[s], 16)

            win = I["w_in0"][0].rearrange("(k p) n -> p k n", p=P)
            sp.wait_ge(mod_ready, 1)
            sp.wait_ge(x_ready, KT)
            sp.dma_start(gatew, win[:, :, GATE_COL:GATE_COL + 16]).then_inc(gw_landed, 16)
            with sp.Fori(0, GDN_PAIRS) as i:
                for j in range(4):
                    sp.wait_ge(proj_out, i * 4 + j + 1)
                    sp.dma_start(pw[:, j], win[:, :, bass.ds(i * P + j * GDN_W, P)]).then_inc(pw_landed[j], 16)

            sp.wait_ge(mix_ready, GDN_PAIRS)
            sp.dma_start(mlaw, win[:, :, DQ_COL:DQ_COL + 416]).then_inc(mla_landed, 16)
            sp.dma_start(uq, I["mla_w_uq"][0].rearrange("(k p) n -> p k n", p=P)).then_inc(mla_landed, 16)
            sp.dma_start(ukv, I["mla_w_ukv"][0]).then_inc(mla_landed, 16)
            sp.dma_start(grow[0:1, 0, :], I["mla_q_head_gain"]).then_inc(mla_landed, 16)
            sp.dma_start(grow[0:1, 1, :], I["mla_k_head_gain"]).then_inc(mla_landed, 16)

            def stream(name, wv, rows):
                b = BLK[name]
                n = wv.shape[2] // 256 * rows
                per = 2 * rows
                with sp.Fori(0, n // per) as i:
                    for s in range(per):
                        sp.wait_ge(w_used, i * per + b + s + 1)
                        r, col = s % rows, s // rows
                        sp.dma_start(wring[:, s % 2],
                                     wv[:, r * KT:(r + 1) * KT, bass.ds(i * 512 + col * 256, 256)]
                                     ).then_inc(w_landed[s % 2], 16)

            def view(w):
                return w.rearrange("(k p) n -> p k n", p=P)

            sp.wait_ge(o_ready, 8)
            stream("o0", view(I["w_out0"][0]), 1)
            stream("up0", view(I["w_up"][0]), 1)
            stream("down0", view(I["w_down"][0]), 4)

            sp.wait_ge(tile_taken, 4 + 48)
            for name, a, n in (("rwkv_w1", 0, 64), ("rwkv_a1", 64, 64), ("rwkv_g1", 128, 160)):
                sp.dma_start(lw1[:, :, a:a + n], view(I[name][0])).then_inc(lw1_landed, 16)
            wp = [view(I[n][0]) for n in ("rwkv_w_r", "rwkv_w_k", "rwkv_w_v")]
            with sp.Fori(0, RWKV_PAIRS) as i:
                for j in range(3):
                    sp.wait_ge(proj_out, i * 6 + 15 + j)
                    sp.dma_start(pw[:, j], wp[j][:, :, bass.ds(i * P, P)]).then_inc(pw_landed[j], 16)
                sp.wait_ge(proj_out, i * 6 + 20)
                for dst, src in ((lw[0:64, 0, :], I["rwkv_w2"][0]), (lw[0:64, 1, :], I["rwkv_a2"][0]),
                                 (lw[:, 2, :], I["rwkv_g2"][0, 0:P]), (lw[0:32, 3, :], I["rwkv_g2"][0, P:160])):
                    sp.dma_start(dst, src[:, bass.ds(i * P, P)]).then_inc(lw_landed, 16)
            sp.wait_ge(mix_ready, GDN_PAIRS + RWKV_PAIRS)
            stream("o1", view(I["rwkv_w_o"][0]), 1)
            stream("up1", view(I["w_up"][1]), 1)
            stream("down1", view(I["w_down"][1]), 4)
            for t in range(TT):
                sp.wait_ge(xo_ready, 2 * t + 2)
                sp.dma_start(out[0, t * P:(t + 1) * P, :], xout[:, t % 2]).then_inc(out_landed[t % 2], 16)
            for b in range(2):
                sp.wait_ge(out_landed[b], 16 * TT // 2)

        @block.tensor
        def _(pe):
            def mm(o, l, r, first=True, last=True):
                return pe.matmul(o, l, r, start=first, stop=last)

            pe.wait_ge(cst_landed, 16)
            pe.wait_ge(tabs_landed, 16 * 18)
            for j, r in ((0, 96), (1, T1_ROWS), (2, T2_ROWS)):
                pe.transpose(PS[:, j, 0:r], tabs[0:r, j, :], ident[0:r, 0:r])
            pe.wait_ge(rows_t, 1)
            pe.transpose(PS[:, 3, 0:TT], pos_f[0:TT, :], ident[0:TT, 0:TT]).then_inc(tabs_T, 1)
            pe.wait_ge(x_landed, 16)
            for k in range(KT):
                if k >= 2:
                    pe.wait_ge(x_ready, k - 1)
                for t in range(TT):
                    m = pe.transpose(PS[:, 4 + k % 2, t * P:(t + 1) * P], xtok[:, t, k * P:(k + 1) * P], ident)
                m.then_inc(x_T, 1)

            def mod_sums(acc, n, phase):
                pe.wait_ge(macc_ready, phase + 1)
                for j in range(n):
                    m = mm(PS[:, 7, j:j + 1], acc[:, j * P:(j + 1) * P], ones1[:])
                m.then_inc(mod_summed, 1)

            def norm_sums(idx):
                for k in range(KT):
                    pe.wait_ge(sq_ready, idx * KT + k + 1)
                    m = mm(PS[:, 6, :], ones, sq[:, k % 2], k == 0, k == KT - 1)
                    m.then_inc(sq_used, 1)

            mod_sums(macc, 16, 0)
            norm_sums(0)

            pe.wait_ge(gw_landed, 16)
            for j in range(2):
                for k in range(KT):
                    pe.wait_ge(h_ready, k + 1)
                    m = mm(PS[0:8, j, :], gatew[:, k, j * 8:j * 8 + 8], hT[:, k], k == 0, k == KT - 1)
                m.then_inc(rows_out, 1)
            pe.wait_ge(rows_done, 1)
            for p in range(GDN_PAIRS):
                for j, src in enumerate((cb[0:8, 0, 0:S], cb[0:8, 2, 0:S])):
                    m = mm(PS[:, 2 * p + j, :], cc("headsel")[0:8, p * P:(p + 1) * P], src)
            m.then_inc(rows_bc, 1)
            pe.wait_ge(gates_ready, 1)

            def recurrence(n, rw):
                pe.wait_ge(r1_ready, n)
                pe.wait_ge(fb_act, 2 * n)
                for c in range(NCH):
                    m = mm(blocks2(0)[:, c], FB[0][:, c], R1[:, c].rearrange("p a t -> p (a t)"))
                if rw:
                    for c in range(NCH):
                        m = mm(blocks2(2)[:, c], FB[1][:, c], R1[:, c].rearrange("p a t -> p (a t)"))
                m.then_inc(a_out, 1)
                src = FB[0] if rw else FB[1]
                for c in range(NCH):
                    m = pe.transpose(blocks2(4)[:, c], src[:, c], ident)
                m.then_inc(tok_out, 1)
                pe.wait_ge(fb_pool, 2 * n)
                for c in range(NCH):
                    m = pe.transpose(blocks2(6)[:, c], FB[2][:, c], ident)
                m.then_inc(tok_out, 1)
                pe.wait_ge(tok_taken, 3 * n - 2)
                if rw:
                    for c in range(NCH):
                        m = pe.transpose(blocks2(4)[:, c], FB[1][:, c], ident)
                    m.then_inc(tok_out, 1)
                pe.wait_ge(tok_taken, 3 * n - 1 if rw else 3 * n)
                for c in range(NCH):
                    m = mm(bank(6)[:, c], FB[3][:, c], istack)
                m.then_inc(vs_out, 1)

                pe.wait_ge(lt_bd, n)
                for c in range(NCH):
                    m = mm(bank(0)[:, c], LTbd[:, c], istack)
                m.then_inc(at_out, 1)
                for lv in range(2, LEVELS + 1):
                    q = 5 * (n - 1) + lv - 1
                    pe.wait_ge(xs_ready, q)
                    for c in range(NCH):
                        m = mm(bank(1)[:, c], LTbd[:, c], Xs[:, c])
                    m.then_inc(p_out, 1)
                    pe.wait_ge(ps_ready, q)
                    if lv < LEVELS:
                        pe.wait_ge(xtbd_ready, 6 * (n - 1) + lv - 1)
                        for c in range(NCH):
                            mm(bank(2)[:, c], XTbd[:, c], Pst[:, c])
                    pe.wait_ge(pbd_ready, q)
                    for c in range(NCH):
                        m = mm(bank(3)[:, c], Pbd[:, c], XTs[:, c])
                    m.then_inc(q_out, 1)

                if rw:
                    pe.wait_ge(vs_ready, n - GDN_PAIRS)
                    for c in range(NCH):
                        m = mm(bank(4)[:, c], AKbd[:, c], Vs[:, c])
                    pe.wait_ge(tok_taken, 3 * n)
                    for c in range(NCH):
                        m = mm(bank(5)[:, c], ktok[:, c], Vs[:, c])
                    m.then_inc(akv_out, 1)
                pe.wait_ge(xtbd_ready, 6 * n)
                pe.wait_ge(akv_ready, n)
                for c in range(NCH):
                    mm(bank(6)[:, c], XTbd[:, c], AKV[:, c])
                for c in range(NCH):
                    m = mm(bank(7)[:, c], atok[:, c], XTs[:, c])
                m.then_inc(u0_out, 1)
                pe.wait_ge(u0_ready, n)
                pe.wait_ge(wt_ready, n)
                for c in range(NCH - 1):
                    if c:
                        pe.wait_ge(us_ready, 7 * (n - 1) + c)
                    mm(PS[:, c % 2, 0:C], btok[:, c], U[:, c]).then_inc(dh_out, 1)
                    pe.wait_ge(hs_ready, 7 * (n - 1) + c + 1)
                    mm(PS[:, 2 + c % 2, 0:C], WTbd[:, c + 1], Hs[:, c + 1]).then_inc(w_out, 1)
                pe.wait_ge(hu_bd, n)
                rt = chunks(RT) if not rw else R1[:, :, 1]
                for c in range(NCH):
                    mm(bank(4)[:, c], Hbd[:, c], rt[:, c], True, False)
                    m = mm(bank(4)[:, c], ubd[:, c], RB[:, c], False, not rw)
                    if rw:
                        m = mm(bank(4)[:, c], Vbd[:, c], RK[:, c], False, True)
                m.then_inc(y_out, 1)

            with pe.Fori(0, GDN_PAIRS) as i:
                n = i + 1
                for j in range(4):
                    pe.wait_ge(pw_landed[j], i * 16 + 16)
                    for k in range(KT):
                        m = mm(PS[:, j, :], pw[:, j, k], hT[:, k], k == 0, k == KT - 1)
                    m.then_inc(proj_out, 1)
                for j in range(2):
                    pe.wait_ge(head_sq, i * 3 + j + 1)
                    m = mm(PS[:, 4 + j, :], blk, sq[:, j])
                m.then_inc(head_ss, 1)
                recurrence(n, False)
                pe.wait_ge(head_sq, i * 3 + 3)
                mm(PS[:, 5, :], blk, sq[:, 0]).then_inc(head_ss, 1)
                pe.wait_ge(mix_ready, n)

            pe.wait_ge(mla_landed, 16 * 5)
            for j in range(3):
                for k in range(KT):
                    m = mm(PS[:, j, :], mlaw[:, k, j * P:(j + 1) * P], hT[:, k], k == 0, k == KT - 1)
                m.then_inc(lat_out, 1)
            for t in range(TT):
                for k in range(KT):
                    m = mm(PS[:, 3, t * ROPE:(t + 1) * ROPE], hT[:, k, t * P:(t + 1) * P], mlaw[:, k, 384:416],
                           k == 0, k == KT - 1)
            m.then_inc(lat_out, 1)
            for j in range(2):
                m = mm(PS[:, 4, j * QK:(j + 1) * QK], ones[0:1, :], grow[0:1, j, :])
            m.then_inc(gains_bc, 1)
            for j in range(3):
                pe.wait_ge(lat_sq, j + 1)
                m = mm(PS[:, 5 + j // 2, :], ones, sq[:, j % 2], j != 1, j != 0)
                m.then_inc(lat_ss, 1)
            pe.wait_ge(lat_ready, 1)
            for t in range(TT):
                if t:
                    pe.wait_ge(tok_copied, t)
                cols = slice(t * P, (t + 1) * P)
                for j in range(2):
                    for k in range(2):
                        mm(PS[:, j, 0:384], dq[:, k, cols], uq[:, k, j * 384:(j + 1) * 384], k == 0, k == 1)
                for j in range(2):
                    m = mm(PS[:, 2 + j, :], dkv[:, cols], ukv[:, j * S:(j + 1) * S])
                m.then_inc(tok_proj, 1)
            with pe.Fori(0, 4) as i:
                for a in range(2):
                    hd = i * 2 + a + 1
                    pe.wait_ge(hslice, hd)
                    for t in range(TT):
                        pe.transpose(PS[0:QK, 0, t * P:(t + 1) * P], qh[:, t], ident)
                    for t in range(TT):
                        m = pe.transpose(PS[0:QK, 1, t * P:(t + 1) * P], kh[:, t], ident)
                    m.then_inc(qkT_out, 1)
                    pe.wait_ge(qkT_ready, hd)
                    for t in range(TT):
                        mm(PS[:, 2 + t, 0:(t + 1) * P], qhT[0:QK, t * P:(t + 1) * P],
                           khT[0:QK, 0:(t + 1) * P]).then_inc(score_out, 1)
                    pe.wait_ge(prob_ready, hd)
                    for kt in range(TT):
                        for t in range(kt, TT):
                            m = pe.transpose(PS[:, 2 + kt, t * P:(t + 1) * P], prob[:, t, kt * P:(kt + 1) * P], ident)
                    m.then_inc(pT_out, 1)
                    pe.wait_ge(pT_ready, hd)
                    for kt in range(TT):
                        m = mm(PS[a * C:(a + 1) * C, 6 + a, kt * P:S], vh[:, kt], probT[:, kt, kt * P:S],
                               kt == 0, kt == TT - 1)
                    m.then_inc(o_out, 1)
                    pe.wait_ge(o_ready, hd)

            def tile(name, i, per, j, src, first=True, last=True, base=0, slot=0, mt=0):
                for k in range(KT):
                    m = mm(PS[:, j, :], wring[:, slot, k, mt * P:(mt + 1) * P], src[:, base + k],
                           first and k == 0, last and k == KT - 1)
                return m

            def stream(name, src, n, rows, ready=None):
                b, t0 = BLK[name], TIL[name]
                per = 2 * rows
                with pe.Fori(0, n // per) as i:
                    for s in range(per):
                        slot, r = s % 2, s % rows
                        pe.wait_ge(w_landed[slot], (i * (per // 2) + (b + s - slot) // 2 + 1) * 16)
                        for mt in range(2):
                            t = (s // rows) * 2 + mt
                            if r == 0:
                                pe.wait_ge(tile_taken, i * 4 + t0 + t + 1)
                            m = tile(name, i, per, t, src, r == 0, r == rows - 1, r * KT, slot, mt)
                            if mt == 1 and r < rows - 1:
                                m.then_inc(w_used, 1)
                            elif r == rows - 1:
                                m.then_inc(tile_out, 1)
                        if r == rows - 1:
                            mm(PS[0:1, 7, 0:1], ones1[:], ones1[:]).then_inc(w_used, 1)

            mod_sums(macc2, 32, 1)
            pe.wait_ge(mod_ready, 2)
            stream("o0", mix0, 4, 1)
            norm_sums(1)
            pe.wait_ge(h_ready, 2 * KT)
            stream("up0", hT, 16, 1)
            pe.wait_ge(tile_taken, 4 + 40)
            stream("down0", hid, 16, 4)
            mod_sums(macc1, 48, 2)
            norm_sums(2)

            pe.wait_ge(lw1_landed, 16 * 3)
            for j, (src, a, m_) in enumerate(((xr, 0, 64), (xk, 64, 64), (xv, 128, P), (xv, 256, 32))):
                pe.wait_ge(xmix_ready, min(j, 2) + 1)
                for k in range(KT):
                    m = mm(PS[0:m_, j, :], lw1[:, k, a:a + m_], src[:, k], k == 0, k == KT - 1)
                m.then_inc(lora_out, 1)
            pe.wait_ge(lora_ready, 4)
            pe.wait_ge(xmix_ready, 6)
            with pe.Fori(0, RWKV_PAIRS) as i:
                n = i + GDN_PAIRS + 1
                for j, src in enumerate((xr, xk, xv)):
                    pe.wait_ge(pw_landed[j], (i + GDN_PAIRS) * 16 + 16)
                    for k in range(KT):
                        m = mm(PS[:, j, :], pw[:, j, k], src[:, k], k == 0, k == KT - 1)
                    m.then_inc(proj_out, 1)
                pe.wait_ge(lw_landed, i * 64 + 64)
                mm(PS[:, 3, :], lw[0:64, 0], lora[0:64, 0]).then_inc(proj_out, 1)
                mm(PS[:, 4, :], lw[0:64, 1], lora[0:64, 1]).then_inc(proj_out, 1)
                mm(PS[:, 5, :], lw[:, 2], lora[:, 2], True, False)
                mm(PS[:, 5, :], lw[0:32, 3], lora[0:32, 3], False, True).then_inc(proj_out, 1)
                pe.wait_ge(head_sq, i * 4 + 13)
                mm(PS[:, 6, :], blk, sq[:, 0]).then_inc(head_ss, 1)
                pe.wait_ge(head_sq, i * 4 + 14)
                mm(PS[:, 7, :], blk, sq[:, 1]).then_inc(head_ss, 1)
                pe.wait_ge(post_a, i + 1)
                recurrence(n, True)
                pe.wait_ge(head_sq, i * 4 + 15)
                mm(PS[:, 5, :], blk, sq[:, 0]).then_inc(head_ss, 1)
                pe.wait_ge(head_sq, i * 4 + 16)
                mm(PS[:, 6, :], blk, sq[:, 1]).then_inc(head_ss, 1)
                pe.wait_ge(mix_ready, n)
            stream("o1", hT, 4, 1)
            norm_sums(3)
            pe.wait_ge(h_ready, 4 * KT)
            stream("up1", hT, 16, 1)
            pe.wait_ge(tile_taken, 4 + 88)
            stream("down1", hid, 16, 4)
            pe.wait_ge(tile_taken, 4 + 96)
            for t in range(TT):
                for hf in range(2):
                    q = 2 * t + hf
                    if q >= 2:
                        pe.wait_ge(xo_ready, q - 1)
                    for k in range(4):
                        m = pe.transpose(PS[:, q % 2, k * P:(k + 1) * P], xT[:, hf * 4 + k, t * P:(t + 1) * P], ident)
                    m.then_inc(xo_T, 1)

        @block.vector
        def _(dve):
            do = Steps(dve, vec)
            tt, ts, stt = dve.tensor_tensor, dve.tensor_scalar, dve.scalar_tensor_tensor
            dve.memset(ones1[:], 1.0).then_inc(tile_taken, 4)
            dve.wait_ge(tile_taken, 4)
            dve.memset(ones1[:], 1.0).then_inc(w_used, 2)
            dve.wait_ge(w_used, 2)
            dve.memset(ones1[:], 1.0).then_inc(mw_used, 2)
            dve.wait_ge(mw_used, 2)
            dve.memset(ones1[:], 1.0).then_inc(proj_out, 4)
            dve.wait_ge(proj_out, 4)

            dve.wait_ge(tabs_landed, 16 * 18)
            do.tell(dve.tensor_copy(pos_f[0:TT, :], pos_i[0:TT, :]), rows_t, 1)
            dve.wait_ge(tabs_T, 1)
            do(dve.tensor_copy(bmodT[:], PS[:, 0, 0:96]))
            do(dve.tensor_copy(t1T[:], PS[:, 1, 0:T1_ROWS]))
            do(dve.tensor_copy(t2T[:], PS[:, 2, 0:T2_ROWS]))
            do(dve.tensor_copy(posT[:], PS[:, 3, 0:TT]))
            do(ts(t1T[:, T1["w0"]:T1["w0"] + 16], t1T[:, T1["w0"]:T1["w0"] + 16], 0.5, None, ALU.mult))
            do(ts(t2T[:, 0:56], t2T[:, 0:56], 0.5, None, ALU.mult))
            do.tell(dve.tensor_copy(cond_t[:, 0], t2T[:, 48:56]), tabs_ready, 1)
            dve.wait_ge(cond_tanh, 1)
            do(stt(cond[:], cond_t[:, 1], 1.0, cond_t[:, 0], ALU.add, ALU.mult))
            do.tell(dve.tensor_copy(cond_t[:, 0], cond[:]), cond_ready, 1)

            def mod_block(i):
                for s in range(2):
                    dve.wait_ge(mw_landed[s], i * 16 + 16)
                    do(ts(mblk[:, s], mwring[:, s, 0], cond[:, 0:1], None, ALU.mult))
                    for k in range(1, KT - 1):
                        do(stt(mblk[:, s], mwring[:, s, k], cond[:, k:k + 1], mblk[:, s], ALU.mult, ALU.add))
                    do.tell(stt(macc[:, bass.ds(i * 512 + s * 256, 256)], mwring[:, s, KT - 1], cond[:, KT - 1:KT],
                                mblk[:, s], ALU.mult, ALU.add), mw_used, i * 2 + s + 3)
            do.loop(4, 14, mod_block)
            do.tell(dve.tensor_copy(cond_t[:, 0], cond[:]), macc_ready, 1)

            def mod_finish(layer, phase, a, b):
                dve.wait_ge(mod_summed, phase + 1)
                do(tt(modT[:, a:b], PS[:, 7, 0:b - a], bmodT[:, layer * 48 + a:layer * 48 + b], ALU.add))
                for g in SCALE:
                    if a <= g < b:
                        do(ts(modT[:, g:g + KT], modT[:, g:g + KT], 1.0, None, ALU.add))
                do.tell(dve.tensor_copy(cond_t[:, 0], cond[:]), mod_ready, phase + 1)

            def norm(idx):
                half = idx % 2
                dve.wait_ge(rstd_ready, idx + 1)
                for k in range(KT):
                    do(stt(hT[:, k], xT[:, k], modT[:, SCALE[half] + k:SCALE[half] + k + 1], rs[:, 0],
                           ALU.mult, ALU.mult))
                    do.tell(ts(hT[:, k], hT[:, k], modT[:, SHIFT[half] + k:SHIFT[half] + k + 1], None, ALU.add),
                            h_ready, idx * KT + k + 1)

            mod_finish(0, 0, 0, 16)
            norm(0)

            rA, rE, rB = cb[0:8, 0, 0:S], cb[0:8, 1, 0:S], cb[0:8, 2, 0:S]
            rC = tmp[0:8]
            dve.wait_ge(rows_out, 2)
            do(ts(rA, PS[0:8, 0, :], small8[:, 0:1], None, ALU.add))
            do.tell(stt(rE, rA, -1.0, rA, ALU.mult, ALU.min), rows_e, 1)
            dve.wait_ge(rows_l, 2)
            do(ts(rA, rA, 0.0, None, ALU.max))
            do(tt(rA, rA, rE, ALU.add))
            do(ts(rC, rA, small8[:, 2:3], -1.0, ALU.mult, ALU.mult))
            do(dve.tensor_tensor_scan(rA, reset[0:8, :], rC, 0.0, ALU.mult, ALU.add))
            do.tell(ts(rB, rB, 0.5, 0.5, ALU.mult, ALU.add), rows_done, 1)
            dve.wait_ge(gates_ready, 1)
            dve.memset(Hs[:, 0], 0.0).then_inc(vec, 1)
            do.n += 1
            do.tell(dve.memset(cb[:], 0.0), cb_zeroed, 1)

            def recurrence(n, rw):
                q0 = n - GDN_PAIRS if rw else n
                dve.wait_ge(a_out, n)
                two = lambda mask: over_chunks(mask)
                if rw:
                    do(tt(LTs, blocks2(0)[:, :, 0:C], two(strictT), ALU.mult))
                    do.tell(tt(RB, blocks2(0)[:, :, C:P], two(inclT), ALU.mult), lts_ready, n)
                    do.tell(tt(AKs, blocks2(2)[:, :, 0:C], two(strictT), ALU.mult), aks_ready, q0)
                    do(tt(RK, blocks2(2)[:, :, C:P], two(inclT), ALU.mult))
                else:
                    do(tt(LTs, blocks2(0)[:, :, 0:C], chunks(S1), ALU.mult))
                    do.tell(tt(RB, blocks2(0)[:, :, C:P], chunks(S2), ALU.mult), lts_ready, n)
                    dve.wait_ge(vs_out, n)
                    do.tell(tt(AKV, bank(6), bcol.unsqueeze(2).broadcast_to([P, NCH, C]), ALU.mult), akv_ready, n)
                do(tt(XTs, LTs, over_chunks(level1T), ALU.mult))
                do.tell(tt(XTs, XTs, over_chunks(istack), ALU.add), xt_ready, 6 * (n - 1) + 1)
                dve.wait_ge(at_out, n)
                do(tt(Xs, bank(0), over_chunks(level(1)), ALU.mult))
                do.tell(tt(Xs, Xs, over_chunks(istack), ALU.add), xs_ready, 5 * (n - 1) + 1)
                dve.wait_ge(xtbd_ready, 6 * (n - 1) + 1)
                for lv in range(2, LEVELS + 1):
                    q = 5 * (n - 1) + lv - 1
                    dve.wait_ge(p_out, q)
                    do.tell(tt(Pst, bank(1), over_chunks(level(lv)), ALU.mult), ps_ready, q)
                    dve.wait_ge(q_out, q)
                    do.tell(tt(XTs, XTs, bank(3), ALU.add), xt_ready, 6 * (n - 1) + lv)
                    if lv < LEVELS:
                        do.tell(tt(Xs, Xs, bank(2), ALU.add), xs_ready, q + 1)
                if rw:
                    dve.wait_ge(akv_out, q0)
                    do.tell(dve.tensor_copy(AKV, bank(4)), akv_ready, n)
                    do(tt(KVe, bank(5), egC.unsqueeze(2).broadcast_to([P, NCH, C]), ALU.mult))
                for c in range(NCH - 1):
                    e = egC[:, c:c + 1]
                    if rw:
                        do(stt(te[:, 0], Hs[:, c], e, KVe[:, c], ALU.mult, ALU.add))
                    dve.wait_ge(dh_out, 7 * (n - 1) + c + 1)
                    if rw:
                        h = stt(Hs[:, c + 1], PS[:, c % 2, 0:C], e, te[:, 0], ALU.mult, ALU.add)
                    else:
                        h = stt(Hs[:, c + 1], Hs[:, c], e, PS[:, c % 2, 0:C], ALU.mult, ALU.add)
                    do.tell(h, hs_ready, 7 * (n - 1) + c + 1)
                    dve.wait_ge(w_out, 7 * (n - 1) + c + 1)
                    do.tell(tt(U[:, c + 1], U[:, c + 1], PS[:, 2 + c % 2, 0:C], ALU.add), us_ready,
                            7 * (n - 1) + c + 1)

            def silu(x, t):
                return stt(x, t, 1.0, x, ALU.add, ALU.mult)

            def gdn_pair(i):
                n = i + 1
                for j, x in enumerate((qf, kf, vf)):
                    dve.wait_ge(proj_act, i * 5 + j + 1)
                    w = [pc[:, tap * 3 + j:tap * 3 + j + 1] for tap in range(4)]
                    if j == 0:
                        for tap in range(4):
                            do(dve.tensor_copy(pc[:, tap * 3:tap * 3 + 3], t2T[:, bass.ds(i + tap * 12, 3, step=4)]))
                    do(ts(x, cb[:, j, 0:S], w[0], None, ALU.mult))
                    for tap in range(1, 3):
                        do(stt(x, cb[:, j, tap:tap + S], w[tap], x, ALU.mult, ALU.add))
                    do.tell(stt(x, cb[:, j, 3:3 + S], w[3], x, ALU.mult, ALU.add), proj_vec, i * 3 + j + 1)
                dve.wait_ge(proj_act, i * 5 + 5)
                do(silu(zf, th))
                for j, (x, t) in enumerate(((qf, S1), (kf, S2), (vf, S3))):
                    dve.wait_ge(d_in, i * 3 + j + 1)
                    do.tell(silu(x, t), lat_taken, i * 3 + j + 1)
                do(dve.tensor_copy(Gp, Grow[:, i]))
                do(dve.tensor_copy(Bp, Brow[:, i]))
                do(tt(chunks(tmp), chunks(Gp), over_chunks(istack), ALU.mult))
                do(dve.tensor_reduce(gcol, chunks(tmp), AX.X, ALU.add))
                do(tt(chunks(tmp), chunks(Bp), over_chunks(istack), ALU.mult))
                do(dve.tensor_reduce(bcol, chunks(tmp), AX.X, ALU.add))
                do(dve.tensor_copy(glast, chunks(Gp)[:, :, C - 1]))
                do(tt(chunks(S1), chunks(Gp), gcol.unsqueeze(2).broadcast_to([P, NCH, C]), ALU.subtract))
                do(ts(S1, S1, 0.0, None, ALU.min))
                do.tell(tt(chunks(S2), glast.unsqueeze(2).broadcast_to([P, NCH, C]), chunks(Gp), ALU.subtract),
                        d_exp, n)
                dve.wait_ge(head_rs, i * 3 + 2)
                do(stt(qf, qf, float(C) ** -0.5, rs[:, 0], ALU.mult, ALU.mult))
                do.tell(tt(kf, kf, rs[:, 1], ALU.mult), fm_ready, i * 3 + 1)
                dve.wait_ge(gates_ready, n + 1)
                do.tell(tt(tmp, kf, S2, ALU.mult), fm_ready, i * 3 + 2)
                do(dve.tensor_copy(R1[:, :, 1], chunks(qf)))
                do(tt(RT, qf, Gp, ALU.mult))
                do(stt(R1[:, :, 0], chunks(kf), -1.0, chunks(Bp), ALU.mult, ALU.mult))
                do.tell(tt(chunks(S3), R1[:, :, 0], chunks(Gp), ALU.mult), fm_ready, i * 3 + 3)
                do(tt(chunks(S2), chunks(S1), over_chunks(inclT), ALU.mult))
                do.tell(tt(chunks(S1), chunks(S1), over_chunks(strictT), ALU.mult), r1_ready, n)
                recurrence(n, False)
                dve.wait_ge(head_rs, i * 3 + 3)
                do(tt(post, PS[:, 4, :], rs[:, 0], ALU.mult))
                do.tell(stt(mix0[:, i], post, t2T[:, 59:60], zf, ALU.mult, ALU.mult), mix_ready, n)
            do.loop(GDN_PAIRS, GDN_STEPS, gdn_pair)

            TWO_PI = 6.283185307179586
            C1 = 6.28125
            C2 = 0.0019350051879882812
            C3 = TWO_PI - C1 - C2
            inv = cc("invfreq")
            for t in range(TT):
                do(ts(ang[:, t, 1], inv, posT[:, t:t + 1], None, ALU.mult))
                do(dve.tensor_copy(ang[:, t, 0], ang[:, t, 1]))
            MAGIC = 12582912.0
            do(ts(rot[:, :, 1], ang[:, :, 1], 1.0 / TWO_PI, MAGIC, ALU.mult, ALU.add))
            do(ts(rot[:, :, 0], ang[:, :, 0], 1.0 / TWO_PI, 0.25, ALU.mult, ALU.add))
            do(ts(rot[:, :, 0], rot[:, :, 0], MAGIC, None, ALU.add))
            do(ts(rot, rot, -MAGIC, None, ALU.add))
            for const in (C1, C2, C3):
                do(stt(ang, rot, -const, ang, ALU.mult, ALU.add))
            do(ts(ang[:, :, 0], ang[:, :, 0], TWO_PI / 4, None, ALU.add))
            do(ts(ang, ang, 3.1415925, None, ALU.min))
            do.tell(ts(ang, ang, -3.1415925, None, ALU.max), ang_ready, 1)

            for j, x in enumerate((dq[:, 0], dq[:, 1], dkv)):
                dve.wait_ge(lat_out, j + 1)
                do.tell(dve.tensor_copy(x, PS[:, j, :]), lat_taken, 12 + j + 1)
            dve.wait_ge(lat_out, 4)
            do(dve.tensor_copy(krope, PS[:, 3, 0:TT * ROPE].rearrange("p (t r) -> p t r", t=TT)))
            dve.wait_ge(gains_bc, 1)
            do(dve.tensor_copy(gains, PS[:, 4, 0:2 * QK].rearrange("p (a r) -> p a r", a=2)))
            dve.wait_ge(lat_rs, 2)
            for x, g, r in ((dq[:, 0], 56, 0), (dq[:, 1], 57, 0), (dkv, 58, 1)):
                do(stt(x, x, t2T[:, g:g + 1], rs[:, r], ALU.mult, ALU.mult))
            do.tell(dve.tensor_copy(cond_t[:, 0], cond[:]), lat_ready, 1)
            dve.wait_ge(trig_ready, 1)
            cosv = lambda t: trig[:, t, 0].unsqueeze(1).broadcast_to([P, 8, HALF])
            sinv = lambda t: trig[:, t, 1].unsqueeze(1).broadcast_to([P, 8, HALF])
            for t in range(TT):
                dve.wait_ge(tok_copied, t + 1)
                do(dve.tensor_copy(kall[:, t, :, NOPE:QK], krope[:, t].unsqueeze(1).broadcast_to([P, 8, ROPE])))
                for a, x in ((0, qall[:, t]), (1, kall[:, t])):
                    do(tt(sqh, x, x, ALU.mult))
                    do(dve.tensor_reduce(ssh[:, a], sqh, AX.X, ALU.add))
                do.tell(dve.tensor_copy(cond_t[:, 0], cond[:]), ssh_ready, t + 1)
                dve.wait_ge(rsh_ready, t + 1)
                for a, x in ((0, qall[:, t]), (1, kall[:, t])):
                    do(tt(x, x, ssh[:, a].unsqueeze(2).broadcast_to([P, 8, QK]), ALU.mult))
                    do(tt(x, x, gains[:, a].unsqueeze(1).broadcast_to([P, 8, QK]), ALU.mult))
                    x1, x2 = x[:, :, NOPE:NOPE + HALF], x[:, :, NOPE + HALF:QK]
                    do(tt(ropet[:, 0], x1, cosv(t), ALU.mult))
                    do(tt(ropet[:, 1], x2, sinv(t), ALU.mult))
                    do(tt(ropet[:, 2], x2, cosv(t), ALU.mult))
                    do(tt(ropet[:, 3], x1, sinv(t), ALU.mult))
                    do(tt(x1, ropet[:, 0], ropet[:, 1], ALU.subtract))
                    do(tt(x2, ropet[:, 2], ropet[:, 3], ALU.add))
            do.tell(dve.tensor_copy(cond_t[:, 0], cond[:]), heads_ready, 1)

            def attend(i):
                for a in range(2):
                    hd = i * 2 + a + 1
                    for t in range(TT):
                        dve.wait_ge(score_out, i * 8 + a * 4 + t + 1)
                        sc = PS[:, 2 + t, 0:(t + 1) * P]
                        do(tt(PS[:, 2 + t, t * P:(t + 1) * P], PS[:, 2 + t, t * P:(t + 1) * P], causal, ALU.add))
                        do(dve.tensor_reduce(negm[:, t:t + 1], sc, AX.X, ALU.max))
                        do.tell(ts(negm[:, t:t + 1], negm[:, t:t + 1], -float(QK) ** -0.5, None, ALU.mult),
                                max_ready, i * 8 + a * 4 + t + 1)
                    for t in range(TT):
                        dve.wait_ge(exp_ready, i * 8 + a * 4 + t + 1)
                        do(dve.reciprocal(rden[:, t:t + 1], den[:, t:t + 1]))
                        ins = ts(prob[:, t, 0:(t + 1) * P], prob[:, t, 0:(t + 1) * P], rden[:, t:t + 1], None, ALU.mult)
                        if t == TT - 1:
                            do.tell(ins, prob_ready, hd)
                        else:
                            do(ins)
                    dve.wait_ge(o_out, hd)
                    do.tell(dve.tensor_copy(mix0[a * C:(a + 1) * C, i + 4], PS[a * C:(a + 1) * C, 6 + a, :]),
                            o_ready, hd)
            do.loop(4, 30, attend)

            def residual(name, n, gate):
                def body(i):
                    for j in range(4):
                        dve.wait_ge(tile_out, i * 4 + TIL[name] + j + 1)
                        x = xT[:, i * 4 + j]
                        do.tell(stt(x, PS[:, j, :], gate_cols[:, bass.ds(i * 4 + j, 1)], x, ALU.mult, ALU.add),
                                tile_taken, i * 4 + TIL[name] + j + 5)
                do(dve.tensor_copy(gate_cols[:], modT[:, gate:gate + KT]))
                do.loop(n // 4, 0, body)

            def relu2(name):
                def body(i):
                    for j in range(4):
                        dve.wait_ge(tile_out, i * 4 + TIL[name] + j + 1)
                        do(ts(tmp_r[:, j % 2], PS[:, j, :], 0.0, None, ALU.max))
                        do.tell(tt(hid[:, i * 4 + j], tmp_r[:, j % 2], PS[:, j, :], ALU.mult),
                                tile_taken, i * 4 + TIL[name] + j + 5)
                do.loop(FT // 4, 4, body)

            mod_finish(0, 1, 16, 48)
            residual("o0", KT, GATE[0])
            norm(1)
            relu2("up0")
            residual("down0", KT, GATE[1])
            mod_finish(1, 2, 0, 48)
            norm(2)

            dve.wait_ge(h_ready, 3 * KT)
            do(tt(xx[:, :, 1:S], hT[:, :, 0:S - 1], hT[:, :, 1:S], ALU.subtract))
            do(ts(xx[:, :, 0:1], hT[:, :, 0:1], -1.0, None, ALU.mult))
            for q, (j, x) in enumerate(((1, xr), (4, xk), (5, xv), (0, xr), (2, xk), (3, xv))):
                if q >= 3:
                    dve.wait_ge(lora_out, (1, 2, 4)[q - 3])
                for k in range(KT):
                    col = t1T[:, j * KT + k:j * KT + k + 1]
                    ins = stt(x[:, k], xx[:, k], col, hT[:, k], ALU.mult, ALU.add)
                    if k < KT - 1:
                        do(ins)
                do.tell(ins, xmix_ready, q + 1)
            dve.wait_ge(lora_ready, 2)
            for j, r in ((2, P), (3, 32)):
                dve.wait_ge(proj_vec, 12 + j - 1)
                do.tell(ts(lora[0:r, j], lora[0:r, j], 0.5, 0.5, ALU.mult, ALU.add), lora_ready, j + 1)
            dve.wait_ge(zeroed, 2)
            do(dve.memset(Hs[:, 0], 0.0))

            def rwkv_pair(i):
                n = i + GDN_PAIRS + 1
                for a, b in ((0, 0), (1, 1), (2, 2), (3, 3), (4, 4), (5, 5), (6, 6)):
                    src = t1T[:, bass.ds(i + 48 + a * KT, 1)]
                    ins = dve.tensor_copy(pc[:, b:b + 1], src)
                    if a < 6:
                        do(ins)
                do.tell(ins, d_exp, n)
                w0c, a0c, kkc, kac, rkc, lgc, lbc = (pc[:, b:b + 1] for b in range(7))
                dve.wait_ge(proj_act, 20 + i * 5 + 2)
                do(ts(tmp, kf, kkc, None, ALU.mult))
                do.tell(tt(sq[:, 0], tmp, tmp, ALU.mult), head_sq, i * 4 + 13)
                dve.wait_ge(proj_act, 20 + i * 5 + 5)
                do(ts(S1, S1, -0.5 * DECAY, -0.5 * DECAY, ALU.mult, ALU.add))
                do(dve.tensor_tensor_scan(S3, reset, S1, 0.0, ALU.mult, ALU.add))
                do.tell(tt(S1, S3, S1, ALU.subtract), d_in, 12 + i + 1)
                do(ts(S2, S2, 0.5, 0.5, ALU.mult, ALU.add))
                do(ts(th, S2, -1.0, kac, ALU.add, ALU.mult))
                do(stt(kf, th, 1.0, kf, ALU.add, ALU.mult))
                do.tell(stt(sq[:, 1], qf, rkc, kf, ALU.mult, ALU.mult), head_sq, i * 4 + 14)
                dve.wait_ge(head_rs, 12 + i * 2 + 1)
                do(tt(tmp, tmp, rs[:, 0], ALU.mult))
                dve.wait_ge(gates_ready, GDN_PAIRS + 1 + i + 1)
                do(tt(R1[:, :, 1], chunks(qf), chunks(S3), ALU.mult))
                do(tt(th, tmp, S2, ALU.mult))
                do.tell(tt(S2, th, RT, ALU.mult), fm_ready, 12 + i * 3 + 1)
                do.tell(tt(S3, kf, RT, ALU.mult), fm_ready, 12 + i * 3 + 2)
                do.tell(stt(R1[:, :, 0], chunks(tmp), -1.0, chunks(S1), ALU.mult, ALU.mult),
                        fm_ready, 12 + i * 3 + 3)
                dve.wait_ge(head_ss, 8 + i * 4 + 2)
                do.tell(tt(post, PS[:, 7, :], vf, ALU.mult), post_a, i + 1)
                do.tell(ts(te[:, 1, 0:1], w0c, 1.0, None, ALU.mult), r1_ready, n)
                recurrence(n, True)
                dve.wait_ge(y_out, n)
                do.tell(dve.tensor_copy(sq[:, 0], PS[:, 4, :]), head_sq, i * 4 + 15)
                dve.wait_ge(head_ss, 8 + i * 4 + 3)
                do(stt(tmp, PS[:, 5, :], -1.0 / C, sq[:, 0], ALU.mult, ALU.add))
                do.tell(tt(sq[:, 1], tmp, tmp, ALU.mult), head_sq, i * 4 + 16)
                dve.wait_ge(head_rs, 12 + i * 2 + 2)
                do(tt(tmp, tmp, rs[:, 1], ALU.mult))
                do(ts(tmp, tmp, lgc, lbc, ALU.mult, ALU.add))
                do(tt(tmp, tmp, post, ALU.add))
                do.tell(tt(hT[:, i], tmp, zf, ALU.mult), mix_ready, n)
            do.loop(RWKV_PAIRS, RWKV_STEPS, rwkv_pair)

            residual("o1", KT, GATE[0])
            norm(3)
            relu2("up1")
            residual("down1", KT, GATE[1])

        @block.scalar
        def _(act):
            do = Steps(act, act_)
            fn = act.activation
            act.wait_ge(tabs_ready, 1)
            do.tell(fn(cond_t[:, 1], cond_t[:, 0], ACT.Tanh), cond_tanh, 1)
            for k in range(KT):
                act.wait_ge(x_T, k + 1)
                do.tell(fn(xT[:, k], PS[:, 4 + k % 2, :], ACT.Copy), x_ready, k + 1)

            def rsqrt(o, ps, scale, eps, sem_, value):
                do(fn(o, ps, ACT.Ln, scale=scale, bias=eps))
                do.tell(fn(o, o, ACT.Exp, scale=-0.5), sem_, value)

            def norm(idx):
                for k in range(KT):
                    if idx:
                        act.wait_ge(tile_taken, X_DONE[idx] - KT + k + 1)
                    if k >= 2:
                        act.wait_ge(sq_used, idx * KT + k - 1)
                    do.tell(fn(sq[:, k % 2], xT[:, k], ACT.Square), sq_ready, idx * KT + k + 1)
                act.wait_ge(sq_used, idx * KT + KT)
                rsqrt(rs[:, 0], PS[:, 6, :], 1.0 / D, eps6, rstd_ready, idx + 1)

            norm(0)
            act.wait_ge(rows_e, 1)
            rE, rB = cb[0:8, 1, 0:S], cb[0:8, 2, 0:S]
            do(fn(rE, rE, ACT.Exp))
            do(fn(small8[:, 2:3], small8[:, 1:2], ACT.Exp))
            do.tell(fn(rE, rE, ACT.Ln, bias=one[0:8]), rows_l, 1)
            do.tell(fn(rB, PS[0:8, 1, :], ACT.Tanh, scale=0.5), rows_l, 2)
            act.wait_ge(rows_bc, 1)
            for p in range(GDN_PAIRS):
                do(fn(Grow[:, p], PS[:, 2 * p, :], ACT.Copy))
                ins = fn(Brow[:, p], PS[:, 2 * p + 1, :], ACT.Copy)
                if p < GDN_PAIRS - 1:
                    do(ins)
            do.tell(ins, gates_ready, 1)

            def halves(dst, src, sem_=None, value=None):
                do(fn(dst[0:C, :, 0:C], src[0:C], ACT.Copy))
                ins = fn(dst[C:P, :, C:P], src[C:P], ACT.Copy)
                if sem_ is None:
                    do(ins)
                else:
                    do.tell(ins, sem_, value)

            def recurrence(n, rw):
                q0 = n - GDN_PAIRS if rw else n
                act.wait_ge(tok_out, (4 + q0 * 3 - 2 + 4) if rw else q0 * 2 - 1)
                do.tell(fn(btok, blocks2(4), ACT.Copy), tok_taken, 3 * n - 2)
                act.wait_ge(tok_out, (4 + q0 * 3 - 1 + 4) if rw else q0 * 2)
                if rw:
                    do.tell(fn(atok, blocks2(6), ACT.Copy), tok_taken, 3 * n - 1)
                    act.wait_ge(tok_out, 8 + q0 * 3)
                    do.tell(fn(ktok, blocks2(4), ACT.Copy), tok_taken, 3 * n)
                    act.wait_ge(vs_out, n)
                    do.tell(fn(Vs, bank(6), ACT.Copy), vs_ready, q0)
                else:
                    do.tell(fn(atok[:, 0:4], blocks2(6)[:, 0:4], ACT.Copy), tok_taken, 3 * n - 1)
                    do.tell(fn(atok[:, 4:8], blocks2(6)[:, 4:8], ACT.Copy), tok_taken, 3 * n)
                act.wait_ge(lts_ready, n)
                halves(LTbd, LTs, lt_bd, n)
                if rw:
                    act.wait_ge(aks_ready, q0)
                    halves(AKbd, AKs)
                for lv in range(1, LEVELS + 1):
                    if lv > 1:
                        act.wait_ge(ps_ready, 5 * (n - 1) + lv - 1)
                        halves(Pbd, Pst, pbd_ready, 5 * (n - 1) + lv - 1)
                    act.wait_ge(xt_ready, 6 * (n - 1) + lv)
                    halves(XTbd, XTs, xtbd_ready, 6 * (n - 1) + lv)
                if rw:
                    halves(Vbd, Vs)
                act.wait_ge(u0_out, n)
                do.tell(fn(U, bank(6), ACT.Copy), u0_ready, n)
                halves(WTbd, bank(7), wt_ready, n)
                act.wait_ge(us_ready, 7 * n)
                act.wait_ge(hs_ready, 7 * n)
                halves(Hbd, Hs[:, 0:NCH])
                halves(ubd, U, hu_bd, n)

            def gdn_pair(i):
                n = i + 1
                for j in range(3):
                    act.wait_ge(proj_out, i * 4 + j + 5)
                    do.tell(fn(cb[:, j, 3:3 + S], PS[:, j, :], ACT.Copy), proj_act, i * 5 + j + 1)
                act.wait_ge(proj_out, i * 4 + 8)
                do.tell(fn(zf, PS[:, 3, :], ACT.Copy, scale=0.5), proj_act, i * 5 + 4)
                do.tell(fn(th, PS[:, 3, :], ACT.Tanh, scale=0.5), proj_act, i * 5 + 5)
                for j, (x, t) in enumerate(((qf, S1), (kf, S2), (vf, S3))):
                    act.wait_ge(proj_vec, i * 3 + j + 1)
                    do.tell(fn(t, x, ACT.Tanh), d_in, i * 3 + j + 1)
                for j, x in enumerate((qf, kf)):
                    act.wait_ge(lat_taken, i * 3 + j + 1)
                    do.tell(fn(sq[:, j], x, ACT.Square), head_sq, i * 3 + j + 1)
                act.wait_ge(head_ss, i * 2 + 1)
                for j in range(2):
                    rsqrt(rs[:, j], PS[:, 4 + j, :], 1.0, eps12, head_rs, i * 3 + j + 1)
                act.wait_ge(d_exp, n)
                do(fn(S1, S1, ACT.Exp))
                do(fn(S2, S2, ACT.Exp))
                do(fn(egC, glast, ACT.Exp))
                do.tell(fn(Gp, Gp, ACT.Exp), gates_ready, n + 1)
                act.wait_ge(fm_ready, i * 3 + 1)
                halves(FB[0], chunks(kf), fb_act, i * 2 + 1)
                act.wait_ge(fm_ready, i * 3 + 2)
                halves(FB[1], chunks(tmp), fb_act, i * 2 + 2)
                recurrence(n, False)
                act.wait_ge(y_out, n)
                do.tell(fn(sq[:, 0], PS[:, 4, :], ACT.Square), head_sq, i * 3 + 3)
                act.wait_ge(head_ss, i * 2 + 2)
                rsqrt(rs[:, 0], PS[:, 5, :], 1.0 / C, eps6, head_rs, i * 3 + 3)
            act.wait_ge(zeroed, 1)
            act.wait_ge(cb_zeroed, 1)
            do.loop(GDN_PAIRS, GDN_ACT_STEPS, gdn_pair)

            act.wait_ge(ang_ready, 1)
            do.tell(fn(trig, ang, ACT.Sin), trig_ready, 1)
            for j, x in enumerate((dq[:, 0], dq[:, 1], dkv)):
                act.wait_ge(lat_taken, 12 + j + 1)
                if j == 2:
                    act.wait_ge(lat_ss, 1)
                do.tell(fn(sq[:, j % 2], x, ACT.Square), lat_sq, j + 1)
            act.wait_ge(lat_ss, 2)
            rsqrt(rs[:, 0], PS[:, 5, :], 1.0 / 256, eps6, lat_rs, 1)
            act.wait_ge(lat_ss, 3)
            rsqrt(rs[:, 1], PS[:, 6, :], 1.0 / 128, eps6, lat_rs, 2)
            for t in range(TT):
                act.wait_ge(tok_proj, t + 1)
                for j in range(2):
                    do(fn(qall[:, t, j * 4:j * 4 + 4], PS[:, j, 0:384].rearrange("p (h d) -> p h d", h=4), ACT.Copy))
                kv = [PS[:, 2 + j, :].rearrange("p (h d) -> p h d", h=4) for j in range(2)]
                for j in range(2):
                    do(fn(kall[:, t, j * 4:j * 4 + 4, 0:NOPE], kv[j][:, :, 0:NOPE], ACT.Copy))
                    ins = fn(vall[:, t, j * 4:j * 4 + 4], kv[j][:, :, NOPE:P], ACT.Copy)
                    if j == 0:
                        do(ins)
                do.tell(ins, tok_copied, t + 1)
                act.wait_ge(ssh_ready, t + 1)
                do(fn(ssh, ssh, ACT.Ln, scale=1.0 / QK, bias=eps6))
                do.tell(fn(ssh, ssh, ACT.Exp, scale=-0.5), rsh_ready, t + 1)

            def attend(i):
                for a in range(2):
                    hd = i * 2 + a + 1
                    act.wait_ge(qkT_out, hd)
                    do(fn(qhT[0:QK], PS[0:QK, 0, :], ACT.Copy))
                    do.tell(fn(khT[0:QK], PS[0:QK, 1, :], ACT.Copy), qkT_ready, hd)
                    for t in range(TT):
                        act.wait_ge(max_ready, i * 8 + a * 4 + t + 1)
                        do.tell(fn(prob[:, t, 0:(t + 1) * P], PS[:, 2 + t, 0:(t + 1) * P], ACT.Exp,
                                   bias=negm[:, t:t + 1], scale=float(QK) ** -0.5, accum_out=den[:, t:t + 1]),
                                exp_ready, i * 8 + a * 4 + t + 1)
                    act.wait_ge(pT_out, hd)
                    for kt in range(TT):
                        ins = fn(probT[:, kt, kt * P:S], PS[:, 2 + kt, kt * P:S], ACT.Copy)
                        if kt < TT - 1:
                            do(ins)
                    do.tell(ins, pT_ready, hd)
            do.loop(4, 8, attend)
            norm(1)
            norm(2)

            for j, (m_, f) in enumerate(((64, ACT.Tanh), (64, ACT.Copy), (P, ACT.Tanh), (32, ACT.Tanh))):
                act.wait_ge(lora_out, j + 1)
                ins = fn(lora[0:m_, j], PS[0:m_, j, :], f, scale=0.5 if j >= 2 else 1.0)
                if j < 2:
                    do.tell(ins, lora_ready, j + 1)
                else:
                    do.tell(ins, proj_vec, 12 + j - 1)
            act.wait_ge(zeroed, 2)

            def rwkv_pair(i):
                n = i + GDN_PAIRS + 1
                w0c, a0c = pc[:, 0:1], pc[:, 1:2]
                for j, x in enumerate((qf, kf, vf)):
                    act.wait_ge(proj_out, 20 + i * 6 + j + 1)
                    do.tell(fn(x, PS[:, j, :], ACT.Copy), proj_act, 20 + i * 5 + j + 1)
                act.wait_ge(d_exp, n)
                act.wait_ge(proj_out, 20 + i * 6 + 4)
                do.tell(fn(S1, PS[:, 3, :], ACT.Tanh, scale=0.5, bias=w0c), proj_act, 20 + i * 5 + 4)
                act.wait_ge(proj_out, 20 + i * 6 + 5)
                do.tell(fn(S2, PS[:, 4, :], ACT.Tanh, scale=0.5, bias=a0c), proj_act, 20 + i * 5 + 5)
                act.wait_ge(proj_out, 20 + i * 6 + 6)
                do(fn(zf, PS[:, 5, :], ACT.Copy))
                act.wait_ge(head_ss, 8 + i * 4 + 1)
                rsqrt(rs[:, 0], PS[:, 6, :], 1.0, eps12, head_rs, 12 + i * 2 + 1)
                act.wait_ge(d_in, 12 + i + 1)
                do(fn(RT, S3, ACT.Exp, scale=-1.0))
                do(fn(egC, chunks(S3)[:, :, C - 1], ACT.Exp))
                do(fn(S3, S3, ACT.Exp))
                do.tell(fn(S1, S1, ACT.Exp), gates_ready, GDN_PAIRS + 1 + i + 1)
                act.wait_ge(fm_ready, 12 + i * 3 + 1)
                halves(FB[0], chunks(S2), fb_act, 8 + i * 2 + 1)
                act.wait_ge(fm_ready, 12 + i * 3 + 2)
                halves(FB[1], chunks(S3), fb_act, 8 + i * 2 + 2)
                recurrence(n, True)
                act.wait_ge(head_ss, 8 + i * 4 + 4)
                rsqrt(rs[:, 1], PS[:, 6, :], 1.0 / C, epsgn, head_rs, 12 + i * 2 + 2)
            do.loop(RWKV_PAIRS, RWKV_ACT_STEPS, rwkv_pair)
            norm(3)
            for q in range(2 * TT):
                t, hf = divmod(q, 2)
                act.wait_ge(xo_T, q + 1)
                if t >= 2:
                    act.wait_ge(out_landed[t % 2], 16)
                do.tell(fn(xout[:, t % 2, hf * S:(hf + 1) * S], PS[:, q % 2, :], ACT.Copy), xo_ready, q + 1)

        @block.gpsimd
        def _(pool):
            do = Steps(pool, pool_)

            def copy(dst, src):
                pool.wait_ge(cst_landed, 16)
                return pool.tensor_copy(dst, src)

            def zero(count):
                for b in FB:
                    do(pool.memset(b, 0.0))
                do.tell(pool.memset(Vbd, 0.0), zeroed, count)

            def expand(dst, src, value):
                do(pool.tensor_tensor(dst[0:C, :, 0:C], src[0:C], over_chunks(ones[:, 0:C])[0:C], ALU.mult))
                do.tell(pool.tensor_tensor(dst[C:P, :, C:P], src[C:P], over_chunks(ones[:, 0:C])[C:P], ALU.mult), fb_pool, value)

            pool.wait_ge(mod_ready, 1)
            zero(1)

            def gdn_pair(i):
                pool.wait_ge(fm_ready, i * 3 + 3)
                expand(FB[2], chunks(S3), i * 2 + 1)
                expand(FB[3], chunks(vf), i * 2 + 2)
            do.loop(GDN_PAIRS, 2, gdn_pair)

            def modulation(layer, first, blocks, ring, acc, part, fills):
                wm = I["w_mod"][layer].rearrange("(k p) n -> p k n", p=P)

                def fetch(s, col):
                    pool.dma_start(ring[:, s], wm[:, :, col]).then_inc(pmw_landed[s], 16)

                def body(i):
                    for s in range(2):
                        fetch(s, bass.ds(i * 512 + first + s * 256, 256))
                    for s in range(2):
                        pool.wait_ge(pmw_landed[s], i * 16 + 16 * (fills + 1))
                        w = ring[:, s]
                        do(pool.tensor_tensor(w, w, cond[:].unsqueeze(2).broadcast_to([P, KT, 256]), ALU.mult))
                        do(pool.tensor_tensor(w[:, 0:4], w[:, 0:4], w[:, 4:8], ALU.add))
                        do(pool.tensor_tensor(w[:, 0:2], w[:, 0:2], w[:, 2:4], ALU.add))
                        do(pool.tensor_tensor(part[:, s], w[:, 0], w[:, 1], ALU.add))
                        do(copy(acc[:, bass.ds(i * 512 + s * 256, 256)], part[:, s]))
                do.loop(blocks // 2, 10, body)

            pool.wait_ge(mix_ready, GDN_PAIRS)
            pool.wait_ge(heads_ready, 1)

            def slices(i):
                for a in range(2):
                    hd = i * 2 + a + 1
                    do(copy(qh, qall[:, :, i * 2 + a]))
                    do(copy(kh, kall[:, :, i * 2 + a]))
                    do.tell(copy(vh, vall[:, :, i * 2 + a]), hslice, hd)
                    pool.wait_ge(o_ready, hd)
            do.loop(4, 4, slices)
            modulation(0, 2048, 16, mwring2, macc2, mblk2, 0)
            do.tell(pool.memset(mblk2, 0.0), macc_ready, 2)
            pool.wait_ge(mod_ready, 2)
            pool.wait_ge(tile_taken, 4 + 8)
            modulation(1, 0, 24, mwring1, macc1, mblk1, 8)
            do.tell(pool.memset(mblk1, 0.0), macc_ready, 3)
            pool.wait_ge(xmix_ready, 6)
            pool.wait_ge(lora_out, 4)
            zero(2)

            def rwkv_pair(i):
                pool.wait_ge(fm_ready, 12 + i * 3 + 3)
                expand(FB[2], R1[:, :, 0], 8 + i * 2 + 1)
                expand(FB[3], chunks(vf), 8 + i * 2 + 2)
            do.loop(RWKV_PAIRS, 2, rwkv_pair)


def constants():
    import numpy as np

    t = np.zeros((P, NCONST), np.float32)

    def put(name, a):
        at, n = CONST_COLS[name]
        t[:a.shape[0], at:at + n] = a
    j, i = np.meshgrid(np.arange(P) % C, np.arange(C), indexing="ij")
    put("ident", np.eye(P))
    put("ones", np.ones((P, P)))
    put("blk", np.kron(np.eye(2), np.ones((C, C))))
    put("istack", j == i)
    put("strictT", j < i)
    put("inclT", j <= i)

    def doubling(r, c, n):
        return (r >> n == c >> n) & ((r >> (n - 1)) % 2 == 1) & ((c >> (n - 1)) % 2 == 0)
    put("level", np.concatenate([doubling(j, i, n) for n in range(1, LEVELS + 1)], 1))
    put("level1T", doubling(i, j, 1))
    a, b = np.meshgrid(np.arange(P), np.arange(P), indexing="ij")
    put("causal", np.where(b <= a, 0.0, -1e30))
    put("reset", np.tile((np.arange(S) % C != 0).astype(np.float32), (P, 1)))
    put("invfreq", np.tile(np.float32(10000.0) ** (-np.arange(0, ROPE, 2, dtype=np.float32) / ROPE), (P, 1)))
    heads = np.zeros((8, GDN_PAIRS * P))
    for h in range(8):
        heads[h, h * C:(h + 1) * C] = 1
    put("headsel", heads)
    put("eps", np.tile(np.array([EPS, L2_EPS, GN_EPS, 1.0]), (P, 1)))
    return t


def kernel(**inputs):
    import numpy as _np
    import concourse.bacc as _bacc
    from concourse import mybir as _mybir
    from concourse.bass_utils import run_bass_kernel_spmd as _run

    nc = _bacc.Bacc("TRN2", target_bir_lowering=False, num_devices=1)
    arrays, args = {}, {}
    for name, a in dict(inputs, const=constants()).items():
        a = _np.ascontiguousarray(a)
        arrays[f"in_{name}_dram"] = a
        args[name] = nc.dram_tensor(f"in_{name}_dram", a.shape, _mybir.dt.from_np(a.dtype), kind="ExternalInput").ap()
    out = nc.dram_tensor("out_0_dram", (1, S, D), F32, kind="ExternalOutput").ap()
    build(nc, args, out)
    r = _run(nc, [arrays], core_ids=[0])
    return r.results[0]["out_0_dram"]
```

```python
from contextlib import ExitStack

import concourse.bass as bass
from concourse import mybir

F32 = mybir.dt.float32
I32 = mybir.dt.int32
ALU = mybir.AluOpType
ACT = mybir.ActivationFunctionType
AX = mybir.AxisListType

P = 128
S = 512
D = 1024
KT = D // P
TT = S // P
C = 64
NCH = S // C
FF = 4096
FT = FF // P
GDN_W = 512
GDN_PAIRS = 4
RWKV_PAIRS = 8
EVAC = {False: [3, 5], True: [3, 5]}
FILL = {False: (8, 2, 2, 1, 2, 1), True: (6, 2, 1, 1, 1, 1)}
GDN_STEPS, GDN_ACT_STEPS, RWKV_STEPS, RWKV_ACT_STEPS = 32, 25, 32, 29
GATE_COL = 2048
DQ_COL, DKV_COL, KROPE_COL = 2064, 2320, 2448
REST = 2480 - GATE_COL
QK = 96
NOPE, ROPE, HALF = 64, 32, 16
LEVELS = 6
EPS, L2_EPS, GN_EPS = 1e-6, 1e-12, 64e-5
DECAY = 0.6065306597126334

CONST_COLS = {}
_at = 0
for _name, _n in (("ident", P), ("ones", P), ("blk", P), ("istack", C), ("strictT", C), ("inclT", C),
                  ("level", LEVELS * C), ("level1T", C), ("causal", P), ("reset", S), ("invfreq", HALF),
                  ("headsel", GDN_PAIRS * P), ("eps", 4)):
    CONST_COLS[_name] = (_at, _n)
    _at += _n
NCONST = _at

T1 = {"mu": 0, "w0": 48, "a0": 56, "k_k": 64, "k_a": 72, "r_k": 80, "ln_g": 88, "ln_b": 96}
T1_ROWS = 104
T2 = {"conv": 0, "c": 48, "qng": 56, "kvng": 58, "gdng": 59}
T2_ROWS = 60


def build(nc, I, out):
    with ExitStack() as ctx:
        def sb(name, shape, dt=F32):
            return ctx.enter_context(nc.sbuf_tensor(name, shape, dt))

        def sem(name):
            return ctx.enter_context(nc.semaphore(name))

        PS = ctx.enter_context(nc.psum_tensor("PS", [P, 8, S], F32))
        cst = sb("cst", [P, NCONST])

        def cc(name):
            at, n = CONST_COLS[name]
            return cst[:, at:at + n]

        ident, ones, blk, istack = cc("ident"), cc("ones"), cc("blk"), cc("istack")
        strictT, inclT, level1T, causal, reset = cc("strictT"), cc("inclT"), cc("level1T"), cc("causal"), cc("reset")
        eps6, eps12, epsgn = (cc("eps")[:, j:j + 1] for j in range(3))

        def level(n):
            return cc("level")[:, (n - 1) * C:n * C]

        def over_chunks(mask, n=NCH):
            return mask.unsqueeze(1).broadcast_to([P, n, C])

        def chunks(x):
            return x.rearrange("p (c t) -> p c t", c=NCH)

        def tokens(x):
            return x.rearrange("p c t -> p (c t)")

        def bank(j):
            return PS[:, j, :].rearrange("p (c t) -> p c t", c=NCH)

        def blocks2(j):
            return PS[:, j:j + 2, :].rearrange("p b (c t) -> p (b c) t", c=4)

        xT = sb("xT", [P, KT, S])
        hT = sb("hT", [P, KT, S])
        bmodT = sb("bmodT", [P, 96])
        t1T = sb("t1T", [P, T1_ROWS])
        t2T = sb("t2T", [P, T2_ROWS])
        modT = sb("modT", [P, 48])
        cond = sb("cond", [P, KT])
        cond_t = sb("cond_t", [P, 2, KT])
        sq = sb("sq", [P, 2, S])
        rs = sb("rs", [P, 2, S])
        ones1 = sb("ones1", [P, 1])
        ARENA = 40400
        arena = sb("arena", [P, ARENA])
        cursor = [0]

        def region(*shape):
            n = 1
            for x in shape:
                n *= x
            a = arena[:, cursor[0]:cursor[0] + n]
            cursor[0] += n
            assert cursor[0] <= ARENA, (cursor[0], shape)
            if len(shape) == 2:
                a = a.rearrange("p (a b) -> p a b", a=shape[0])
            if len(shape) == 3:
                a = a.rearrange("p (a b c) -> p a b c", a=shape[0], b=shape[1])
            return a

        xtok = region(TT, D)
        tabs = region(3, P)
        pos_i = region(P).bitcast(I32)
        pos_f = region(P)
        mwring = region(2, KT, 256)
        macc = region(6 * D)
        mblk = region(2, 256)
        cursor[0] = 0
        mix0 = region(KT, S)
        pc = region(16)
        pw = region(4, KT, P)
        FB_AT = cursor[0]
        FB = [region(NCH, P) for _ in range(4)]
        TOK_AT = cursor[0]
        btok, ktok, atok, Vbd = (region(NCH, P) for _ in range(4))
        LTbd, AKbd, XTbd, Pbd = FB
        WTbd, Hbd, ubd = Pbd, XTbd, AKbd
        R1 = region(NCH, 2, C)
        RB, RK, LTs, XTs, Xs, Pst, Vs, KVe = (region(NCH, C) for _ in range(8))
        AKs, AKV, U = Pst, LTs, Xs
        Hs = region(NCH + 1, C)
        te = region(2, C)
        egC = region(NCH)
        S1, S2, S3, RT, qf, kf, vf, zf, th, tmp, post = (region(S) for _ in range(11))
        PAIR_END = cursor[0]
        Grow, Brow = region(GDN_PAIRS, S), region(GDN_PAIRS, S)
        Gp, Bp = post, region(S)
        cb = region(3, S + 3)
        gcol, bcol, glast = region(NCH), region(NCH), region(NCH)
        gatew = region(KT, 16)
        mwring2 = region(2, KT, P)
        MACC2_AT = cursor[0]
        macc2 = region(4 * D)
        cursor[0] = PAIR_END
        xr, xk = region(KT, S), region(KT, S)
        lora = region(4, S)
        lw = region(4, P)
        xv = mix0
        xx = arena[:, FB_AT:FB_AT + KT * S].rearrange("p (k s) -> p k s", k=KT)
        lw1 = arena[:, TOK_AT:TOK_AT + KT * 288].rearrange("p (k f) -> p k f", k=KT)
        cursor[0] = KT * S
        mlaw = region(KT, 416)
        uq = region(2, 768)
        ukv = region(D)
        dq, dkv = region(2, S), region(S)
        grow = region(2, QK)
        gains = region(2, QK)
        krope = region(TT, ROPE)
        ang, rot, trig = region(TT, 2, HALF), region(TT, 2, HALF), region(TT, 2, HALF)
        qall, kall = region(TT, 8, QK), region(TT, 8, QK)
        vall = region(TT, 8, C)
        sqh = region(8, QK)
        ropet = region(4, 8, HALF)
        ssh = region(2, 8)
        qh, kh, vh = region(TT, QK), region(TT, QK), region(TT, C)
        qhT, khT = region(S), region(S)
        prob = region(TT, S)
        probT = region(TT, S)
        negm, den, rden = region(TT), region(TT), region(TT)
        assert cursor[0] <= MACC2_AT
        cursor[0] = 0
        hid = region(FT, S)
        wring = region(2, KT, 256)
        mwring1 = region(2, KT, 256)
        macc1 = region(6 * D)
        mblk1 = region(2, 256)
        xout = region(2, D)

        tabs_landed, x_landed, cst_landed = sem("tabs_landed"), sem("x_landed"), sem("cst_landed")
        tabs_T, tabs_ready, x_T, x_ready = sem("tabs_T"), sem("tabs_ready"), sem("x_T"), sem("x_ready")
        cond_tanh, cond_ready = sem("cond_tanh"), sem("cond_ready")
        mw_landed = [sem("mw0_landed"), sem("mw1_landed")]
        pmw_landed = [sem("pmw0_landed"), sem("pmw1_landed")]
        lw1_landed = sem("lw1_landed")
        mw_used = sem("mw_used")
        macc_ready, mod_summed, mod_ready = sem("macc_ready"), sem("mod_summed"), sem("mod_ready")
        vec, act_, pool_ = sem("vec_steps"), sem("act_steps"), sem("pool_steps")
        sq_ready, sq_used, ss_ready, rstd_ready, h_ready = (
            sem("sq_ready"), sem("sq_used"), sem("ss_ready"), sem("rstd_ready"), sem("h_ready"))
        w_landed = [sem("w0_landed"), sem("w1_landed")]
        w_used, tile_out, tile_taken = sem("w_used"), sem("tile_out"), sem("tile_taken")
        zeroed = sem("zeroed")
        gw_landed, rows_out, rows_t, rows_e, rows_l, rows_done, rows_bc, gates_ready = (
            sem("gw_landed"), sem("rows_out"), sem("rows_t"), sem("rows_e"), sem("rows_l"), sem("rows_done"),
            sem("rows_bc"), sem("gates_ready"))
        pw_landed = [sem(f"pw{j}_landed") for j in range(4)]
        lw_landed, low_out, proj_out, proj_act, proj_vec = sem("lw_landed"), sem("low_out"), sem("proj_out"), sem("proj_act"), sem("proj_vec")
        head_sq, head_ss, head_rs = sem("head_sq"), sem("head_ss"), sem("head_rs")
        d_in, d_exp, fm_ready = sem("d_in"), sem("d_exp"), sem("fm_ready")
        fb_act, fb_pool, r1_ready = sem("fb_act"), sem("fb_pool"), sem("r1_ready")
        a_out, tok_out, tok_taken, lts_ready, lt_bd, aks_ready = (
            sem("a_out"), sem("tok_out"), sem("tok_taken"), sem("lts_ready"), sem("lt_bd"), sem("aks_ready"))
        vs_out, vs_ready, vbd_ready = sem("vs_out"), sem("vs_ready"), sem("vbd_ready")
        at_out, xs_ready, xt_ready, xtbd_ready = sem("at_out"), sem("xs_ready"), sem("xt_ready"), sem("xtbd_ready")
        x_out, p_out, ps_ready, pbd_ready, q_out = sem("x_out"), sem("p_out"), sem("ps_ready"), sem("pbd_ready"), sem("q_out")
        akv_out, akv_ready, kv_ready, u0_out, u0_ready, wt_out = (
            sem("akv_out"), sem("akv_ready"), sem("kv_ready"), sem("u0_out"), sem("u0_ready"), sem("wt_out"))
        dh_out, hs_ready, w_out, us_ready, hu_bd, y_out = (
            sem("dh_out"), sem("hs_ready"), sem("w_out"), sem("us_ready"), sem("hu_bd"), sem("y_out"))
        post_a, post_b, post_c, mix_ready = sem("post_a"), sem("post_b"), sem("post_c"), sem("mix_ready")
        mla_landed, lat_out, lat_taken, lat_sq, lat_ss, lat_rs, lat_ready = (
            sem("mla_landed"), sem("lat_out"), sem("lat_taken"), sem("lat_sq"), sem("lat_ss"), sem("lat_rs"),
            sem("lat_ready"))
        ang_ready, trig_ready, gains_bc, tok_proj, tok_copied, ssh_ready, rsh_ready, heads_ready = (
            sem("ang_ready"), sem("trig_ready"), sem("gains_bc"), sem("tok_proj"), sem("tok_copied"),
            sem("ssh_ready"), sem("rsh_ready"), sem("heads_ready"))
        hslice, qkT_out, qkT_ready, score_out, max_ready, exp_ready, prob_ready = (
            sem("hslice"), sem("qkT_out"), sem("qkT_ready"), sem("score_out"), sem("max_ready"), sem("exp_ready"),
            sem("prob_ready"))
        pT_out, pT_ready, o_out, o_ready = sem("pT_out"), sem("pT_ready"), sem("o_out"), sem("o_ready")
        xmix_ready, lora_out, lora_ready, xx_ready = sem("xmix_ready"), sem("lora_out"), sem("lora_ready"), sem("xx_ready")
        xo_T, xo_ready, out_landed = sem("xo_T"), sem("xo_ready"), [sem("out0_landed"), sem("out1_landed")]
        cb_zeroed = sem("cb_zeroed")
        class Steps:

            def __init__(self, eng, sem_):
                self.eng, self.sem, self.n, self.off = eng, sem_, 0, 0

            def __call__(self, ins):
                self.n += 1
                ins.then_inc(self.sem, 1)
                self.eng.wait_ge(self.sem, self.off + self.n)

            def tell(self, ins, sem_, value):
                ins.then_inc(sem_, 1)
                self.eng.wait_ge(sem_, value)

            def loop(self, count, steps, body):
                start = self.n
                with self.eng.Fori(0, count) as i:
                    self.off = i * steps
                    body(i)
                assert self.n - start == steps, f"the loop has {self.n - start} steps"
                self.off, self.n = 0, start + count * steps

        small8 = sb("small8", [8, 4])
        posT = sb("posT", [P, TT])
        gate_cols = sb("gate_cols", [P, KT])
        tmp_r = sq
        one = cc("eps")[:, 3:4]

        BLK = {"o0": 0, "up0": 4, "down0": 20, "o1": 36, "up1": 40, "down1": 56}
        TIL = {"o0": 0, "up0": 8, "down0": 40, "o1": 48, "up1": 56, "down1": 88}
        X_DONE = [None, 4 + 8, 4 + 48, 4 + 56]
        SHIFT, SCALE, GATE = (0, 24), (8, 32), (16, 40)

        block = ctx.enter_context(nc.Block())

        @block.sync
        def _(sp):
            sp.dma_start(cst[:], I["const"][:, :]).then_inc(cst_landed, 16)

            def table(dst, src):
                sp.dma_start(dst, src).then_inc(tabs_landed, 16)
            table(tabs[0:96, 0, :], I["b_mod"].rearrange("l (r f) -> (l r) f", f=P))
            table(tabs[0:48, 1, :], I["rwkv_mu"].rearrange("a j (r f) -> (a j r) f", f=P))
            for name in ("w0", "a0", "k_k", "k_a", "ln_g", "ln_b"):
                src = {"ln_g": "rwkv_ln_gain", "ln_b": "rwkv_ln_bias"}.get(name, "rwkv_" + name)
                table(tabs[T1[name]:T1[name] + KT, 1, :], I[src].rearrange("a (r f) -> (a r) f", f=P))
            table(tabs[T1["r_k"]:T1["r_k"] + KT, 1, :], I["rwkv_r_k"].rearrange("a (r h) d -> (a r) (h d)", h=2))
            table(tabs[0:48, 2, :], I["gdn_conv_w"].rearrange("a j (r f) -> (a j r) f", f=P))
            table(tabs[48:56, 2, :], I["c"].rearrange("a (r f) -> (a r) f", f=P))
            table(tabs[56:58, 2, :], I["mla_q_norm_gain"].rearrange("a (r f) -> (a r) f", f=P))
            table(tabs[58:59, 2, :], I["mla_kv_norm_gain"])
            table(tabs[59:60, 2, 0:C], I["gdn_norm_gain"])
            table(tabs[59:60, 2, C:P], I["gdn_norm_gain"])
            table(pos_i[0:TT, :], I["positions"].rearrange("a (t p) -> (a t) p", p=P))
            table(small8[:, 0:1], I["gdn_dt_bias"].rearrange("a h -> h a"))
            table(small8[:, 1:2], I["gdn_a_log"].rearrange("a h -> h a"))
            sp.dma_start(xtok, I["x"][0].rearrange("(t p) d -> p t d", p=P)).then_inc(x_landed, 16)

            wm = I["w_mod"][0].rearrange("(k p) n -> p k n", p=P)
            with sp.Fori(0, 4) as i:
                for s in range(2):
                    sp.wait_ge(mw_used, i * 2 + s + 1)
                    sp.dma_start(mwring[:, s], wm[:, :, bass.ds(i * 512 + s * 256, 256)]).then_inc(mw_landed[s], 16)

            win = I["w_in0"][0].rearrange("(k p) n -> p k n", p=P)
            sp.wait_ge(mod_ready, 1)
            sp.wait_ge(x_ready, KT)
            sp.dma_start(gatew, win[:, :, GATE_COL:GATE_COL + 16]).then_inc(gw_landed, 16)
            with sp.Fori(0, GDN_PAIRS) as i:
                for j in range(4):
                    sp.wait_ge(proj_out, i * 4 + j + 1)
                    sp.dma_start(pw[:, j], win[:, :, bass.ds(i * P + j * GDN_W, P)]).then_inc(pw_landed[j], 16)

            sp.wait_ge(mix_ready, GDN_PAIRS)
            sp.dma_start(mlaw, win[:, :, DQ_COL:DQ_COL + 416]).then_inc(mla_landed, 16)
            sp.dma_start(uq, I["mla_w_uq"][0].rearrange("(k p) n -> p k n", p=P)).then_inc(mla_landed, 16)
            sp.dma_start(ukv, I["mla_w_ukv"][0]).then_inc(mla_landed, 16)
            sp.dma_start(grow[0:1, 0, :], I["mla_q_head_gain"]).then_inc(mla_landed, 16)
            sp.dma_start(grow[0:1, 1, :], I["mla_k_head_gain"]).then_inc(mla_landed, 16)

            def stream(name, wv, rows):
                b = BLK[name]
                n = wv.shape[2] // 256 * rows
                per = 2 * rows
                with sp.Fori(0, n // per) as i:
                    for s in range(per):
                        sp.wait_ge(w_used, i * per + b + s + 1)
                        r, col = s % rows, s // rows
                        sp.dma_start(wring[:, s % 2],
                                     wv[:, r * KT:(r + 1) * KT, bass.ds(i * 512 + col * 256, 256)]
                                     ).then_inc(w_landed[s % 2], 16)

            def view(w):
                return w.rearrange("(k p) n -> p k n", p=P)

            sp.wait_ge(o_ready, 8)
            stream("o0", view(I["w_out0"][0]), 1)
            stream("up0", view(I["w_up"][0]), 1)
            stream("down0", view(I["w_down"][0]), 4)

            sp.wait_ge(tile_taken, 4 + 48)
            for name, a, n in (("rwkv_w1", 0, 64), ("rwkv_a1", 64, 64), ("rwkv_g1", 128, 160)):
                sp.dma_start(lw1[:, :, a:a + n], view(I[name][0])).then_inc(lw1_landed, 16)
            wp = [view(I[n][0]) for n in ("rwkv_w_r", "rwkv_w_k", "rwkv_w_v")]
            with sp.Fori(0, RWKV_PAIRS) as i:
                for j in range(3):
                    sp.wait_ge(proj_out, i * 3 + 18 + j)
                    sp.dma_start(pw[:, j], wp[j][:, :, bass.ds(i * P, P)]).then_inc(pw_landed[j], 16)
                sp.wait_ge(low_out, i * 3 + 3)
                for dst, src in ((lw[0:64, 0, :], I["rwkv_w2"][0]), (lw[0:64, 1, :], I["rwkv_a2"][0]),
                                 (lw[:, 2, :], I["rwkv_g2"][0, 0:P]), (lw[0:32, 3, :], I["rwkv_g2"][0, P:160])):
                    sp.dma_start(dst, src[:, bass.ds(i * P, P)]).then_inc(lw_landed, 16)
            sp.wait_ge(mix_ready, GDN_PAIRS + RWKV_PAIRS)
            stream("o1", view(I["rwkv_w_o"][0]), 1)
            stream("up1", view(I["w_up"][1]), 1)
            stream("down1", view(I["w_down"][1]), 4)
            for t in range(TT):
                sp.wait_ge(xo_ready, 2 * t + 2)
                sp.dma_start(out[0, t * P:(t + 1) * P, :], xout[:, t % 2]).then_inc(out_landed[t % 2], 16)
            for b in range(2):
                sp.wait_ge(out_landed[b], 16 * TT // 2)

        @block.tensor
        def _(pe):
            def mm(o, l, r, first=True, last=True):
                return pe.matmul(o, l, r, start=first, stop=last)

            pe.wait_ge(cst_landed, 16)
            pe.wait_ge(tabs_landed, 16 * 18)
            for j, r in ((0, 96), (1, T1_ROWS), (2, T2_ROWS)):
                pe.transpose(PS[:, j, 0:r], tabs[0:r, j, :], ident[0:r, 0:r])
            pe.wait_ge(rows_t, 1)
            pe.transpose(PS[:, 3, 0:TT], pos_f[0:TT, :], ident[0:TT, 0:TT]).then_inc(tabs_T, 1)
            pe.wait_ge(x_landed, 16)
            for k in range(KT):
                if k >= 2:
                    pe.wait_ge(x_ready, k - 1)
                for t in range(TT):
                    m = pe.transpose(PS[:, 4 + k % 2, t * P:(t + 1) * P], xtok[:, t, k * P:(k + 1) * P], ident)
                m.then_inc(x_T, 1)

            def mod_sums(acc, n, phase):
                pe.wait_ge(macc_ready, phase + 1)
                for j in range(n):
                    m = mm(PS[:, 7, j:j + 1], acc[:, j * P:(j + 1) * P], ones1[:])
                m.then_inc(mod_summed, 1)

            def norm_sums(idx):
                for k in range(KT):
                    pe.wait_ge(sq_ready, idx * KT + k + 1)
                    m = mm(PS[:, 6, :], ones, sq[:, k % 2], k == 0, k == KT - 1)
                    m.then_inc(sq_used, 1)

            mod_sums(macc, 16, 0)
            norm_sums(0)

            pe.wait_ge(gw_landed, 16)
            for j in range(2):
                for k in range(KT):
                    pe.wait_ge(h_ready, k + 1)
                    m = mm(PS[0:8, j, :], gatew[:, k, j * 8:j * 8 + 8], hT[:, k], k == 0, k == KT - 1)
                m.then_inc(rows_out, 1)
            pe.wait_ge(rows_done, 1)
            for p in range(GDN_PAIRS):
                for j, src in enumerate((cb[0:8, 0, 0:S], cb[0:8, 2, 0:S])):
                    m = mm(PS[:, 2 * p + j, :], cc("headsel")[0:8, p * P:(p + 1) * P], src)
            m.then_inc(rows_bc, 1)
            pe.wait_ge(gates_ready, 1)

            def projection(pair, j, src, landed, taken):
                for k in range(KT):
                    if k == 0:
                        pe.wait_ge(pw_landed[j], landed)
                        if taken is not None:
                            pe.wait_ge(proj_act, taken)
                    m = mm(PS[:, 6 + j % 2, :], pw[:, j, k], src[:, k], k == 0, k == KT - 1)
                    if k == KT - 1:
                        m.then_inc(proj_out, 1)
                    yield

            def project(pair, base, srcs, first=False):
                done = (base + pair) * 5
                for j, src in enumerate(srcs):
                    if j >= 2:
                        taken = done + j - 1
                    elif first:
                        taken = None
                    elif j == 0 or len(srcs) == 3:
                        taken = done - 2
                    else:
                        taken = done
                    yield from projection(pair, j, src, (pair + base) * 16 + 16, taken)

            def drop(_count):
                return None

            def filler(products):
                def fill(count):
                    for _ in range(count):
                        next(products, None)
                return fill

            def recurrence(n, rw, fill):
                fill(FILL[rw][0])
                pe.wait_ge(r1_ready, n)
                pe.wait_ge(fb_act, 2 * n)
                for c in range(NCH):
                    m = mm(blocks2(0)[:, c], FB[0][:, c], R1[:, c].rearrange("p a t -> p (a t)"))
                if rw:
                    for c in range(NCH):
                        m = mm(blocks2(2)[:, c], FB[1][:, c], R1[:, c].rearrange("p a t -> p (a t)"))
                m.then_inc(a_out, 1)
                src = FB[0] if rw else FB[1]
                for c in range(NCH):
                    m = pe.transpose(blocks2(4)[:, c], src[:, c], ident)
                m.then_inc(tok_out, 1)
                fill(FILL[rw][1])
                pe.wait_ge(fb_pool, 2 * n)
                pe.wait_ge(tok_taken, 3 * n - 2)
                for c in range(NCH):
                    m = pe.transpose(blocks2(4)[:, c], FB[2][:, c], ident)
                m.then_inc(tok_out, 1)
                fill(FILL[rw][1])
                if rw:
                    pe.wait_ge(tok_taken, 3 * n - 1)
                    for c in range(NCH):
                        m = pe.transpose(blocks2(4)[:, c], FB[1][:, c], ident)
                    m.then_inc(tok_out, 1)
                    fill(FILL[rw][1])
                pe.wait_ge(tok_taken, 3 * n)
                for c in range(NCH):
                    m = mm(bank(4)[:, c], FB[3][:, c], istack)
                m.then_inc(vs_out, 1)

                pe.wait_ge(lt_bd, n)
                for c in range(NCH):
                    m = mm(bank(0)[:, c], LTbd[:, c], istack)
                m.then_inc(at_out, 1)
                fill(FILL[rw][2])
                for lv in range(2, LEVELS + 1):
                    q = 5 * (n - 1) + lv - 1
                    pe.wait_ge(xs_ready, q)
                    for c in range(NCH):
                        m = mm(bank(1)[:, c], LTbd[:, c], Xs[:, c])
                    m.then_inc(p_out, 1)
                    fill(FILL[rw][3])
                    pe.wait_ge(ps_ready, q)
                    if lv < LEVELS:
                        pe.wait_ge(xtbd_ready, 6 * (n - 1) + lv - 1)
                        for c in range(NCH):
                            m = mm(bank(2)[:, c], XTbd[:, c], Pst[:, c])
                        m.then_inc(x_out, 1)
                    elif rw:
                        pe.wait_ge(vs_ready, n - GDN_PAIRS)
                        for c in range(NCH):
                            m = mm(bank(4)[:, c], AKbd[:, c], Vs[:, c])
                        for c in range(NCH):
                            m = mm(bank(5)[:, c], ktok[:, c], Vs[:, c])
                        m.then_inc(akv_out, 1)
                    pe.wait_ge(pbd_ready, q)
                    for c in range(NCH):
                        m = mm(bank(3)[:, c], Pbd[:, c], XTs[:, c])
                    m.then_inc(q_out, 1)
                fill(FILL[rw][4])
                pe.wait_ge(xt_ready, 6 * n)
                for c in range(NCH):
                    m = mm(bank(1)[:, c], atok[:, c], XTs[:, c])
                m.then_inc(wt_out, 1)
                pe.wait_ge(xtbd_ready, 6 * n)
                pe.wait_ge(akv_ready, n)
                for c in range(NCH):
                    m = mm(bank(0)[:, c], XTbd[:, c], AKV[:, c])
                m.then_inc(u0_out, 1)
                fill(1)
                pe.wait_ge(u0_ready, n)
                for c in range(NCH - 1):
                    if c:
                        pe.wait_ge(us_ready, 7 * (n - 1) + c)
                    mm(PS[:, c % 2, 0:C], btok[:, c], U[:, c]).then_inc(dh_out, 1)
                    fill(FILL[rw][5])
                    pe.wait_ge(hs_ready, 7 * (n - 1) + c + 1)
                    mm(PS[:, 2 + c % 2, 0:C], WTbd[:, c + 1], Hs[:, c + 1]).then_inc(w_out, 1)
                    fill(FILL[rw][5])
                fill(8 * KT)
                pe.wait_ge(hu_bd, n)
                rt = chunks(RT) if not rw else R1[:, :, 1]
                for c in range(NCH):
                    mm(bank(4)[:, c], Hbd[:, c], rt[:, c], True, False)
                    m = mm(bank(4)[:, c], ubd[:, c], RB[:, c], False, not rw)
                    if rw:
                        m = mm(bank(4)[:, c], Vbd[:, c], RK[:, c], False, True)
                m.then_inc(y_out, 1)

            def gdn_pair(i, last):
                for j in range(2):
                    pe.wait_ge(head_sq, i * 3 + j + 1)
                    m = mm(PS[:, 4 + j, :], blk, sq[:, j])
                m.then_inc(head_ss, 1)
                recurrence(i + 1, False, drop if last else filler(project(i + 1, 0, [hT] * 4)))
                pe.wait_ge(head_sq, i * 3 + 3)
                mm(PS[:, 5, :], blk, sq[:, 0]).then_inc(head_ss, 1)
                if last:
                    pe.wait_ge(mix_ready, i + 1)

            for _ in project(0, 0, [hT] * 4, first=True):
                pass
            with pe.Fori(0, GDN_PAIRS - 1) as i:
                gdn_pair(i, False)
            gdn_pair(GDN_PAIRS - 1, True)

            pe.wait_ge(mla_landed, 16 * 5)
            for j in range(3):
                for k in range(KT):
                    m = mm(PS[:, j, :], mlaw[:, k, j * P:(j + 1) * P], hT[:, k], k == 0, k == KT - 1)
                m.then_inc(lat_out, 1)
            for t in range(TT):
                for k in range(KT):
                    m = mm(PS[:, 3, t * ROPE:(t + 1) * ROPE], hT[:, k, t * P:(t + 1) * P], mlaw[:, k, 384:416],
                           k == 0, k == KT - 1)
            m.then_inc(lat_out, 1)
            for j in range(2):
                m = mm(PS[:, 4, j * QK:(j + 1) * QK], ones[0:1, :], grow[0:1, j, :])
            m.then_inc(gains_bc, 1)
            for j in range(3):
                pe.wait_ge(lat_sq, j + 1)
                m = mm(PS[:, 5 + j // 2, :], ones, sq[:, j % 2], j != 1, j != 0)
                m.then_inc(lat_ss, 1)
            pe.wait_ge(lat_ready, 1)
            for t in range(TT):
                if t:
                    pe.wait_ge(tok_copied, t)
                cols = slice(t * P, (t + 1) * P)
                for j in range(2):
                    for k in range(2):
                        mm(PS[:, j, 0:384], dq[:, k, cols], uq[:, k, j * 384:(j + 1) * 384], k == 0, k == 1)
                for j in range(2):
                    m = mm(PS[:, 2 + j, :], dkv[:, cols], ukv[:, j * S:(j + 1) * S])
                m.then_inc(tok_proj, 1)
            with pe.Fori(0, 4) as i:
                for a in range(2):
                    hd = i * 2 + a + 1
                    pe.wait_ge(hslice, hd)
                    for t in range(TT):
                        pe.transpose(PS[0:QK, 0, t * P:(t + 1) * P], qh[:, t], ident)
                    for t in range(TT):
                        m = pe.transpose(PS[0:QK, 1, t * P:(t + 1) * P], kh[:, t], ident)
                    m.then_inc(qkT_out, 1)
                    pe.wait_ge(qkT_ready, hd)
                    for t in range(TT):
                        mm(PS[:, 2 + t, 0:(t + 1) * P], qhT[0:QK, t * P:(t + 1) * P],
                           khT[0:QK, 0:(t + 1) * P]).then_inc(score_out, 1)
                    pe.wait_ge(prob_ready, hd)
                    for kt in range(TT):
                        for t in range(kt, TT):
                            m = pe.transpose(PS[:, 2 + kt, t * P:(t + 1) * P], prob[:, t, kt * P:(kt + 1) * P], ident)
                    m.then_inc(pT_out, 1)
                    pe.wait_ge(pT_ready, hd)
                    for kt in range(TT):
                        m = mm(PS[a * C:(a + 1) * C, 6 + a, kt * P:S], vh[:, kt], probT[:, kt, kt * P:S],
                               kt == 0, kt == TT - 1)
                    m.then_inc(o_out, 1)
                    pe.wait_ge(o_ready, hd)

            def tile(name, i, per, j, src, first=True, last=True, base=0, slot=0, mt=0):
                for k in range(KT):
                    m = mm(PS[:, j, :], wring[:, slot, k, mt * P:(mt + 1) * P], src[:, base + k],
                           first and k == 0, last and k == KT - 1)
                return m

            def stream(name, src, n, rows, ready=None):
                b, t0 = BLK[name], TIL[name]
                per = 2 * rows
                with pe.Fori(0, n // per) as i:
                    for s in range(per):
                        slot, r = s % 2, s % rows
                        pe.wait_ge(w_landed[slot], (i * (per // 2) + (b + s - slot) // 2 + 1) * 16)
                        for mt in range(2):
                            t = (s // rows) * 2 + mt
                            if r == 0:
                                pe.wait_ge(tile_taken, i * 4 + t0 + t + 1)
                            m = tile(name, i, per, t, src, r == 0, r == rows - 1, r * KT, slot, mt)
                            if mt == 1 and r < rows - 1:
                                m.then_inc(w_used, 1)
                            elif r == rows - 1:
                                m.then_inc(tile_out, 1)
                        if r == rows - 1:
                            mm(PS[0:1, 7, 0:1], ones1[:], ones1[:]).then_inc(w_used, 1)

            mod_sums(macc2, 32, 1)
            pe.wait_ge(mod_ready, 2)
            stream("o0", mix0, 4, 1)
            norm_sums(1)
            pe.wait_ge(h_ready, 2 * KT)
            stream("up0", hT, 16, 1)
            pe.wait_ge(tile_taken, 4 + 40)
            stream("down0", hid, 16, 4)
            mod_sums(macc1, 48, 2)
            norm_sums(2)

            pe.wait_ge(lw1_landed, 16 * 3)
            for j, (src, a, m_) in enumerate(((xr, 0, 64), (xk, 64, 64), (xv, 128, P), (xv, 256, 32))):
                pe.wait_ge(xmix_ready, min(j, 2) + 1)
                for k in range(KT):
                    m = mm(PS[0:m_, j, :], lw1[:, k, a:a + m_], src[:, k], k == 0, k == KT - 1)
                m.then_inc(lora_out, 1)
            pe.wait_ge(lora_ready, 4)
            pe.wait_ge(xmix_ready, 6)
            def rwkv_pair(i, last):
                pe.wait_ge(lw_landed, i * 64 + 64)
                mm(PS[:, 3, :], lw[0:64, 0], lora[0:64, 0]).then_inc(low_out, 1)
                mm(PS[:, 4, :], lw[0:64, 1], lora[0:64, 1]).then_inc(low_out, 1)
                mm(PS[:, 5, :], lw[:, 2], lora[:, 2], True, False)
                mm(PS[:, 5, :], lw[0:32, 3], lora[0:32, 3], False, True).then_inc(low_out, 1)
                pe.wait_ge(head_sq, i * 4 + 13)
                mm(PS[:, 0, :], blk, sq[:, 0]).then_inc(head_ss, 1)
                pe.wait_ge(head_sq, i * 4 + 14)
                mm(PS[:, 1, :], blk, sq[:, 1]).then_inc(head_ss, 1)
                recurrence(i + GDN_PAIRS + 1, True,
                           drop if last else filler(project(i + 1, GDN_PAIRS, [xr, xk, xv])))
                pe.wait_ge(head_sq, i * 4 + 15)
                mm(PS[:, 5, :], blk, sq[:, 0]).then_inc(head_ss, 1)
                pe.wait_ge(head_sq, i * 4 + 16)
                mm(PS[:, 4, :], blk, sq[:, 1]).then_inc(head_ss, 1)
                pe.wait_ge(head_rs, 12 + i * 2 + 2)
                if last:
                    pe.wait_ge(mix_ready, i + GDN_PAIRS + 1)

            for _ in project(0, GDN_PAIRS, [xr, xk, xv], first=True):
                pass
            with pe.Fori(0, RWKV_PAIRS - 1) as i:
                rwkv_pair(i, False)
            rwkv_pair(RWKV_PAIRS - 1, True)
            stream("o1", hT, 4, 1)
            norm_sums(3)
            pe.wait_ge(h_ready, 4 * KT)
            stream("up1", hT, 16, 1)
            pe.wait_ge(tile_taken, 4 + 88)
            stream("down1", hid, 16, 4)
            pe.wait_ge(tile_taken, 4 + 96)
            for t in range(TT):
                for hf in range(2):
                    q = 2 * t + hf
                    if q >= 2:
                        pe.wait_ge(xo_ready, q - 1)
                    for k in range(4):
                        m = pe.transpose(PS[:, q % 2, k * P:(k + 1) * P], xT[:, hf * 4 + k, t * P:(t + 1) * P], ident)
                    m.then_inc(xo_T, 1)

        @block.vector
        def _(dve):
            do = Steps(dve, vec)
            tt, ts, stt = dve.tensor_tensor, dve.tensor_scalar, dve.scalar_tensor_tensor
            dve.memset(ones1[:], 1.0).then_inc(tile_taken, 4)
            dve.wait_ge(tile_taken, 4)
            dve.memset(ones1[:], 1.0).then_inc(w_used, 2)
            dve.wait_ge(w_used, 2)
            dve.memset(ones1[:], 1.0).then_inc(mw_used, 2)
            dve.wait_ge(mw_used, 2)
            dve.memset(ones1[:], 1.0).then_inc(proj_out, 4)
            dve.wait_ge(proj_out, 4)
            dve.memset(ones1[:], 1.0).then_inc(low_out, 3)
            dve.wait_ge(low_out, 3)

            dve.wait_ge(tabs_landed, 16 * 18)
            do.tell(dve.tensor_copy(pos_f[0:TT, :], pos_i[0:TT, :]), rows_t, 1)
            dve.wait_ge(tabs_T, 1)
            do(dve.tensor_copy(bmodT[:], PS[:, 0, 0:96]))
            do(dve.tensor_copy(t1T[:], PS[:, 1, 0:T1_ROWS]))
            do(dve.tensor_copy(t2T[:], PS[:, 2, 0:T2_ROWS]))
            do(dve.tensor_copy(posT[:], PS[:, 3, 0:TT]))
            do(ts(t1T[:, T1["w0"]:T1["w0"] + 16], t1T[:, T1["w0"]:T1["w0"] + 16], 0.5, None, ALU.mult))
            do(ts(t2T[:, 0:56], t2T[:, 0:56], 0.5, None, ALU.mult))
            do.tell(dve.tensor_copy(cond_t[:, 0], t2T[:, 48:56]), tabs_ready, 1)
            dve.wait_ge(cond_tanh, 1)
            do(stt(cond[:], cond_t[:, 1], 1.0, cond_t[:, 0], ALU.add, ALU.mult))
            do.tell(dve.tensor_copy(cond_t[:, 0], cond[:]), cond_ready, 1)

            def mod_block(i):
                for s in range(2):
                    dve.wait_ge(mw_landed[s], i * 16 + 16)
                    do(ts(mblk[:, s], mwring[:, s, 0], cond[:, 0:1], None, ALU.mult))
                    for k in range(1, KT - 1):
                        do(stt(mblk[:, s], mwring[:, s, k], cond[:, k:k + 1], mblk[:, s], ALU.mult, ALU.add))
                    do.tell(stt(macc[:, bass.ds(i * 512 + s * 256, 256)], mwring[:, s, KT - 1], cond[:, KT - 1:KT],
                                mblk[:, s], ALU.mult, ALU.add), mw_used, i * 2 + s + 3)
            do.loop(4, 14, mod_block)
            do.tell(dve.tensor_copy(cond_t[:, 0], cond[:]), macc_ready, 1)

            def mod_finish(layer, phase, a, b):
                dve.wait_ge(mod_summed, phase + 1)
                do(tt(modT[:, a:b], PS[:, 7, 0:b - a], bmodT[:, layer * 48 + a:layer * 48 + b], ALU.add))
                for g in SCALE:
                    if a <= g < b:
                        do(ts(modT[:, g:g + KT], modT[:, g:g + KT], 1.0, None, ALU.add))
                do.tell(dve.tensor_copy(cond_t[:, 0], cond[:]), mod_ready, phase + 1)

            def norm(idx):
                half = idx % 2
                dve.wait_ge(rstd_ready, idx + 1)
                for k in range(KT):
                    do(stt(hT[:, k], xT[:, k], modT[:, SCALE[half] + k:SCALE[half] + k + 1], rs[:, 0],
                           ALU.mult, ALU.mult))
                    do.tell(ts(hT[:, k], hT[:, k], modT[:, SHIFT[half] + k:SHIFT[half] + k + 1], None, ALU.add),
                            h_ready, idx * KT + k + 1)

            mod_finish(0, 0, 0, 16)
            norm(0)

            rA, rE, rB = cb[0:8, 0, 0:S], cb[0:8, 1, 0:S], cb[0:8, 2, 0:S]
            rC = tmp[0:8]
            dve.wait_ge(rows_out, 2)
            do(ts(rA, PS[0:8, 0, :], small8[:, 0:1], None, ALU.add))
            do.tell(stt(rE, rA, -1.0, rA, ALU.mult, ALU.min), rows_e, 1)
            dve.wait_ge(rows_l, 2)
            do(ts(rA, rA, 0.0, None, ALU.max))
            do(tt(rA, rA, rE, ALU.add))
            do(ts(rC, rA, small8[:, 2:3], -1.0, ALU.mult, ALU.mult))
            do(dve.tensor_tensor_scan(rA, reset[0:8, :], rC, 0.0, ALU.mult, ALU.add))
            do.tell(ts(rB, rB, 0.5, 0.5, ALU.mult, ALU.add), rows_done, 1)
            dve.wait_ge(gates_ready, 1)
            dve.memset(Hs[:, 0], 0.0).then_inc(vec, 1)
            do.n += 1
            do.tell(dve.memset(cb[:], 0.0), cb_zeroed, 1)

            def recurrence(n, rw):
                q0 = n - GDN_PAIRS if rw else n
                dve.wait_ge(a_out, n)
                two = lambda mask: over_chunks(mask)
                if rw:
                    do(tt(LTs, blocks2(0)[:, :, 0:C], two(strictT), ALU.mult))
                    do.tell(tt(RB, blocks2(0)[:, :, C:P], two(inclT), ALU.mult), lts_ready, n)
                    do.tell(tt(AKs, blocks2(2)[:, :, 0:C], two(strictT), ALU.mult), aks_ready, q0)
                    do(tt(RK, blocks2(2)[:, :, C:P], two(inclT), ALU.mult))
                else:
                    do(tt(LTs, blocks2(0)[:, :, 0:C], chunks(S1), ALU.mult))
                    do.tell(tt(RB, blocks2(0)[:, :, C:P], chunks(S2), ALU.mult), lts_ready, n)
                do(tt(XTs, LTs, over_chunks(level1T), ALU.mult))
                do.tell(tt(XTs, XTs, over_chunks(istack), ALU.add), xt_ready, 6 * (n - 1) + 1)
                dve.wait_ge(at_out, n)
                do(tt(Xs, bank(0), over_chunks(level(1)), ALU.mult))
                do.tell(tt(Xs, Xs, over_chunks(istack), ALU.add), xs_ready, 5 * (n - 1) + 1)
                dve.wait_ge(xtbd_ready, 6 * (n - 1) + 1)
                if not rw:
                    dve.wait_ge(vs_out, n)
                    do.tell(tt(AKV, bank(4), bcol.unsqueeze(2).broadcast_to([P, NCH, C]), ALU.mult), akv_ready, n)
                for lv in range(2, LEVELS + 1):
                    q = 5 * (n - 1) + lv - 1
                    dve.wait_ge(p_out, q)
                    do.tell(tt(Pst, bank(1), over_chunks(level(lv)), ALU.mult), ps_ready, q)
                    if lv < LEVELS:
                        dve.wait_ge(x_out, 4 * (n - 1) + lv - 1)
                        do.tell(tt(Xs, Xs, bank(2), ALU.add), xs_ready, q + 1)
                    elif rw:
                        dve.wait_ge(akv_out, q0)
                        do.tell(dve.tensor_copy(AKV, bank(4)), akv_ready, n)
                        do(tt(KVe, bank(5), egC.unsqueeze(2).broadcast_to([P, NCH, C]), ALU.mult))
                    dve.wait_ge(q_out, q)
                    do.tell(tt(XTs, XTs, bank(3), ALU.add), xt_ready, 6 * (n - 1) + lv)
                for c in range(NCH - 1):
                    e = egC[:, c:c + 1]
                    if rw:
                        do(stt(te[:, 0], Hs[:, c], e, KVe[:, c], ALU.mult, ALU.add))
                    dve.wait_ge(dh_out, 7 * (n - 1) + c + 1)
                    if rw:
                        h = stt(Hs[:, c + 1], PS[:, c % 2, 0:C], e, te[:, 0], ALU.mult, ALU.add)
                    else:
                        h = stt(Hs[:, c + 1], Hs[:, c], e, PS[:, c % 2, 0:C], ALU.mult, ALU.add)
                    do.tell(h, hs_ready, 7 * (n - 1) + c + 1)
                    dve.wait_ge(w_out, 7 * (n - 1) + c + 1)
                    do.tell(tt(U[:, c + 1], U[:, c + 1], PS[:, 2 + c % 2, 0:C], ALU.add), us_ready,
                            7 * (n - 1) + c + 1)

            def silu(x, t):
                return stt(x, t, 1.0, x, ALU.add, ALU.mult)

            def gdn_pair(i):
                n = i + 1
                for j, x in enumerate((qf, kf, vf)):
                    dve.wait_ge(proj_act, i * 5 + j + 1)
                    w = [pc[:, tap * 3 + j:tap * 3 + j + 1] for tap in range(4)]
                    if j == 0:
                        for tap in range(4):
                            do(dve.tensor_copy(pc[:, tap * 3:tap * 3 + 3], t2T[:, bass.ds(i + tap * 12, 3, step=4)]))
                    do(ts(x, cb[:, j, 0:S], w[0], None, ALU.mult))
                    for tap in range(1, 3):
                        do(stt(x, cb[:, j, tap:tap + S], w[tap], x, ALU.mult, ALU.add))
                    do.tell(stt(x, cb[:, j, 3:3 + S], w[3], x, ALU.mult, ALU.add), proj_vec, i * 3 + j + 1)
                dve.wait_ge(proj_act, i * 5 + 5)
                do(silu(zf, th))
                for j, (x, t) in enumerate(((qf, S1), (kf, S2), (vf, S3))):
                    dve.wait_ge(d_in, i * 3 + j + 1)
                    do.tell(silu(x, t), lat_taken, i * 3 + j + 1)
                do(dve.tensor_copy(Gp, Grow[:, i]))
                do(dve.tensor_copy(Bp, Brow[:, i]))
                do(tt(chunks(tmp), chunks(Gp), over_chunks(istack), ALU.mult))
                do(dve.tensor_reduce(gcol, chunks(tmp), AX.X, ALU.add))
                do(tt(chunks(tmp), chunks(Bp), over_chunks(istack), ALU.mult))
                do(dve.tensor_reduce(bcol, chunks(tmp), AX.X, ALU.add))
                do(dve.tensor_copy(glast, chunks(Gp)[:, :, C - 1]))
                do(tt(chunks(S1), chunks(Gp), gcol.unsqueeze(2).broadcast_to([P, NCH, C]), ALU.subtract))
                do(ts(S1, S1, 0.0, None, ALU.min))
                do.tell(tt(chunks(S2), glast.unsqueeze(2).broadcast_to([P, NCH, C]), chunks(Gp), ALU.subtract),
                        d_exp, n)
                dve.wait_ge(head_rs, i * 3 + 2)
                do(stt(qf, qf, float(C) ** -0.5, rs[:, 0], ALU.mult, ALU.mult))
                do.tell(tt(kf, kf, rs[:, 1], ALU.mult), fm_ready, i * 3 + 1)
                dve.wait_ge(gates_ready, n + 1)
                do.tell(tt(tmp, kf, S2, ALU.mult), fm_ready, i * 3 + 2)
                do(dve.tensor_copy(R1[:, :, 1], chunks(qf)))
                do(tt(RT, qf, Gp, ALU.mult))
                do(stt(R1[:, :, 0], chunks(kf), -1.0, chunks(Bp), ALU.mult, ALU.mult))
                do.tell(tt(chunks(S3), R1[:, :, 0], chunks(Gp), ALU.mult), fm_ready, i * 3 + 3)
                do(tt(chunks(S2), chunks(S1), over_chunks(inclT), ALU.mult))
                do.tell(tt(chunks(S1), chunks(S1), over_chunks(strictT), ALU.mult), r1_ready, n)
                recurrence(n, False)
                dve.wait_ge(head_rs, i * 3 + 3)
                do(tt(tmp, PS[:, 4, :], rs[:, 0], ALU.mult))
                do.tell(stt(mix0[:, i], tmp, t2T[:, 59:60], zf, ALU.mult, ALU.mult), mix_ready, n)
            do.loop(GDN_PAIRS, GDN_STEPS, gdn_pair)

            TWO_PI = 6.283185307179586
            C1 = 6.28125
            C2 = 0.0019350051879882812
            C3 = TWO_PI - C1 - C2
            inv = cc("invfreq")
            for t in range(TT):
                do(ts(ang[:, t, 1], inv, posT[:, t:t + 1], None, ALU.mult))
                do(dve.tensor_copy(ang[:, t, 0], ang[:, t, 1]))
            MAGIC = 12582912.0
            do(ts(rot[:, :, 1], ang[:, :, 1], 1.0 / TWO_PI, MAGIC, ALU.mult, ALU.add))
            do(ts(rot[:, :, 0], ang[:, :, 0], 1.0 / TWO_PI, 0.25, ALU.mult, ALU.add))
            do(ts(rot[:, :, 0], rot[:, :, 0], MAGIC, None, ALU.add))
            do(ts(rot, rot, -MAGIC, None, ALU.add))
            for const in (C1, C2, C3):
                do(stt(ang, rot, -const, ang, ALU.mult, ALU.add))
            do(ts(ang[:, :, 0], ang[:, :, 0], TWO_PI / 4, None, ALU.add))
            do(ts(ang, ang, 3.1415925, None, ALU.min))
            do.tell(ts(ang, ang, -3.1415925, None, ALU.max), ang_ready, 1)

            for j, x in enumerate((dq[:, 0], dq[:, 1], dkv)):
                dve.wait_ge(lat_out, j + 1)
                do.tell(dve.tensor_copy(x, PS[:, j, :]), lat_taken, 12 + j + 1)
            dve.wait_ge(lat_out, 4)
            do(dve.tensor_copy(krope, PS[:, 3, 0:TT * ROPE].rearrange("p (t r) -> p t r", t=TT)))
            dve.wait_ge(gains_bc, 1)
            do(dve.tensor_copy(gains, PS[:, 4, 0:2 * QK].rearrange("p (a r) -> p a r", a=2)))
            dve.wait_ge(lat_rs, 2)
            for x, g, r in ((dq[:, 0], 56, 0), (dq[:, 1], 57, 0), (dkv, 58, 1)):
                do(stt(x, x, t2T[:, g:g + 1], rs[:, r], ALU.mult, ALU.mult))
            do.tell(dve.tensor_copy(cond_t[:, 0], cond[:]), lat_ready, 1)
            dve.wait_ge(trig_ready, 1)
            cosv = lambda t: trig[:, t, 0].unsqueeze(1).broadcast_to([P, 8, HALF])
            sinv = lambda t: trig[:, t, 1].unsqueeze(1).broadcast_to([P, 8, HALF])
            for t in range(TT):
                dve.wait_ge(tok_copied, t + 1)
                do(dve.tensor_copy(kall[:, t, :, NOPE:QK], krope[:, t].unsqueeze(1).broadcast_to([P, 8, ROPE])))
                for a, x in ((0, qall[:, t]), (1, kall[:, t])):
                    do(tt(sqh, x, x, ALU.mult))
                    do(dve.tensor_reduce(ssh[:, a], sqh, AX.X, ALU.add))
                do.tell(dve.tensor_copy(cond_t[:, 0], cond[:]), ssh_ready, t + 1)
                dve.wait_ge(rsh_ready, t + 1)
                for a, x in ((0, qall[:, t]), (1, kall[:, t])):
                    do(tt(x, x, ssh[:, a].unsqueeze(2).broadcast_to([P, 8, QK]), ALU.mult))
                    do(tt(x, x, gains[:, a].unsqueeze(1).broadcast_to([P, 8, QK]), ALU.mult))
                    x1, x2 = x[:, :, NOPE:NOPE + HALF], x[:, :, NOPE + HALF:QK]
                    do(tt(ropet[:, 0], x1, cosv(t), ALU.mult))
                    do(tt(ropet[:, 1], x2, sinv(t), ALU.mult))
                    do(tt(ropet[:, 2], x2, cosv(t), ALU.mult))
                    do(tt(ropet[:, 3], x1, sinv(t), ALU.mult))
                    do(tt(x1, ropet[:, 0], ropet[:, 1], ALU.subtract))
                    do(tt(x2, ropet[:, 2], ropet[:, 3], ALU.add))
            do.tell(dve.tensor_copy(cond_t[:, 0], cond[:]), heads_ready, 1)

            def attend(i):
                for a in range(2):
                    hd = i * 2 + a + 1
                    for t in range(TT):
                        dve.wait_ge(score_out, i * 8 + a * 4 + t + 1)
                        sc = PS[:, 2 + t, 0:(t + 1) * P]
                        do(tt(PS[:, 2 + t, t * P:(t + 1) * P], PS[:, 2 + t, t * P:(t + 1) * P], causal, ALU.add))
                        do(dve.tensor_reduce(negm[:, t:t + 1], sc, AX.X, ALU.max))
                        do.tell(ts(negm[:, t:t + 1], negm[:, t:t + 1], -float(QK) ** -0.5, None, ALU.mult),
                                max_ready, i * 8 + a * 4 + t + 1)
                    for t in range(TT):
                        dve.wait_ge(exp_ready, i * 8 + a * 4 + t + 1)
                        do(dve.reciprocal(rden[:, t:t + 1], den[:, t:t + 1]))
                        ins = ts(prob[:, t, 0:(t + 1) * P], prob[:, t, 0:(t + 1) * P], rden[:, t:t + 1], None, ALU.mult)
                        if t == TT - 1:
                            do.tell(ins, prob_ready, hd)
                        else:
                            do(ins)
                    dve.wait_ge(o_out, hd)
                    do.tell(dve.tensor_copy(mix0[a * C:(a + 1) * C, i + 4], PS[a * C:(a + 1) * C, 6 + a, :]),
                            o_ready, hd)
            do.loop(4, 30, attend)

            def residual(name, n, gate):
                def body(i):
                    for j in range(4):
                        dve.wait_ge(tile_out, i * 4 + TIL[name] + j + 1)
                        x = xT[:, i * 4 + j]
                        do.tell(stt(x, PS[:, j, :], gate_cols[:, bass.ds(i * 4 + j, 1)], x, ALU.mult, ALU.add),
                                tile_taken, i * 4 + TIL[name] + j + 5)
                do(dve.tensor_copy(gate_cols[:], modT[:, gate:gate + KT]))
                do.loop(n // 4, 0, body)

            def relu2(name):
                def body(i):
                    for j in range(4):
                        dve.wait_ge(tile_out, i * 4 + TIL[name] + j + 1)
                        do(ts(tmp_r[:, j % 2], PS[:, j, :], 0.0, None, ALU.max))
                        do.tell(tt(hid[:, i * 4 + j], tmp_r[:, j % 2], PS[:, j, :], ALU.mult),
                                tile_taken, i * 4 + TIL[name] + j + 5)
                do.loop(FT // 4, 4, body)

            mod_finish(0, 1, 16, 48)
            residual("o0", KT, GATE[0])
            norm(1)
            relu2("up0")
            residual("down0", KT, GATE[1])
            mod_finish(1, 2, 0, 48)
            norm(2)

            dve.wait_ge(h_ready, 3 * KT)
            do(tt(xx[:, :, 1:S], hT[:, :, 0:S - 1], hT[:, :, 1:S], ALU.subtract))
            do(ts(xx[:, :, 0:1], hT[:, :, 0:1], -1.0, None, ALU.mult))
            for q, (j, x) in enumerate(((1, xr), (4, xk), (5, xv), (0, xr), (2, xk), (3, xv))):
                if q >= 3:
                    dve.wait_ge(lora_out, (1, 2, 4)[q - 3])
                for k in range(KT):
                    col = t1T[:, j * KT + k:j * KT + k + 1]
                    ins = stt(x[:, k], xx[:, k], col, hT[:, k], ALU.mult, ALU.add)
                    if k < KT - 1:
                        do(ins)
                do.tell(ins, xmix_ready, q + 1)
            dve.wait_ge(lora_ready, 2)
            for j, r in ((2, P), (3, 32)):
                dve.wait_ge(proj_vec, 12 + j - 1)
                do.tell(ts(lora[0:r, j], lora[0:r, j], 0.5, 0.5, ALU.mult, ALU.add), lora_ready, j + 1)
            dve.wait_ge(zeroed, 2)
            do(dve.memset(Hs[:, 0], 0.0))

            def rwkv_pair(i):
                n = i + GDN_PAIRS + 1
                for a, b in ((0, 0), (1, 1), (2, 2), (3, 3), (4, 4), (5, 5), (6, 6)):
                    src = t1T[:, bass.ds(i + 48 + a * KT, 1)]
                    ins = dve.tensor_copy(pc[:, b:b + 1], src)
                    if a < 6:
                        do(ins)
                do.tell(ins, d_exp, n)
                w0c, a0c, kkc, kac, rkc, lgc, lbc = (pc[:, b:b + 1] for b in range(7))
                dve.wait_ge(proj_act, 20 + i * 5 + 2)
                do(ts(tmp, kf, kkc, None, ALU.mult))
                do.tell(tt(sq[:, 0], tmp, tmp, ALU.mult), head_sq, i * 4 + 13)
                dve.wait_ge(proj_act, 20 + i * 5 + 5)
                do(ts(S1, S1, -0.5 * DECAY, -0.5 * DECAY, ALU.mult, ALU.add))
                do(dve.tensor_tensor_scan(S3, reset, S1, 0.0, ALU.mult, ALU.add))
                do.tell(tt(S1, S3, S1, ALU.subtract), d_in, 12 + i + 1)
                do(ts(S2, S2, 0.5, 0.5, ALU.mult, ALU.add))
                do(ts(th, S2, -1.0, kac, ALU.add, ALU.mult))
                do(stt(kf, th, 1.0, kf, ALU.add, ALU.mult))
                do.tell(stt(sq[:, 1], qf, rkc, kf, ALU.mult, ALU.mult), head_sq, i * 4 + 14)
                dve.wait_ge(head_rs, 12 + i * 2 + 1)
                do(tt(tmp, tmp, rs[:, 0], ALU.mult))
                dve.wait_ge(gates_ready, GDN_PAIRS + 1 + i + 1)
                do(tt(R1[:, :, 1], chunks(qf), chunks(S3), ALU.mult))
                do(tt(th, tmp, S2, ALU.mult))
                do.tell(tt(S2, th, RT, ALU.mult), fm_ready, 12 + i * 3 + 1)
                do.tell(tt(S3, kf, RT, ALU.mult), fm_ready, 12 + i * 3 + 2)
                do.tell(stt(R1[:, :, 0], chunks(tmp), -1.0, chunks(S1), ALU.mult, ALU.mult),
                        fm_ready, 12 + i * 3 + 3)
                dve.wait_ge(head_ss, 8 + i * 4 + 2)
                do(tt(post, PS[:, 1, :], vf, ALU.mult))
                do.tell(ts(te[:, 1, 0:1], w0c, 1.0, None, ALU.mult), r1_ready, n)
                recurrence(n, True)
                dve.wait_ge(y_out, n)
                do.tell(dve.tensor_copy(sq[:, 0], PS[:, 4, :]), head_sq, i * 4 + 15)
                dve.wait_ge(head_ss, 8 + i * 4 + 3)
                do(stt(tmp, PS[:, 5, :], -1.0 / C, sq[:, 0], ALU.mult, ALU.add))
                do.tell(tt(sq[:, 1], tmp, tmp, ALU.mult), head_sq, i * 4 + 16)
                dve.wait_ge(head_rs, 12 + i * 2 + 2)
                do(tt(tmp, tmp, rs[:, 1], ALU.mult))
                do(ts(tmp, tmp, lgc, lbc, ALU.mult, ALU.add))
                do(tt(tmp, tmp, post, ALU.add))
                do.tell(tt(hT[:, i], tmp, zf, ALU.mult), mix_ready, n)
            do.loop(RWKV_PAIRS, RWKV_STEPS, rwkv_pair)

            residual("o1", KT, GATE[0])
            norm(3)
            relu2("up1")
            residual("down1", KT, GATE[1])

        @block.scalar
        def _(act):
            do = Steps(act, act_)
            fn = act.activation
            act.wait_ge(tabs_ready, 1)
            do.tell(fn(cond_t[:, 1], cond_t[:, 0], ACT.Tanh), cond_tanh, 1)
            for k in range(KT):
                act.wait_ge(x_T, k + 1)
                do.tell(fn(xT[:, k], PS[:, 4 + k % 2, :], ACT.Copy), x_ready, k + 1)

            def rsqrt(o, ps, scale, eps, sem_, value):
                do(fn(o, ps, ACT.Ln, scale=scale, bias=eps))
                do.tell(fn(o, o, ACT.Exp, scale=-0.5), sem_, value)

            def norm(idx):
                for k in range(KT):
                    if idx:
                        act.wait_ge(tile_taken, X_DONE[idx] - KT + k + 1)
                    if k >= 2:
                        act.wait_ge(sq_used, idx * KT + k - 1)
                    do.tell(fn(sq[:, k % 2], xT[:, k], ACT.Square), sq_ready, idx * KT + k + 1)
                act.wait_ge(sq_used, idx * KT + KT)
                rsqrt(rs[:, 0], PS[:, 6, :], 1.0 / D, eps6, rstd_ready, idx + 1)

            norm(0)
            act.wait_ge(rows_e, 1)
            rE, rB = cb[0:8, 1, 0:S], cb[0:8, 2, 0:S]
            do(fn(rE, rE, ACT.Exp))
            do(fn(small8[:, 2:3], small8[:, 1:2], ACT.Exp))
            do.tell(fn(rE, rE, ACT.Ln, bias=one[0:8]), rows_l, 1)
            do.tell(fn(rB, PS[0:8, 1, :], ACT.Tanh, scale=0.5), rows_l, 2)
            act.wait_ge(rows_bc, 1)
            for p in range(GDN_PAIRS):
                do(fn(Grow[:, p], PS[:, 2 * p, :], ACT.Copy))
                ins = fn(Brow[:, p], PS[:, 2 * p + 1, :], ACT.Copy)
                if p < GDN_PAIRS - 1:
                    do(ins)
            do.tell(ins, gates_ready, 1)

            def halves(dst, src, sem_=None, value=None):
                do(fn(dst[0:C, :, 0:C], src[0:C], ACT.Copy))
                ins = fn(dst[C:P, :, C:P], src[C:P], ACT.Copy)
                if sem_ is None:
                    do(ins)
                else:
                    do.tell(ins, sem_, value)

            def recurrence(n, rw, evacuate):
                q0 = n - GDN_PAIRS if rw else n
                first = 8 + q0 * 3 - 2 if rw else q0 * 2 - 1
                act.wait_ge(tok_out, first)
                do.tell(fn(btok, blocks2(4), ACT.Copy), tok_taken, 3 * n - 2)
                act.wait_ge(tok_out, first + 1)
                if rw:
                    do.tell(fn(atok, blocks2(4), ACT.Copy), tok_taken, 3 * n - 1)
                    act.wait_ge(tok_out, first + 2)
                    do.tell(fn(ktok, blocks2(4), ACT.Copy), tok_taken, 3 * n)
                    act.wait_ge(lts_ready, n)
                    halves(LTbd, LTs, lt_bd, n)
                    act.wait_ge(vs_out, n)
                    do.tell(fn(Vs, bank(4), ACT.Copy), vs_ready, q0)
                else:
                    do.tell(fn(atok[:, 0:4], blocks2(4)[:, 0:4], ACT.Copy), tok_taken, 3 * n - 1)
                    do.tell(fn(atok[:, 4:8], blocks2(4)[:, 4:8], ACT.Copy), tok_taken, 3 * n)
                    act.wait_ge(lts_ready, n)
                    halves(LTbd, LTs, lt_bd, n)
                if rw:
                    act.wait_ge(aks_ready, q0)
                    halves(AKbd, AKs)
                for lv in range(1, LEVELS + 1):
                    if lv > 1:
                        act.wait_ge(ps_ready, 5 * (n - 1) + lv - 1)
                        if lv == 2:
                            act.wait_ge(vs_out, n)
                        halves(Pbd, Pst, pbd_ready, 5 * (n - 1) + lv - 1)
                    act.wait_ge(xt_ready, 6 * (n - 1) + lv)
                    halves(XTbd, XTs, xtbd_ready, 6 * (n - 1) + lv)
                    if lv in EVAC[rw]:
                        evacuate(EVAC[rw].index(lv))
                if rw:
                    halves(Vbd, Vs)
                act.wait_ge(wt_out, n)
                halves(WTbd, bank(1))
                act.wait_ge(u0_out, n)
                do.tell(fn(U, bank(0), ACT.Copy), u0_ready, n)
                evacuate(2)
                act.wait_ge(us_ready, 7 * n)
                act.wait_ge(hs_ready, 7 * n)
                halves(Hbd, Hs[:, 0:NCH])
                halves(ubd, U, hu_bd, n)

            def gdn_taken(pair):
                def evacuate(j):
                    act.wait_ge(proj_out, pair * 4 + j + 5)
                    do.tell(fn(cb[:, j, 3:3 + S], PS[:, 6 + j % 2, :], ACT.Copy), proj_act, pair * 5 + j + 1)
                return evacuate

            def gdn_pair(i, last=False):
                n = i + 1
                act.wait_ge(proj_out, i * 4 + 8)
                do.tell(fn(zf, PS[:, 7, :], ACT.Copy, scale=0.5), proj_act, i * 5 + 4)
                do.tell(fn(th, PS[:, 7, :], ACT.Tanh, scale=0.5), proj_act, i * 5 + 5)
                for j, (x, t) in enumerate(((qf, S1), (kf, S2), (vf, S3))):
                    act.wait_ge(proj_vec, i * 3 + j + 1)
                    do.tell(fn(t, x, ACT.Tanh), d_in, i * 3 + j + 1)
                for j, x in enumerate((qf, kf)):
                    act.wait_ge(lat_taken, i * 3 + j + 1)
                    do.tell(fn(sq[:, j], x, ACT.Square), head_sq, i * 3 + j + 1)
                act.wait_ge(head_ss, i * 2 + 1)
                for j in range(2):
                    do(fn(rs[:, j], PS[:, 4 + j, :], ACT.Ln, bias=eps12))
                for j in range(2):
                    do.tell(fn(rs[:, j], rs[:, j], ACT.Exp, scale=-0.5), head_rs, i * 3 + j + 1)
                act.wait_ge(d_exp, n)
                do(fn(S1, S1, ACT.Exp))
                do(fn(S2, S2, ACT.Exp))
                do(fn(egC, glast, ACT.Exp))
                do.tell(fn(Gp, Gp, ACT.Exp), gates_ready, n + 1)
                act.wait_ge(fm_ready, i * 3 + 1)
                halves(FB[0], chunks(kf), fb_act, i * 2 + 1)
                act.wait_ge(fm_ready, i * 3 + 2)
                halves(FB[1], chunks(tmp), fb_act, i * 2 + 2)
                recurrence(n, False, (lambda j: None) if last else gdn_taken(i + 1))
                act.wait_ge(y_out, n)
                do.tell(fn(sq[:, 0], PS[:, 4, :], ACT.Square), head_sq, i * 3 + 3)
                act.wait_ge(head_ss, i * 2 + 2)
                rsqrt(rs[:, 0], PS[:, 5, :], 1.0 / C, eps6, head_rs, i * 3 + 3)
                act.wait_ge(mix_ready, n)
            act.wait_ge(zeroed, 1)
            act.wait_ge(cb_zeroed, 1)
            for j in range(3):
                gdn_taken(0)(j)
            do.loop(GDN_PAIRS - 1, GDN_ACT_STEPS, gdn_pair)
            gdn_pair(GDN_PAIRS - 1, True)

            act.wait_ge(ang_ready, 1)
            do.tell(fn(trig, ang, ACT.Sin), trig_ready, 1)
            for j, x in enumerate((dq[:, 0], dq[:, 1], dkv)):
                act.wait_ge(lat_taken, 12 + j + 1)
                if j == 2:
                    act.wait_ge(lat_ss, 1)
                do.tell(fn(sq[:, j % 2], x, ACT.Square), lat_sq, j + 1)
            act.wait_ge(lat_ss, 2)
            rsqrt(rs[:, 0], PS[:, 5, :], 1.0 / 256, eps6, lat_rs, 1)
            act.wait_ge(lat_ss, 3)
            rsqrt(rs[:, 1], PS[:, 6, :], 1.0 / 128, eps6, lat_rs, 2)
            for t in range(TT):
                act.wait_ge(tok_proj, t + 1)
                for j in range(2):
                    do(fn(qall[:, t, j * 4:j * 4 + 4], PS[:, j, 0:384].rearrange("p (h d) -> p h d", h=4), ACT.Copy))
                kv = [PS[:, 2 + j, :].rearrange("p (h d) -> p h d", h=4) for j in range(2)]
                for j in range(2):
                    do(fn(kall[:, t, j * 4:j * 4 + 4, 0:NOPE], kv[j][:, :, 0:NOPE], ACT.Copy))
                    ins = fn(vall[:, t, j * 4:j * 4 + 4], kv[j][:, :, NOPE:P], ACT.Copy)
                    if j == 0:
                        do(ins)
                do.tell(ins, tok_copied, t + 1)
                act.wait_ge(ssh_ready, t + 1)
                do(fn(ssh, ssh, ACT.Ln, scale=1.0 / QK, bias=eps6))
                do.tell(fn(ssh, ssh, ACT.Exp, scale=-0.5), rsh_ready, t + 1)

            def attend(i):
                for a in range(2):
                    hd = i * 2 + a + 1
                    act.wait_ge(qkT_out, hd)
                    do(fn(qhT[0:QK], PS[0:QK, 0, :], ACT.Copy))
                    do.tell(fn(khT[0:QK], PS[0:QK, 1, :], ACT.Copy), qkT_ready, hd)
                    for t in range(TT):
                        act.wait_ge(max_ready, i * 8 + a * 4 + t + 1)
                        do.tell(fn(prob[:, t, 0:(t + 1) * P], PS[:, 2 + t, 0:(t + 1) * P], ACT.Exp,
                                   bias=negm[:, t:t + 1], scale=float(QK) ** -0.5, accum_out=den[:, t:t + 1]),
                                exp_ready, i * 8 + a * 4 + t + 1)
                    act.wait_ge(pT_out, hd)
                    for kt in range(TT):
                        ins = fn(probT[:, kt, kt * P:S], PS[:, 2 + kt, kt * P:S], ACT.Copy)
                        if kt < TT - 1:
                            do(ins)
                    do.tell(ins, pT_ready, hd)
            do.loop(4, 8, attend)
            norm(1)
            norm(2)

            for j, (m_, f) in enumerate(((64, ACT.Tanh), (64, ACT.Copy), (P, ACT.Tanh), (32, ACT.Tanh))):
                act.wait_ge(lora_out, j + 1)
                ins = fn(lora[0:m_, j], PS[0:m_, j, :], f, scale=0.5 if j >= 2 else 1.0)
                if j < 2:
                    do.tell(ins, lora_ready, j + 1)
                else:
                    do.tell(ins, proj_vec, 12 + j - 1)
            act.wait_ge(zeroed, 2)

            def rwkv_taken(pair):
                def evacuate(j):
                    act.wait_ge(proj_out, 20 + pair * 3 + j + 1)
                    do.tell(fn((qf, kf, vf)[j], PS[:, 6 + j % 2, :], ACT.Copy), proj_act, 20 + pair * 5 + j + 1)
                return evacuate

            def rwkv_pair(i, last=False):
                n = i + GDN_PAIRS + 1
                w0c, a0c = pc[:, 0:1], pc[:, 1:2]
                act.wait_ge(d_exp, n)
                act.wait_ge(low_out, i * 3 + 4)
                do.tell(fn(S1, PS[:, 3, :], ACT.Tanh, scale=0.5, bias=w0c), proj_act, 20 + i * 5 + 4)
                act.wait_ge(low_out, i * 3 + 5)
                do.tell(fn(S2, PS[:, 4, :], ACT.Tanh, scale=0.5, bias=a0c), proj_act, 20 + i * 5 + 5)
                act.wait_ge(low_out, i * 3 + 6)
                do(fn(zf, PS[:, 5, :], ACT.Copy))
                act.wait_ge(head_ss, 8 + i * 4 + 1)
                rsqrt(rs[:, 0], PS[:, 0, :], 1.0, eps12, head_rs, 12 + i * 2 + 1)
                act.wait_ge(d_in, 12 + i + 1)
                do(fn(RT, S3, ACT.Exp, scale=-1.0))
                do(fn(egC, chunks(S3)[:, :, C - 1], ACT.Exp))
                do(fn(S3, S3, ACT.Exp))
                do.tell(fn(S1, S1, ACT.Exp), gates_ready, GDN_PAIRS + 1 + i + 1)
                act.wait_ge(fm_ready, 12 + i * 3 + 1)
                halves(FB[0], chunks(S2), fb_act, 8 + i * 2 + 1)
                act.wait_ge(fm_ready, 12 + i * 3 + 2)
                halves(FB[1], chunks(S3), fb_act, 8 + i * 2 + 2)
                recurrence(n, True, (lambda j: None) if last else rwkv_taken(i + 1))
                act.wait_ge(head_ss, 8 + i * 4 + 4)
                rsqrt(rs[:, 1], PS[:, 4, :], 1.0 / C, epsgn, head_rs, 12 + i * 2 + 2)
                act.wait_ge(mix_ready, n)
            for j in range(3):
                rwkv_taken(0)(j)
            do.loop(RWKV_PAIRS - 1, RWKV_ACT_STEPS, rwkv_pair)
            rwkv_pair(RWKV_PAIRS - 1, True)
            norm(3)
            for q in range(2 * TT):
                t, hf = divmod(q, 2)
                act.wait_ge(xo_T, q + 1)
                if t >= 2:
                    act.wait_ge(out_landed[t % 2], 16)
                do.tell(fn(xout[:, t % 2, hf * S:(hf + 1) * S], PS[:, q % 2, :], ACT.Copy), xo_ready, q + 1)

        @block.gpsimd
        def _(pool):
            do = Steps(pool, pool_)

            def copy(dst, src):
                pool.wait_ge(cst_landed, 16)
                return pool.tensor_copy(dst, src)

            def zero(count):
                for b in FB:
                    do(pool.memset(b, 0.0))
                do.tell(pool.memset(Vbd, 0.0), zeroed, count)

            def expand(dst, src, value):
                do(pool.tensor_tensor(dst[0:C, :, 0:C], src[0:C], over_chunks(ones[:, 0:C])[0:C], ALU.mult))
                do.tell(pool.tensor_tensor(dst[C:P, :, C:P], src[C:P], over_chunks(ones[:, 0:C])[C:P], ALU.mult), fb_pool, value)

            pool.wait_ge(mod_ready, 1)
            zero(1)

            def modulation(wm, i, blocks, first, ring, acc, fills, width):
                step = blocks * width

                def fetch(b):
                    col = bass.ds(i * step + first + b * width, width)
                    pool.dma_start(ring[:, b % 2], wm[:, :, col]).then_inc(pmw_landed[b % 2], 16)
                fetch(0)
                fetch(1)
                for b in range(blocks):
                    pool.wait_ge(pmw_landed[b % 2], i * (8 * blocks) + 16 * (fills + b // 2 + 1))
                    w = ring[:, b % 2]
                    do(pool.tensor_tensor(w, w, cond[:].unsqueeze(2).broadcast_to([P, KT, width]), ALU.mult))
                    do(pool.tensor_tensor(w[:, 0:4], w[:, 0:4], w[:, 4:8], ALU.add))
                    do(pool.tensor_tensor(w[:, 0:2], w[:, 0:2], w[:, 2:4], ALU.add))
                    do(pool.tensor_tensor(acc[:, bass.ds(i * step + b * width, width)], w[:, 0], w[:, 1], ALU.add))
                    if b + 2 < blocks:
                        fetch(b + 2)

            def view(layer):
                return I["w_mod"][layer].rearrange("(k p) n -> p k n", p=P)

            def gdn_pair(i):
                pool.wait_ge(fm_ready, i * 3 + 3)
                expand(FB[2], chunks(S3), i * 2 + 1)
                expand(FB[3], chunks(vf), i * 2 + 2)
                modulation(view(0), i, 8, 2048, mwring2, macc2, 0, P)
            do.loop(GDN_PAIRS, 34, gdn_pair)
            do.tell(pool.memset(mwring2[:, 0, 0], 0.0), macc_ready, 2)

            pool.wait_ge(mix_ready, GDN_PAIRS)
            pool.wait_ge(heads_ready, 1)

            def slices(i):
                for a in range(2):
                    hd = i * 2 + a + 1
                    do(copy(qh, qall[:, :, i * 2 + a]))
                    do(copy(kh, kall[:, :, i * 2 + a]))
                    do.tell(copy(vh, vall[:, :, i * 2 + a]), hslice, hd)
                    pool.wait_ge(o_ready, hd)
            do.loop(4, 4, slices)
            pool.wait_ge(mod_ready, 2)
            pool.wait_ge(tile_taken, 4 + 8)
            do.loop(6, 16, lambda i: modulation(view(1), i, 4, 0, mwring1, macc1, 16, 256))
            do.tell(pool.memset(mblk1, 0.0), macc_ready, 3)
            pool.wait_ge(xmix_ready, 6)
            pool.wait_ge(lora_out, 4)
            zero(2)

            def rwkv_pair(i):
                pool.wait_ge(fm_ready, 12 + i * 3 + 3)
                expand(FB[2], R1[:, :, 0], 8 + i * 2 + 1)
                expand(FB[3], chunks(vf), 8 + i * 2 + 2)
            do.loop(RWKV_PAIRS, 2, rwkv_pair)


def constants():
    import numpy as np

    t = np.zeros((P, NCONST), np.float32)

    def put(name, a):
        at, n = CONST_COLS[name]
        t[:a.shape[0], at:at + n] = a
    j, i = np.meshgrid(np.arange(P) % C, np.arange(C), indexing="ij")
    put("ident", np.eye(P))
    put("ones", np.ones((P, P)))
    put("blk", np.kron(np.eye(2), np.ones((C, C))))
    put("istack", j == i)
    put("strictT", j < i)
    put("inclT", j <= i)

    def doubling(r, c, n):
        return (r >> n == c >> n) & ((r >> (n - 1)) % 2 == 1) & ((c >> (n - 1)) % 2 == 0)
    put("level", np.concatenate([doubling(j, i, n) for n in range(1, LEVELS + 1)], 1))
    put("level1T", doubling(i, j, 1))
    a, b = np.meshgrid(np.arange(P), np.arange(P), indexing="ij")
    put("causal", np.where(b <= a, 0.0, -1e30))
    put("reset", np.tile((np.arange(S) % C != 0).astype(np.float32), (P, 1)))
    put("invfreq", np.tile(np.float32(10000.0) ** (-np.arange(0, ROPE, 2, dtype=np.float32) / ROPE), (P, 1)))
    heads = np.zeros((8, GDN_PAIRS * P))
    for h in range(8):
        heads[h, h * C:(h + 1) * C] = 1
    put("headsel", heads)
    put("eps", np.tile(np.array([EPS, L2_EPS, GN_EPS, 1.0]), (P, 1)))
    return t


def kernel(**inputs):
    import numpy as _np
    import concourse.bacc as _bacc
    from concourse import mybir as _mybir
    from concourse.bass_utils import run_bass_kernel_spmd as _run

    nc = _bacc.Bacc("TRN2", target_bir_lowering=False, num_devices=1)
    arrays, args = {}, {}
    for name, a in dict(inputs, const=constants()).items():
        a = _np.ascontiguousarray(a)
        arrays[f"in_{name}_dram"] = a
        args[name] = nc.dram_tensor(f"in_{name}_dram", a.shape, _mybir.dt.from_np(a.dtype), kind="ExternalInput").ap()
    out = nc.dram_tensor("out_0_dram", (1, S, D), F32, kind="ExternalOutput").ap()
    build(nc, args, out)
    r = _run(nc, [arrays], core_ids=[0])
    return r.results[0]["out_0_dram"]
```

```python
from contextlib import ExitStack

import concourse.bass as bass
from concourse import mybir

F32 = mybir.dt.float32
I32 = mybir.dt.int32
ALU = mybir.AluOpType
ACT = mybir.ActivationFunctionType
AX = mybir.AxisListType

P = 128
S = 512
D = 1024
KT = D // P
TT = S // P
C = 64
NCH = S // C
FF = 4096
FT = FF // P
GDN_W = 512
GDN_PAIRS = 4
RWKV_PAIRS = 8
GDN_STEPS, GDN_ACT_STEPS, RWKV_STEPS, RWKV_ACT_STEPS = 35, 7, 36, 6
GATE_COL = 2048
DQ_COL, DKV_COL, KROPE_COL = 2064, 2320, 2448
REST = 2480 - GATE_COL
QK = 96
NOPE, ROPE, HALF = 64, 32, 16
LEVELS = 6
EPS, L2_EPS, GN_EPS = 1e-6, 1e-12, 64e-5
DECAY = 0.6065306597126334

CONST_COLS = {}
_at = 0
for _name, _n in (("ident", P), ("ones", P), ("blk", P), ("istack", C), ("strictT", C), ("inclT", C),
                  ("level", LEVELS * C), ("level1T", C), ("causal", P), ("reset", S), ("invfreq", HALF),
                  ("headsel", GDN_PAIRS * P), ("eps", 4)):
    CONST_COLS[_name] = (_at, _n)
    _at += _n
NCONST = _at

T1 = {"mu": 0, "w0": 48, "a0": 56, "k_k": 64, "k_a": 72, "r_k": 80, "ln_g": 88, "ln_b": 96}
T1_ROWS = 104
T2 = {"conv": 0, "c": 48, "qng": 56, "kvng": 58, "gdng": 59}
T2_ROWS = 60


def build(nc, I, out):
    with ExitStack() as ctx:
        def sb(name, shape, dt=F32):
            return ctx.enter_context(nc.sbuf_tensor(name, shape, dt))

        def sem(name):
            return ctx.enter_context(nc.semaphore(name))

        PS = ctx.enter_context(nc.psum_tensor("PS", [P, 8, S], F32))
        cst = sb("cst", [P, NCONST])

        def cc(name):
            at, n = CONST_COLS[name]
            return cst[:, at:at + n]

        ident, ones, blk, istack = cc("ident"), cc("ones"), cc("blk"), cc("istack")
        strictT, inclT, level1T, causal, reset = cc("strictT"), cc("inclT"), cc("level1T"), cc("causal"), cc("reset")
        eps6, eps12, epsgn = (cc("eps")[:, j:j + 1] for j in range(3))

        def level(n):
            return cc("level")[:, (n - 1) * C:n * C]

        def over_chunks(mask, n=NCH):
            return mask.unsqueeze(1).broadcast_to([P, n, C])

        def chunks(x):
            return x.rearrange("p (c t) -> p c t", c=NCH)

        def tokens(x):
            return x.rearrange("p c t -> p (c t)")

        def bank(j):
            return PS[:, j, :].rearrange("p (c t) -> p c t", c=NCH)

        def blocks2(j):
            return PS[:, j:j + 2, :].rearrange("p b (c t) -> p (b c) t", c=4)

        xT = sb("xT", [P, KT, S])
        hT = sb("hT", [P, KT, S])
        bmodT = sb("bmodT", [P, 96])
        t1T = sb("t1T", [P, T1_ROWS])
        t2T = sb("t2T", [P, T2_ROWS])
        modT = sb("modT", [P, 48])
        cond = sb("cond", [P, KT])
        cond_t = sb("cond_t", [P, 2, KT])
        sq = sb("sq", [P, 2, S])
        rs = sb("rs", [P, 2, S])
        ones1 = sb("ones1", [P, 1])
        ARENA = 40400
        arena = sb("arena", [P, ARENA])
        cursor = [0]

        def region(*shape):
            n = 1
            for x in shape:
                n *= x
            a = arena[:, cursor[0]:cursor[0] + n]
            cursor[0] += n
            assert cursor[0] <= ARENA, (cursor[0], shape)
            if len(shape) == 2:
                a = a.rearrange("p (a b) -> p a b", a=shape[0])
            if len(shape) == 3:
                a = a.rearrange("p (a b c) -> p a b c", a=shape[0], b=shape[1])
            return a

        xtok = region(TT, D)
        tabs = region(3, P)
        pos_i = region(P).bitcast(I32)
        pos_f = region(P)
        mwring = region(2, KT, 256)
        macc = region(6 * D)
        mblk = region(2, 256)
        cursor[0] = 0
        mix0 = region(KT, S)
        pc = region(16)
        pw = region(4, KT, P)
        EARLY_AT = cursor[0]
        btok, ktok, atok = (region(NCH, C) for _ in range(3))
        R1 = region(NCH, 2, C)
        RB, RK, LTs, XTs, Xs, Pst, Vs, KVe, AKs, AKV, WTs = (region(NCH, C) for _ in range(11))
        U = Xs
        Hs = region(NCH + 1, C)
        gate_k, query_k, bonus_k = region(S), region(S), region(S)
        RBk, RKk = region(NCH, C), region(NCH, C)
        te = region(2, C)
        egC, egK = region(NCH), region(NCH)
        S1, S2, S3, RT, qf, kf, vf, zf, th, tmp, post = (region(S) for _ in range(11))
        PAIR_END = cursor[0]
        Grow, Brow = region(GDN_PAIRS, S), region(GDN_PAIRS, S)
        Gp, Bp = region(S), region(S)
        cb = region(3, S + 3)
        gcol, bcol, glast = region(NCH), region(NCH), region(NCH)
        gatew = region(KT, 16)
        mwring2 = region(2, KT, P)
        MACC2_AT = cursor[0]
        macc2 = region(4 * D)
        rA, rE, rB = tokens(AKs)[0:8], tokens(AKV)[0:8], tokens(WTs)[0:8]
        cursor[0] = PAIR_END
        xr, xk = region(KT, S), region(KT, S)
        lora = region(4, S)
        lw = region(4, P)
        xv = mix0
        xx = arena[:, EARLY_AT:EARLY_AT + KT * S].rearrange("p (k s) -> p k s", k=KT)
        lw1 = arena[:, ARENA - KT * 288:ARENA].rearrange("p (k f) -> p k f", k=KT)
        cursor[0] = KT * S + 16
        mlaw = region(KT, 416)
        assert cursor[0] <= EARLY_AT
        uq = region(2, 768)
        ukv = region(D)
        dq, dkv = region(2, S), region(S)
        grow = region(2, QK)
        gains = region(2, QK)
        krope = region(TT, ROPE)
        ang, rot, trig = region(TT, 2, HALF), region(TT, 2, HALF), region(TT, 2, HALF)
        qall, kall = region(TT, 8, QK), region(TT, 8, QK)
        vall = region(TT, 8, C)
        sqh = region(8, QK)
        ssh = region(2, TT * 8)
        qh, kh = region(TT, QK), region(TT, QK)
        vh = [region(TT, C) for _ in range(2)]
        qhT, khT = region(S), region(S)
        prob = region(TT, S)
        probT = region(TT, S)
        negm, den, rden = region(TT), region(TT), region(TT)
        ropet = [x.rearrange("p a b -> p (a b)").rearrange("p (r t h d) -> p r t h d", r=4, t=TT, h=8)
                 for x in (prob, probT)]
        WRING_AT = cursor[0]
        assert cursor[0] <= MACC2_AT
        cursor[0] = 0
        hid = region(FT, S)
        MLP_AT = cursor[0]
        mwring1 = region(2, KT, 256)
        macc1 = region(6 * D)
        assert cursor[0] <= WRING_AT
        cursor[0] = WRING_AT
        wring = region(2, KT, 256)
        assert cursor[0] <= MACC2_AT
        cursor[0] = MLP_AT
        xout = region(2, D)

        tabs_landed, x_landed, cst_landed = sem("tabs_landed"), sem("x_landed"), sem("cst_landed")
        tabs_T, tabs_ready, x_T, x_ready = sem("tabs_T"), sem("tabs_ready"), sem("x_T"), sem("x_ready")
        cond_tanh, cond_ready = sem("cond_tanh"), sem("cond_ready")
        mw_landed = [sem("mw0_landed"), sem("mw1_landed")]
        pmw_landed = [sem("pmw0_landed"), sem("pmw1_landed")]
        lw1_landed = sem("lw1_landed")
        mw_used = sem("mw_used")
        macc_ready, mod_summed, mod_ready = sem("macc_ready"), sem("mod_summed"), sem("mod_ready")
        vec, act_, pool_ = sem("vec_steps"), sem("act_steps"), sem("pool_steps")
        sq_ready, sq_used, rstd_ready, h_ready = (
            sem("sq_ready"), sem("sq_used"), sem("rstd_ready"), sem("h_ready"))
        w_landed = [sem("w0_landed"), sem("w1_landed")]
        w_used, tile_out, tile_taken = sem("w_used"), sem("tile_out"), sem("tile_taken")
        gw_landed, rows_out, rows_t, rows_e, rows_l, rows_done, rows_bc, gates_ready = (
            sem("gw_landed"), sem("rows_out"), sem("rows_t"), sem("rows_e"), sem("rows_l"), sem("rows_done"),
            sem("rows_bc"), sem("gates_ready"))
        pw_landed = [sem(f"pw{j}_landed") for j in range(4)]
        lw_landed, low_out, proj_out, proj_act, proj_vec = (
            sem("lw_landed"), sem("low_out"), sem("proj_out"), sem("proj_act"), sem("proj_vec"))
        head_sq, head_ss, head_rs = sem("head_sq"), sem("head_ss"), sem("head_rs")
        d_in, d_exp, fm_ready = sem("d_in"), sem("d_exp"), sem("fm_ready")
        r1_ready = sem("r1_ready")
        a_out, tok_out, tok_taken, lts_ready, aks_ready = (
            sem("a_out"), sem("tok_out"), sem("tok_taken"), sem("lts_ready"), sem("aks_ready"))
        vs_out, vs_ready = sem("vs_out"), sem("vs_ready")
        at_out, xs_ready, xt_ready = sem("at_out"), sem("xs_ready"), sem("xt_ready")
        x_out, p_out, ps_ready, q_out = sem("x_out"), sem("p_out"), sem("ps_ready"), sem("q_out")
        akv_out, akv_ready, u0_out, u0_ready, wt_out = (
            sem("akv_out"), sem("akv_ready"), sem("u0_out"), sem("u0_ready"), sem("wt_out"))
        dh_out, hs_ready, w_out, us_ready, y_out = (
            sem("dh_out"), sem("hs_ready"), sem("w_out"), sem("us_ready"), sem("y_out"))
        post_sq, post_ss, post_rs, mix_ready = sem("post_sq"), sem("post_ss"), sem("post_rs"), sem("mix_ready")
        kept, bonus_used = sem("kept"), sem("bonus_used")
        mlaw_landed, hx_ready = sem("mlaw_landed"), sem("hx_ready")
        mla_landed, lat_out, lat_taken, lat_sq, lat_ss, lat_rs, lat_ready = (
            sem("mla_landed"), sem("lat_out"), sem("lat_taken"), sem("lat_sq"), sem("lat_ss"), sem("lat_rs"),
            sem("lat_ready"))
        ang_ready, trig_ready, gains_bc, tok_proj, tok_copied, ssh_ready, rsh_ready, heads_ready = (
            sem("ang_ready"), sem("trig_ready"), sem("gains_bc"), sem("tok_proj"), sem("tok_copied"),
            sem("ssh_ready"), sem("rsh_ready"), sem("heads_ready"))
        hslice, qkT_out, qkT_ready, score_out, max_ready, exp_ready, prob_ready = (
            sem("hslice"), sem("qkT_out"), sem("qkT_ready"), sem("score_out"), sem("max_ready"), sem("exp_ready"),
            sem("prob_ready"))
        pT_out, pT_ready, o_out, o_ready = sem("pT_out"), sem("pT_ready"), sem("o_out"), sem("o_ready")
        xmix_ready, lora_out, lora_ready = sem("xmix_ready"), sem("lora_out"), sem("lora_ready")
        xo_T, xo_ready, out_landed = sem("xo_T"), sem("xo_ready"), [sem("out0_landed"), sem("out1_landed")]
        cb_zeroed = sem("cb_zeroed")

        class Steps:

            def __init__(self, eng, sem_):
                self.eng, self.sem, self.n, self.off = eng, sem_, 0, 0

            def __call__(self, ins):
                self.n += 1
                ins.then_inc(self.sem, 1)
                self.eng.wait_ge(self.sem, self.off + self.n)

            def tell(self, ins, sem_, value):
                ins.then_inc(sem_, 1)
                self.eng.wait_ge(sem_, value)

            def loop(self, count, steps, body):
                start = self.n
                with self.eng.Fori(0, count) as i:
                    self.off = i * steps
                    body(i)
                assert self.n - start == steps, f"the loop has {self.n - start} steps"
                self.off, self.n = 0, start + count * steps

        small8 = sb("small8", [8, 4])
        posT = sb("posT", [P, TT])
        gate_cols = sb("gate_cols", [P, KT])
        tmp_r = sq
        one = cc("eps")[:, 3:4]

        BLK = {"o0": 0, "up0": 4, "down0": 20, "o1": 36, "up1": 40, "down1": 56}
        TIL = {"o0": 0, "up0": 8, "down0": 40, "o1": 48, "up1": 56, "down1": 88}
        X_DONE = [None, 4 + 8, 4 + 48, 4 + 56]
        SHIFT, SCALE, GATE = (0, 24), (8, 32), (16, 40)

        def rotate(do, eng, a, x):
            tt = eng.tensor_tensor
            flat = x.rearrange("p t h d -> p (t h) d")
            do(tt(flat, flat, ssh[:, a].unsqueeze(2).broadcast_to([P, TT * 8, QK]), ALU.mult))
            do(tt(flat, flat, gains[:, a].unsqueeze(1).broadcast_to([P, TT * 8, QK]), ALU.mult))
            x1, x2 = x[:, :, :, NOPE:NOPE + HALF], x[:, :, :, NOPE + HALF:QK]
            cos, sin = (trig[:, :, b].unsqueeze(2).broadcast_to([P, TT, 8, HALF]) for b in range(2))
            for r, (y, f) in enumerate(((x1, cos), (x2, sin), (x2, cos), (x1, sin))):
                do(tt(ropet[a][:, r], y, f, ALU.mult))
            do(tt(x1, ropet[a][:, 0], ropet[a][:, 1], ALU.subtract))
            do(tt(x2, ropet[a][:, 2], ropet[a][:, 3], ALU.add))

        block = ctx.enter_context(nc.Block())

        @block.sync
        def _(sp):
            sp.dma_start(cst[:], I["const"][:, :]).then_inc(cst_landed, 16)

            def table(dst, src):
                sp.dma_start(dst, src).then_inc(tabs_landed, 16)
            table(tabs[0:96, 0, :], I["b_mod"].rearrange("l (r f) -> (l r) f", f=P))
            table(tabs[0:48, 1, :], I["rwkv_mu"].rearrange("a j (r f) -> (a j r) f", f=P))
            for name in ("w0", "a0", "k_k", "k_a", "ln_g", "ln_b"):
                src = {"ln_g": "rwkv_ln_gain", "ln_b": "rwkv_ln_bias"}.get(name, "rwkv_" + name)
                table(tabs[T1[name]:T1[name] + KT, 1, :], I[src].rearrange("a (r f) -> (a r) f", f=P))
            table(tabs[T1["r_k"]:T1["r_k"] + KT, 1, :], I["rwkv_r_k"].rearrange("a (r h) d -> (a r) (h d)", h=2))
            table(tabs[0:48, 2, :], I["gdn_conv_w"].rearrange("a j (r f) -> (a j r) f", f=P))
            table(tabs[48:56, 2, :], I["c"].rearrange("a (r f) -> (a r) f", f=P))
            table(tabs[56:58, 2, :], I["mla_q_norm_gain"].rearrange("a (r f) -> (a r) f", f=P))
            table(tabs[58:59, 2, :], I["mla_kv_norm_gain"])
            table(tabs[59:60, 2, 0:C], I["gdn_norm_gain"])
            table(tabs[59:60, 2, C:P], I["gdn_norm_gain"])
            table(pos_i[0:TT, :], I["positions"].rearrange("a (t p) -> (a t) p", p=P))
            table(small8[:, 0:1], I["gdn_dt_bias"].rearrange("a h -> h a"))
            table(small8[:, 1:2], I["gdn_a_log"].rearrange("a h -> h a"))
            sp.dma_start(xtok, I["x"][0].rearrange("(t p) d -> p t d", p=P)).then_inc(x_landed, 16)

            wm = I["w_mod"][0].rearrange("(k p) n -> p k n", p=P)
            with sp.Fori(0, 4) as i:
                for s in range(2):
                    sp.wait_ge(mw_used, i * 2 + s + 1)
                    sp.dma_start(mwring[:, s], wm[:, :, bass.ds(i * 512 + s * 256, 256)]).then_inc(mw_landed[s], 16)

            win = I["w_in0"][0].rearrange("(k p) n -> p k n", p=P)
            sp.wait_ge(mod_ready, 1)
            sp.wait_ge(x_ready, KT)
            sp.dma_start(gatew, win[:, :, GATE_COL:GATE_COL + 16]).then_inc(gw_landed, 16)
            with sp.Fori(0, GDN_PAIRS) as i:
                for j in range(4):
                    sp.wait_ge(proj_out, i * 4 + j + 1)
                    sp.dma_start(pw[:, j], win[:, :, bass.ds(i * P + j * GDN_W, P)]).then_inc(pw_landed[j], 16)

            sp.wait_ge(proj_out, 4 + 4 * GDN_PAIRS)
            sp.dma_start(mlaw, win[:, :, DQ_COL:DQ_COL + 416]).then_inc(mlaw_landed, 16)
            sp.wait_ge(mix_ready, GDN_PAIRS)
            sp.dma_start(uq, I["mla_w_uq"][0].rearrange("(k p) n -> p k n", p=P)).then_inc(mla_landed, 16)
            sp.dma_start(ukv, I["mla_w_ukv"][0]).then_inc(mla_landed, 16)
            sp.dma_start(grow[0:1, 0, :], I["mla_q_head_gain"]).then_inc(mla_landed, 16)
            sp.dma_start(grow[0:1, 1, :], I["mla_k_head_gain"]).then_inc(mla_landed, 16)

            def stream(name, wv, rows):
                b = BLK[name]
                n = wv.shape[2] // 256 * rows
                per = 2 * rows
                with sp.Fori(0, n // per) as i:
                    for s in range(per):
                        sp.wait_ge(w_used, i * per + b + s + 1)
                        r, col = s % rows, s // rows
                        sp.dma_start(wring[:, s % 2],
                                     wv[:, r * KT:(r + 1) * KT, bass.ds(i * 512 + col * 256, 256)]
                                     ).then_inc(w_landed[s % 2], 16)

            def view(w):
                return w.rearrange("(k p) n -> p k n", p=P)

            sp.wait_ge(macc_ready, 2)
            stream("o0", view(I["w_out0"][0]), 1)
            stream("up0", view(I["w_up"][0]), 1)

            sp.wait_ge(mod_ready, 2)
            for name, a, n in (("rwkv_w1", 0, 64), ("rwkv_a1", 64, 64), ("rwkv_g1", 128, 160)):
                sp.dma_start(lw1[:, :, a:a + n], view(I[name][0])).then_inc(lw1_landed, 16)
            stream("down0", view(I["w_down"][0]), 4)

            sp.wait_ge(tile_taken, 4 + 48)
            wp = [view(I[n][0]) for n in ("rwkv_w_r", "rwkv_w_k", "rwkv_w_v")]
            with sp.Fori(0, RWKV_PAIRS) as i:
                for j in range(3):
                    sp.wait_ge(proj_out, i * 3 + 18 + j)
                    sp.dma_start(pw[:, j], wp[j][:, :, bass.ds(i * P, P)]).then_inc(pw_landed[j], 16)
                sp.wait_ge(low_out, i * 3 + 3)
                for dst, src in ((lw[0:64, 0, :], I["rwkv_w2"][0]), (lw[0:64, 1, :], I["rwkv_a2"][0]),
                                 (lw[:, 2, :], I["rwkv_g2"][0, 0:P]), (lw[0:32, 3, :], I["rwkv_g2"][0, P:160])):
                    sp.dma_start(dst, src[:, bass.ds(i * P, P)]).then_inc(lw_landed, 16)
            sp.wait_ge(mix_ready, GDN_PAIRS + RWKV_PAIRS)
            stream("o1", view(I["rwkv_w_o"][0]), 1)
            stream("up1", view(I["w_up"][1]), 1)
            stream("down1", view(I["w_down"][1]), 4)
            for t in range(TT):
                sp.wait_ge(xo_ready, 2 * t + 2)
                sp.dma_start(out[0, t * P:(t + 1) * P, :], xout[:, t % 2]).then_inc(out_landed[t % 2], 16)
            for b in range(2):
                sp.wait_ge(out_landed[b], 16 * TT // 2)

        @block.tensor
        def _(pe):
            def mm(o, l, r, first=True, last=True):
                return pe.matmul(o, l, r, start=first, stop=last)

            def alone(value):
                if not isinstance(value, int):
                    value = pe.to_reg(value)
                    pe.wait_ge(cst_landed, 16)
                return value

            def heads(o, l, r, c, first=True, last=True):
                for h in (slice(0, C), slice(C, P)):
                    m = mm(o[h, c], l[h, c], r[h, c], first, last)
                return m

            def turned(o, src):
                for c in range(NCH):
                    pe.transpose(o[0:C, c], src[0:C, c], ident[0:C, 0:C])
                    m = mm(o[C:P, c], src[C:P, c], istack[C:P])
                return m

            pe.wait_ge(cst_landed, 16)
            pe.wait_ge(tabs_landed, 16 * 18)
            for j, r in ((0, 96), (1, T1_ROWS), (2, T2_ROWS)):
                pe.transpose(PS[:, j, 0:r], tabs[0:r, j, :], ident[0:r, 0:r])
            pe.wait_ge(rows_t, 1)
            pe.transpose(PS[:, 3, 0:TT], pos_f[0:TT, :], ident[0:TT, 0:TT]).then_inc(tabs_T, 1)
            pe.wait_ge(x_landed, 16)
            for k in range(KT):
                if k >= 2:
                    pe.wait_ge(x_ready, k - 1)
                for t in range(TT):
                    m = pe.transpose(PS[:, 4 + k % 2, t * P:(t + 1) * P], xtok[:, t, k * P:(k + 1) * P], ident)
                m.then_inc(x_T, 1)

            def mod_sums(acc, n, phase):
                pe.wait_ge(macc_ready, phase + 1)
                for j in range(n):
                    m = mm(PS[:, 7, j:j + 1], acc[:, j * P:(j + 1) * P], ones1[:])
                m.then_inc(mod_summed, 1)

            def norm_sums(idx):
                for k in range(KT):
                    pe.wait_ge(sq_ready, idx * KT + k + 1)
                    m = mm(PS[:, 6, :], ones, sq[:, k % 2], k == 0, k == KT - 1)
                    m.then_inc(sq_used, 1)

            norm_sums(0)
            mod_sums(macc, 16, 0)

            pe.wait_ge(gw_landed, 16)
            for j in range(2):
                for k in range(KT):
                    pe.wait_ge(h_ready, k + 1)
                    m = mm(PS[0:8, j, :], gatew[:, k, j * 8:j * 8 + 8], hT[:, k], k == 0, k == KT - 1)
                m.then_inc(rows_out, 1)
            def projection(pair, j, src, landed, taken):
                for k in range(KT):
                    if k == 0:
                        pe.wait_ge(pw_landed[j], landed)
                        if taken is not None:
                            pe.wait_ge(proj_act, taken)
                    m = mm(PS[:, 6 + j % 2, :], pw[:, j, k], src[:, k], k == 0, k == KT - 1)
                    if k == KT - 1:
                        m.then_inc(proj_out, 1)
                    yield

            def project(pair, base, srcs, first=False):
                rw = base > 0
                done = 20 + pair * 6 if rw else pair * 5
                for j, src in enumerate(srcs):
                    if j >= 2:
                        taken = done + j - 1
                    elif first:
                        taken = None
                    elif rw:
                        taken = done - 3
                    else:
                        taken = done - 2 + 2 * j
                    yield from projection(pair, j, src, (pair + base) * 16 + 16, taken)

            def drop(_count):
                return None

            def filler(products):
                def fill(count):
                    for _ in range(count):
                        next(products, None)
                return fill

            def decayed(n, rw):
                pe.wait_ge(r1_ready, alone(n))
                pe.wait_ge(fm_ready, alone(12 + (n - GDN_PAIRS) * 3 if rw else n * 3))
                for j, k in enumerate((S2, S3) if rw else (kf,)):
                    for c in range(NCH):
                        m = heads(blocks2(2 * j), chunks(k), R1.rearrange("p c a t -> p c (a t)"), c)
                m.then_inc(a_out, 1)

            def outputs(n, rw):
                pe.wait_ge(kept, alone(n))
                for c in range(NCH):
                    for h in (slice(0, C), slice(C, P)):
                        o = bank(4)[h, c]
                        mm(o, Hs[h, c], chunks(query_k)[h, c], True, False)
                        m = mm(o, U[h, c], RBk[h, c], False, not rw)
                        if rw:
                            m = mm(o, Vs[h, c], RKk[h, c], False, True)
                m.then_inc(y_out, 1)

            def post_sum(value, j, b):
                pe.wait_ge(post_sq, alone(value))
                mm(PS[:, b, :], blk, sq[:, j]).then_inc(post_ss, 1)

            def tokens_major(n, rw, fill, post):
                pe.wait_ge(lts_ready, alone(n))
                turned(bank(0), LTs).then_inc(at_out, 1)
                if rw:
                    pe.wait_ge(aks_ready, alone(n - GDN_PAIRS))
                turned(bank(2), chunks(S2 if rw else tmp)).then_inc(tok_out, 1)
                if rw:
                    turned(bank(3), chunks(S3)).then_inc(tok_out, 1)
                if post is not None:
                    post_sum(post, 0, 5)
                turned(bank(1), chunks(vf)).then_inc(vs_out, 1)
                if rw and post is not None:
                    post_sum(post + 1, 1, 4)
                if rw:
                    pe.wait_ge(vs_ready, alone(n - GDN_PAIRS))
                else:
                    pe.wait_ge(akv_ready, alone(n))

            def levels(n, rw, lo, hi, fill, prep, nxt):
                for lv in range(lo, hi + 1):
                    q = 5 * (n - 1) + lv - 1
                    pe.wait_ge(xs_ready, alone(q))
                    for c in range(NCH):
                        m = heads(bank(1), LTs, Xs, c)
                    m.then_inc(p_out, 1)
                    fill(2)
                    prep()
                    pe.wait_ge(ps_ready, alone(q))
                    pe.wait_ge(xt_ready, alone(6 * (n - 1) + lv - 1))
                    if lv <= 3:
                        pe.wait_ge(tok_taken, alone(3 * n - 3 + lv if rw or lv == 3 else 3 * n - 2))
                    for c in range(NCH):
                        m = heads(bank(3), Pst, XTs, c)
                    m.then_inc(q_out, 1)
                    if lv < LEVELS:
                        for c in range(NCH):
                            m = heads(bank(2), XTs, Pst, c)
                        m.then_inc(x_out, 1)
                        prep()
                        fill(1)
                    if lv == 2:
                        pe.wait_ge(xs_ready, alone(q + 1))
                        turned(bank(2), chunks(S3) if not rw else R1[:, :, 0]).then_inc(tok_out, 1)
                    if lv == LEVELS and rw:
                        if nxt:
                            pe.wait_ge(bonus_used, alone(n - GDN_PAIRS + 1))
                            pe.wait_ge(head_rs, alone(8 + n - GDN_PAIRS + 1))
                        for c in range(NCH):
                            m = heads(bank(4), AKs, Vs, c)
                        m.then_inc(akv_out, 1)

            def across_chunks(n, rw, fill):
                pe.wait_ge(xt_ready, alone(6 * n))
                for c in range(NCH):
                    m = heads(bank(1), atok, XTs, c)
                m.then_inc(wt_out, 1)
                pe.wait_ge(akv_ready, alone(n))
                for c in range(NCH):
                    m = heads(bank(0), XTs, AKV, c)
                m.then_inc(u0_out, 1)
                if rw:
                    for c in range(NCH):
                        m = heads(bank(5), ktok, Vs, c)
                    m.then_inc(akv_out, 1)
                fill(1)
                pe.wait_ge(u0_ready, alone(n))
                for c in range(NCH - 1):
                    if c:
                        pe.wait_ge(us_ready, alone(7 * (n - 1) + c))
                    heads(PS[:, c % 2, 0:C].unsqueeze(1), btok[:, c:c + 1], U[:, c:c + 1], 0).then_inc(dh_out, 1)
                    fill(1)
                    pe.wait_ge(hs_ready, alone(7 * (n - 1) + c + 1))
                    heads(PS[:, 2 + c % 2, 0:C].unsqueeze(1), WTs[:, c + 1:c + 2], Hs[:, c + 1:c + 2], 0
                          ).then_inc(w_out, 1)
                    fill(1)
                fill(1)
                pe.wait_ge(us_ready, alone(7 * n))

            def pair(i, base, rw, sums, srcs, follow, nxt):
                n = i + base + 1
                prepared = sums(i + 1) if nxt else iter(())
                products = project(i + 2, base, srcs) if follow else iter(())

                def fill(count):
                    for _ in range(count):
                        next(products, None)
                levels(n, rw, 3, LEVELS, lambda count: None, lambda: next(prepared, None), nxt)
                for _ in prepared:
                    pass
                across_chunks(n, rw, fill)
                if nxt:
                    decayed(n + 1, rw)
                fill(1)
                outputs(n, rw)
                post = 4 + 2 * i + 1 if rw else i + 1
                if nxt:
                    tokens_major(n + 1, rw, fill, post)
                    levels(n + 1, rw, 2, 2, fill, lambda: None, nxt)
                    fill(8 * KT)
                else:
                    post_sum(post, 0, 5)
                    if rw:
                        post_sum(post + 1, 1, 4)
                pe.wait_ge(mix_ready, alone(n))

            def pairs(count, base, rw, sums, srcs, between):
                products = project(0, base, srcs, first=True)
                for _ in range(2 * KT):
                    next(products)
                between()
                for _ in products:
                    pass
                products = project(1, base, srcs)
                for _ in sums(0):
                    for _ in range(4 if rw else 2):
                        next(products, None)
                for _ in products:
                    pass
                decayed(base + 1, rw)
                tokens_major(base + 1, rw, lambda count: None, None)
                levels(base + 1, rw, 2, 2, lambda count: None, lambda: None, True)
                with pe.Fori(0, count - 2) as i:
                    pair(i, base, rw, sums, srcs, True, True)
                pair(count - 2, base, rw, sums, srcs, False, True)
                pair(count - 1, base, rw, sums, srcs, False, False)

            def gdn_sums(i):
                for _ in range(6):
                    yield
                pe.wait_ge(head_sq, i * 2 + 2)
                for j in range(2):
                    m = mm(PS[:, 4 + j, :], blk, sq[:, j])
                m.then_inc(head_ss, 1)
                yield

            def spread_gates():
                pe.wait_ge(rows_done, 1)
                for p in range(GDN_PAIRS):
                    if p == GDN_PAIRS - 1:
                        pe.wait_ge(gates_ready, 1)
                    for j, src in enumerate((rA, rB)):
                        m = mm(PS[:, 2 * (p % 3) + j, :], cc("headsel")[0:8, p * P:(p + 1) * P], src)
                    if p >= GDN_PAIRS - 2:
                        m.then_inc(rows_bc, 1)
                pe.wait_ge(gates_ready, 2)

            pairs(GDN_PAIRS, 0, False, gdn_sums, [hT] * 4, spread_gates)

            pe.wait_ge(mlaw_landed, 16)
            for j in range(3):
                for k in range(KT):
                    m = mm(PS[:, j, :], mlaw[:, k, j * P:(j + 1) * P], hT[:, k], k == 0, k == KT - 1)
                m.then_inc(lat_out, 1)
            for t in range(TT):
                for k in range(KT):
                    m = mm(PS[:, 3, t * ROPE:(t + 1) * ROPE], hT[:, k, t * P:(t + 1) * P], mlaw[:, k, 384:416],
                           k == 0, k == KT - 1)
            m.then_inc(lat_out, 1)
            pe.wait_ge(mla_landed, 16 * 4)
            for j in range(2):
                m = mm(PS[:, 4, j * QK:(j + 1) * QK], ones[0:1, :], grow[0:1, j, :])
            m.then_inc(gains_bc, 1)
            for j in range(3):
                pe.wait_ge(lat_sq, j + 1)
                m = mm(PS[:, 5 + j // 2, :], ones, sq[:, j % 2], j != 1, j != 0)
                m.then_inc(lat_ss, 1)
            pe.wait_ge(lat_ready, 1)
            for t in range(TT):
                if t:
                    pe.wait_ge(tok_copied, t)
                cols = slice(t * P, (t + 1) * P)
                for j in range(2):
                    for k in range(2):
                        mm(PS[:, j, 0:384], dq[:, k, cols], uq[:, k, j * 384:(j + 1) * 384], k == 0, k == 1)
                for j in range(2):
                    m = mm(PS[:, 2 + j, :], dkv[:, cols], ukv[:, j * S:(j + 1) * S])
                m.then_inc(tok_proj, 1)

            def turn_qk(hd):
                pe.wait_ge(hslice, hd)
                for t in range(TT):
                    pe.transpose(PS[0:QK, 0, t * P:(t + 1) * P], qh[:, t], ident)
                for t in range(TT):
                    m = pe.transpose(PS[0:QK, 1, t * P:(t + 1) * P], kh[:, t], ident)
                m.then_inc(qkT_out, 1)

            def scores(hd):
                pe.wait_ge(qkT_ready, hd)
                for t in range(TT):
                    mm(PS[:, 2 + t, 0:(t + 1) * P], qhT[0:QK, t * P:(t + 1) * P],
                       khT[0:QK, 0:(t + 1) * P]).then_inc(score_out, 1)

            def attend(i, last):
                for a in range(2):
                    hd = i * 2 + a + 1
                    follow = not (last and a == 1)
                    if follow:
                        turn_qk(hd + 1)
                    pe.wait_ge(prob_ready, hd)
                    for kt in range(TT):
                        for t in range(kt, TT):
                            m = pe.transpose(PS[:, 2 + kt, t * P:(t + 1) * P], prob[:, t, kt * P:(kt + 1) * P], ident)
                    m.then_inc(pT_out, 1)
                    pe.wait_ge(pT_ready, hd)
                    if follow:
                        scores(hd + 1)
                    for kt in range(TT):
                        m = mm(PS[a * C:(a + 1) * C, 6 + a, kt * P:S], vh[a][:, kt], probT[:, kt, kt * P:S],
                               kt == 0, kt == TT - 1)
                    m.then_inc(o_out, 1)

            mod_sums(macc2, 32, 1)
            pe.wait_ge(mod_ready, 2)
            turn_qk(1)
            scores(1)
            with pe.Fori(0, 3) as i:
                attend(i, False)
            attend(3, True)
            pe.wait_ge(o_ready, 8)

            def tile(j, src, first, last, base, slot, mt, ready):
                for k in range(KT):
                    if ready is not None:
                        pe.wait_ge(h_ready, ready + k + 1)
                    m = mm(PS[:, j, :], wring[:, slot, k, mt * P:(mt + 1) * P], src[:, base + k],
                           first and k == 0, last and k == KT - 1)
                return m

            def stream(name, src, n, rows, ready=None):
                b, t0 = BLK[name], TIL[name]
                per = 2 * rows
                with pe.Fori(0, n // per) as i:
                    for s in range(per):
                        slot, r = s % 2, s % rows
                        pe.wait_ge(w_landed[slot], (i * (per // 2) + (b + s - slot) // 2 + 1) * 16)
                        for mt in range(2):
                            t = (s // rows) * 2 + mt
                            if r == 0:
                                pe.wait_ge(tile_taken, i * 4 + t0 + t + 1)
                            m = tile(t, src, r == 0, r == rows - 1, r * KT, slot, mt, ready)
                            if mt == 1 and r < rows - 1:
                                m.then_inc(w_used, 1)
                            elif r == rows - 1:
                                m.then_inc(tile_out, 1)
                        if r == rows - 1:
                            mm(PS[0:1, 7, 0:1], ones1[:], ones1[:]).then_inc(w_used, 1)

            stream("o0", mix0, 4, 1)
            norm_sums(1)
            stream("up0", hT, 16, 1, ready=KT)
            pe.wait_ge(tile_taken, 4 + 40)
            stream("down0", hid, 16, 4)
            mod_sums(macc1, 48, 2)
            norm_sums(2)

            pe.wait_ge(lw1_landed, 16 * 3)
            for j, (src, a, m_) in enumerate(((xr, 0, 64), (xk, 64, 64), (xv, 128, P), (xv, 256, 32))):
                for k in range(KT):
                    if j < 3:
                        pe.wait_ge(xmix_ready, j * KT + k + 1)
                    m = mm(PS[0:m_, j, :], lw1[:, k, a:a + m_], src[:, k], k == 0, k == KT - 1)
                m.then_inc(lora_out, 1)
            pe.wait_ge(lora_ready, 4)
            pe.wait_ge(xmix_ready, 6 * KT)

            def rwkv_sums(i):
                pe.wait_ge(lw_landed, i * 64 + 64)
                mm(PS[:, 4, :], lw[0:64, 0], lora[0:64, 0]).then_inc(low_out, 1)
                mm(PS[:, 5, :], lw[0:64, 1], lora[0:64, 1]).then_inc(low_out, 1)
                yield
                pe.wait_ge(proj_act, 20 + i * 6 + 4)
                mm(PS[:, 4, :], lw[:, 2], lora[:, 2], True, False)
                mm(PS[:, 4, :], lw[0:32, 3], lora[0:32, 3], False, True).then_inc(low_out, 1)
                yield
                pe.wait_ge(head_sq, 8 + i * 2 + 1)
                pe.wait_ge(proj_act, 20 + i * 6 + 6)
                mm(PS[:, 5, :], blk, sq[:, 0]).then_inc(head_ss, 1)
                yield
                pe.wait_ge(head_sq, 8 + i * 2 + 2)
                mm(PS[:, 4, :], blk, sq[:, 1]).then_inc(head_ss, 1)
                yield

            pairs(RWKV_PAIRS, GDN_PAIRS, True, rwkv_sums, [xr, xk, xv], lambda: None)
            stream("o1", hT, 4, 1)
            norm_sums(3)
            stream("up1", hT, 16, 1, ready=3 * KT)
            pe.wait_ge(tile_taken, 4 + 88)
            stream("down1", hid, 16, 4)
            pe.wait_ge(tile_taken, 4 + 96)
            for t in range(TT):
                for hf in range(2):
                    q = 2 * t + hf
                    if q >= 2:
                        pe.wait_ge(xo_ready, q - 1)
                    for k in range(4):
                        m = pe.transpose(PS[:, q % 2, k * P:(k + 1) * P], xT[:, hf * 4 + k, t * P:(t + 1) * P], ident)
                    m.then_inc(xo_T, 1)

        @block.vector
        def _(dve):
            do = Steps(dve, vec)
            tt, ts, stt = dve.tensor_tensor, dve.tensor_scalar, dve.scalar_tensor_tensor
            dve.memset(ones1[:], 1.0).then_inc(tile_taken, 4)
            dve.wait_ge(tile_taken, 4)
            dve.memset(ones1[:], 1.0).then_inc(w_used, 2)
            dve.wait_ge(w_used, 2)
            dve.memset(ones1[:], 1.0).then_inc(mw_used, 2)
            dve.wait_ge(mw_used, 2)
            dve.memset(ones1[:], 1.0).then_inc(proj_out, 4)
            dve.wait_ge(proj_out, 4)
            dve.memset(ones1[:], 1.0).then_inc(low_out, 3)
            dve.wait_ge(low_out, 3)
            dve.memset(ones1[:], 1.0).then_inc(o_out, 1)
            dve.wait_ge(o_out, 1)

            dve.wait_ge(tabs_landed, 16 * 18)
            do.tell(dve.tensor_copy(pos_f[0:TT, :], pos_i[0:TT, :]), rows_t, 1)
            dve.wait_ge(tabs_T, 1)
            do(dve.tensor_copy(bmodT[:], PS[:, 0, 0:96]))
            do(dve.tensor_copy(t1T[:], PS[:, 1, 0:T1_ROWS]))
            do(dve.tensor_copy(t2T[:], PS[:, 2, 0:T2_ROWS]))
            do(dve.tensor_copy(posT[:], PS[:, 3, 0:TT]))
            do(ts(t1T[:, T1["w0"]:T1["w0"] + 16], t1T[:, T1["w0"]:T1["w0"] + 16], 0.5, None, ALU.mult))
            do(ts(t2T[:, 0:56], t2T[:, 0:56], 0.5, None, ALU.mult))
            do.tell(dve.tensor_copy(cond_t[:, 0], t2T[:, 48:56]), tabs_ready, 1)
            dve.wait_ge(cond_tanh, 1)
            do(stt(cond[:], cond_t[:, 1], 1.0, cond_t[:, 0], ALU.add, ALU.mult))
            do.tell(dve.tensor_copy(cond_t[:, 0], cond[:]), cond_ready, 1)

            def mod_block(i):
                for s in range(2):
                    dve.wait_ge(mw_landed[s], i * 16 + 16)
                    do(ts(mblk[:, s], mwring[:, s, 0], cond[:, 0:1], None, ALU.mult))
                    for k in range(1, KT - 1):
                        do(stt(mblk[:, s], mwring[:, s, k], cond[:, k:k + 1], mblk[:, s], ALU.mult, ALU.add))
                    do.tell(stt(macc[:, bass.ds(i * 512 + s * 256, 256)], mwring[:, s, KT - 1], cond[:, KT - 1:KT],
                                mblk[:, s], ALU.mult, ALU.add), mw_used, i * 2 + s + 3)
            do.loop(4, 14, mod_block)
            do.tell(dve.tensor_copy(cond_t[:, 0], cond[:]), macc_ready, 1)

            def mod_finish(layer, phase, a, b):
                dve.wait_ge(mod_summed, phase + 1)
                do(tt(modT[:, a:b], PS[:, 7, 0:b - a], bmodT[:, layer * 48 + a:layer * 48 + b], ALU.add))
                for g in SCALE:
                    if a <= g < b:
                        do(ts(modT[:, g:g + KT], modT[:, g:g + KT], 1.0, None, ALU.add))
                do.tell(dve.tensor_copy(cond_t[:, 0], cond[:]), mod_ready, phase + 1)

            def norm(idx):
                half = idx % 2
                dve.wait_ge(rstd_ready, idx + 1)
                for k in range(KT):
                    do.tell(stt(hT[:, k], xT[:, k], modT[:, SCALE[half] + k:SCALE[half] + k + 1], rs[:, 0],
                                ALU.mult, ALU.mult), hx_ready, idx * KT + k + 1)

            mod_finish(0, 0, 0, 16)
            do.tell(dve.memset(cb[:], 0.0), cb_zeroed, 1)
            norm(0)

            rC = tmp[0:8]
            dve.wait_ge(rows_out, 2)
            do(ts(rA, PS[0:8, 0, :], small8[:, 0:1], None, ALU.add))
            do.tell(stt(rE, rA, -1.0, rA, ALU.mult, ALU.min), rows_e, 1)
            dve.wait_ge(rows_l, 2)
            do(ts(rA, rA, 0.0, None, ALU.max))
            do(tt(rA, rA, rE, ALU.add))
            do(ts(rC, rA, small8[:, 2:3], -1.0, ALU.mult, ALU.mult))
            do(dve.tensor_tensor_scan(rA, reset[0:8, :], rC, 0.0, ALU.mult, ALU.add))
            do.tell(ts(rB, rB, 0.5, 0.5, ALU.mult, ALU.add), rows_done, 1)
            dve.wait_ge(gates_ready, 2)
            do(dve.memset(Hs[:, 0], 0.0))

            def masks(n, rw):
                dve.wait_ge(a_out, n)
                if rw:
                    do(tt(LTs, blocks2(0)[:, :, 0:C], over_chunks(strictT), ALU.mult))
                    do.tell(tt(RB, blocks2(0)[:, :, C:P], over_chunks(inclT), ALU.mult), lts_ready, n)
                    do(tt(AKs, blocks2(2)[:, :, 0:C], over_chunks(strictT), ALU.mult))
                    do.tell(tt(RK, blocks2(2)[:, :, C:P], over_chunks(inclT), ALU.mult), aks_ready, n - GDN_PAIRS)
                else:
                    do(tt(LTs, blocks2(0)[:, :, 0:C], chunks(S1), ALU.mult))
                    do.tell(tt(RB, blocks2(0)[:, :, C:P], chunks(S2), ALU.mult), lts_ready, n)

            def first_level(n, rw):
                do(tt(XTs, LTs, over_chunks(level1T), ALU.mult))
                do.tell(tt(XTs, XTs, over_chunks(istack), ALU.add), xt_ready, 6 * (n - 1) + 1)
                dve.wait_ge(at_out, n)
                do(tt(Xs, bank(0), over_chunks(level(1)), ALU.mult))
                do.tell(tt(Xs, Xs, over_chunks(istack), ALU.add), xs_ready, 5 * (n - 1) + 1)
                if not rw:
                    dve.wait_ge(vs_out, n)
                    do.tell(tt(AKV, bank(1), bcol.unsqueeze(2).broadcast_to([P, NCH, C]), ALU.mult), akv_ready, n)

            def levels(n, rw, lo, hi, prep):
                for lv in range(lo, hi + 1):
                    q = 5 * (n - 1) + lv - 1
                    dve.wait_ge(p_out, q)
                    do.tell(tt(Pst, bank(1), over_chunks(level(lv)), ALU.mult), ps_ready, q)
                    prep(3)
                    dve.wait_ge(q_out, q)
                    if lv < LEVELS:
                        dve.wait_ge(x_out, 4 * (n - 1) + lv - 1)
                        do.tell(tt(Xs, Xs, bank(2), ALU.add), xs_ready, q + 1)
                    do.tell(tt(XTs, XTs, bank(3), ALU.add), xt_ready, 6 * (n - 1) + lv)
                    prep(2)

            def across_chunks(n, rw, prep):
                if rw:
                    dve.wait_ge(akv_out, 2 * (n - GDN_PAIRS) - 1)
                    do.tell(dve.tensor_copy(AKV, bank(4)), akv_ready, n)
                prep(2)
                if rw:
                    dve.wait_ge(akv_out, 2 * (n - GDN_PAIRS))
                    do(tt(KVe, bank(5), egK.unsqueeze(2).broadcast_to([P, NCH, C]), ALU.mult))
                dve.wait_ge(u0_ready, n)
                for c in range(NCH - 1):
                    e = egK[:, c:c + 1]
                    if rw:
                        do(stt(te[:, 0], Hs[:, c], e, KVe[:, c], ALU.mult, ALU.add))
                    dve.wait_ge(dh_out, 7 * (n - 1) + c + 1)
                    if rw:
                        h = stt(Hs[:, c + 1], PS[:, c % 2, 0:C], e, te[:, 0], ALU.mult, ALU.add)
                    else:
                        h = stt(Hs[:, c + 1], Hs[:, c], e, PS[:, c % 2, 0:C], ALU.mult, ALU.add)
                    do.tell(h, hs_ready, 7 * (n - 1) + c + 1)
                    dve.wait_ge(w_out, 7 * (n - 1) + c + 1)
                    do.tell(tt(U[:, c + 1], U[:, c + 1], PS[:, 2 + c % 2, 0:C], ALU.add), us_ready,
                            7 * (n - 1) + c + 1)
                    prep(1)

            def keep_pair(n, rw):
                do(dve.tensor_copy(gate_k, zf))
                do(dve.tensor_copy(chunks(query_k), R1[:, :, 1] if rw else chunks(RT)))
                do(dve.tensor_copy(RBk, RB))
                if rw:
                    do(dve.tensor_copy(bonus_k, post))
                    do(dve.tensor_copy(RKk, RK))
                do.tell(dve.tensor_copy(egK, egC), kept, n)

            def pair(i, base, rw, prepare, finish, nxt):
                n = i + base + 1
                steps = prepare(i + 1) if nxt else iter(())

                def prep(count):
                    for _ in range(count):
                        next(steps, None)
                keep_pair(n, rw)
                levels(n, rw, 3, LEVELS, prep)
                across_chunks(n, rw, prep)
                for _ in steps:
                    pass
                if nxt:
                    masks(n + 1, rw)
                finishing = finish(i)
                next(finishing)
                if nxt:
                    first_level(n + 1, rw)
                    levels(n + 1, rw, 2, 2, lambda count: next(finishing, None) if count == 3 else None)
                for _ in finishing:
                    pass

            def pairs(count, base, rw, steps, prepare, finish):
                for _ in prepare(0):
                    pass
                masks(base + 1, rw)
                first_level(base + 1, rw)
                levels(base + 1, rw, 2, 2, lambda count: None)
                do.loop(count - 2, steps, lambda i: pair(i, base, rw, prepare, finish, True))
                pair(count - 2, base, rw, prepare, finish, True)
                pair(count - 1, base, rw, prepare, finish, False)

            def silu(x, t):
                return stt(x, t, 1.0, x, ALU.add, ALU.mult)

            def gdn_prepare(i):
                n = i + 1
                for j, x in enumerate((qf, kf, vf)):
                    dve.wait_ge(proj_act, i * 5 + j + 1)
                    w = [pc[:, tap * 3 + j:tap * 3 + j + 1] for tap in range(4)]
                    if j == 0:
                        for tap in range(4):
                            do(dve.tensor_copy(pc[:, tap * 3:tap * 3 + 3], t2T[:, bass.ds(i + tap * 12, 3, step=4)]))
                    do(ts(x, cb[:, j, 0:S], w[0], None, ALU.mult))
                    yield
                    for tap in range(1, 3):
                        do(stt(x, cb[:, j, tap:tap + S], w[tap], x, ALU.mult, ALU.add))
                        yield
                    do.tell(stt(x, cb[:, j, 3:3 + S], w[3], x, ALU.mult, ALU.add), proj_vec, i * 3 + j + 1)
                    yield
                dve.wait_ge(proj_act, i * 5 + 5)
                do(silu(zf, th))
                yield
                for j, (x, t) in enumerate(((qf, S1), (kf, S2), (vf, S3))):
                    dve.wait_ge(d_in, i * 3 + j + 1)
                    do.tell(silu(x, t), lat_taken, i * 3 + j + 1)
                    yield
                do(dve.tensor_copy(Gp, Grow[:, i]))
                do(dve.tensor_copy(Bp, Brow[:, i]))
                yield
                do(tt(chunks(tmp), chunks(Gp), over_chunks(istack), ALU.mult))
                do(dve.tensor_reduce(gcol, chunks(tmp), AX.X, ALU.add))
                yield
                do(tt(chunks(tmp), chunks(Bp), over_chunks(istack), ALU.mult))
                do(dve.tensor_reduce(bcol, chunks(tmp), AX.X, ALU.add))
                yield
                do(dve.tensor_copy(glast, chunks(Gp)[:, :, C - 1]))
                do(tt(chunks(S1), chunks(Gp), gcol.unsqueeze(2).broadcast_to([P, NCH, C]), ALU.subtract))
                yield
                do(ts(S1, S1, 0.0, None, ALU.min))
                do.tell(tt(chunks(S2), glast.unsqueeze(2).broadcast_to([P, NCH, C]), chunks(Gp), ALU.subtract),
                        d_exp, n)
                yield
                dve.wait_ge(head_rs, i * 2 + 2)
                do.tell(tt(kf, kf, rs[:, 1], ALU.mult), fm_ready, i * 3 + 1)
                yield
                do(stt(qf, qf, float(C) ** -0.5, rs[:, 0], ALU.mult, ALU.mult))
                yield
                dve.wait_ge(gates_ready, n + 2)
                do.tell(tt(tmp, kf, S2, ALU.mult), fm_ready, i * 3 + 2)
                yield
                do(dve.tensor_copy(R1[:, :, 1], chunks(qf)))
                yield
                do(tt(RT, qf, Gp, ALU.mult))
                yield
                do(stt(R1[:, :, 0], chunks(kf), -1.0, chunks(Bp), ALU.mult, ALU.mult))
                yield
                do.tell(tt(chunks(S3), R1[:, :, 0], chunks(Gp), ALU.mult), fm_ready, i * 3 + 3)
                yield
                do(tt(chunks(S2), chunks(S1), over_chunks(inclT), ALU.mult))
                yield
                do.tell(tt(chunks(S1), chunks(S1), over_chunks(strictT), ALU.mult), r1_ready, n)

            def gdn_finish(i):
                yield
                dve.wait_ge(post_rs, i + 1)
                do(tt(th, PS[:, 4, :], rs[:, 0], ALU.mult))
                do.tell(stt(mix0[:, i], th, t2T[:, 59:60], gate_k, ALU.mult, ALU.mult), mix_ready, i + 1)

            pairs(GDN_PAIRS, 0, False, GDN_STEPS, gdn_prepare, gdn_finish)

            TWO_PI = 6.283185307179586
            C1 = 6.28125
            C2 = 0.0019350051879882812
            C3 = TWO_PI - C1 - C2
            inv = cc("invfreq")
            for t in range(TT):
                do(ts(ang[:, t, 1], inv, posT[:, t:t + 1], None, ALU.mult))
                do(dve.tensor_copy(ang[:, t, 0], ang[:, t, 1]))
            MAGIC = 12582912.0
            do(ts(rot[:, :, 1], ang[:, :, 1], 1.0 / TWO_PI, MAGIC, ALU.mult, ALU.add))
            do(ts(rot[:, :, 0], ang[:, :, 0], 1.0 / TWO_PI, 0.25, ALU.mult, ALU.add))
            do(ts(rot[:, :, 0], rot[:, :, 0], MAGIC, None, ALU.add))
            do(ts(rot, rot, -MAGIC, None, ALU.add))
            for const in (C1, C2, C3):
                do(stt(ang, rot, -const, ang, ALU.mult, ALU.add))
            do(ts(ang[:, :, 0], ang[:, :, 0], TWO_PI / 4, None, ALU.add))
            do(ts(ang, ang, 3.1415925, None, ALU.min))
            do.tell(ts(ang, ang, -3.1415925, None, ALU.max), ang_ready, 1)

            for j, x in enumerate((dq[:, 0], dq[:, 1], dkv)):
                dve.wait_ge(lat_out, j + 1)
                do.tell(dve.tensor_copy(x, PS[:, j, :]), lat_taken, 12 + j + 1)
            dve.wait_ge(lat_out, 4)
            do(dve.tensor_copy(krope, PS[:, 3, 0:TT * ROPE].rearrange("p (t r) -> p t r", t=TT)))
            dve.wait_ge(gains_bc, 1)
            do(dve.tensor_copy(gains, PS[:, 4, 0:2 * QK].rearrange("p (a r) -> p a r", a=2)))
            dve.wait_ge(lat_rs, 2)
            for x, g, r in ((dq[:, 0], 56, 0), (dq[:, 1], 57, 0), (dkv, 58, 1)):
                do(stt(x, x, t2T[:, g:g + 1], rs[:, r], ALU.mult, ALU.mult))
            do.tell(dve.tensor_copy(cond_t[:, 0], cond[:]), lat_ready, 1)
            dve.wait_ge(trig_ready, 1)
            for t in range(TT):
                dve.wait_ge(tok_copied, t + 1)
                do(dve.tensor_copy(kall[:, t, :, NOPE:QK], krope[:, t].unsqueeze(1).broadcast_to([P, 8, ROPE])))
                for a, x in ((0, qall[:, t]), (1, kall[:, t])):
                    do(tt(sqh, x, x, ALU.mult))
                    ins = dve.tensor_reduce(ssh[:, a, t * 8:(t + 1) * 8], sqh, AX.X, ALU.add)
                    if (t, a) != (TT - 1, 1):
                        do(ins)
            do.tell(ins, ssh_ready, 1)
            dve.wait_ge(rsh_ready, 1)
            rotate(do, dve, 0, qall)
            do.tell(dve.tensor_copy(cond_t[:, 0], cond[:]), heads_ready, 1)
            mod_finish(0, 1, 16, 48)

            def softmax(at, hd):
                for t in range(TT):
                    dve.wait_ge(score_out, at + t + 1)
                    sc = PS[:, 2 + t, 0:(t + 1) * P]
                    do(tt(PS[:, 2 + t, t * P:(t + 1) * P], PS[:, 2 + t, t * P:(t + 1) * P], causal, ALU.add))
                    do(dve.tensor_reduce(negm[:, t:t + 1], sc, AX.X, ALU.max))
                    do.tell(ts(negm[:, t:t + 1], negm[:, t:t + 1], -float(QK) ** -0.5, None, ALU.mult),
                            max_ready, at + t + 1)
                for t in range(TT):
                    dve.wait_ge(exp_ready, at + t + 1)
                    do(dve.reciprocal(rden[:, t:t + 1], den[:, t:t + 1]))
                    ins = ts(prob[:, t, 0:(t + 1) * P], prob[:, t, 0:(t + 1) * P], rden[:, t:t + 1], None, ALU.mult)
                    if t == TT - 1:
                        do.tell(ins, prob_ready, hd)
                    else:
                        do(ins)

            def attend(i, last=False):
                for a in range(2):
                    hd = i * 2 + a + 1
                    if not (last and a == 1):
                        softmax(i * 8 + a * 4 + 4, hd + 1)
                    dve.wait_ge(o_out, hd + 1)
                    do.tell(dve.tensor_copy(mix0[a * C:(a + 1) * C, i + 4], PS[a * C:(a + 1) * C, 6 + a, :]),
                            o_ready, hd)
            softmax(0, 1)
            do.loop(3, 30, attend)
            attend(3, True)

            def residual(name, n, gate):
                def body(i):
                    for j in range(4):
                        dve.wait_ge(tile_out, i * 4 + TIL[name] + j + 1)
                        x = xT[:, i * 4 + j]
                        do.tell(stt(x, PS[:, j, :], gate_cols[:, bass.ds(i * 4 + j, 1)], x, ALU.mult, ALU.add),
                                tile_taken, i * 4 + TIL[name] + j + 5)
                do(dve.tensor_copy(gate_cols[:], modT[:, gate:gate + KT]))
                do.loop(n // 4, 0, body)

            def relu2(name):
                def body(i):
                    for j in range(4):
                        dve.wait_ge(tile_out, i * 4 + TIL[name] + j + 1)
                        do(ts(tmp_r[:, j % 2], PS[:, j, :], 0.0, None, ALU.max))
                        do.tell(tt(hid[:, i * 4 + j], tmp_r[:, j % 2], PS[:, j, :], ALU.mult),
                                tile_taken, i * 4 + TIL[name] + j + 5)
                do.loop(FT // 4, 4, body)

            residual("o0", KT, GATE[0])
            norm(1)
            relu2("up0")
            residual("down0", KT, GATE[1])
            mod_finish(1, 2, 0, 48)
            norm(2)

            dve.wait_ge(h_ready, 3 * KT)
            do(ts(xx[:, :, 0:1], hT[:, :, 0:1], -1.0, None, ALU.mult))
            for k in range(KT):
                do(tt(xx[:, k, 1:S], hT[:, k, 0:S - 1], hT[:, k, 1:S], ALU.subtract))
            for q, (j, x) in enumerate(((1, xr), (4, xk), (5, xv), (0, xr), (2, xk), (3, xv))):
                if q >= 3:
                    dve.wait_ge(lora_out, (1, 2, 4)[q - 3])
                for k in range(KT):
                    col = t1T[:, j * KT + k:j * KT + k + 1]
                    do.tell(stt(x[:, k], xx[:, k], col, hT[:, k], ALU.mult, ALU.add), xmix_ready, q * KT + k + 1)
            dve.wait_ge(lora_ready, 2)
            for j, r in ((2, P), (3, 32)):
                dve.wait_ge(proj_vec, 12 + j - 1)
                do.tell(ts(lora[0:r, j], lora[0:r, j], 0.5, 0.5, ALU.mult, ALU.add), lora_ready, j + 1)
            dve.wait_ge(lora_out, 4)
            do(dve.memset(Hs[:, 0], 0.0))

            def rwkv_prepare(i):
                n = i + GDN_PAIRS + 1
                for a in range(5):
                    ins = dve.tensor_copy(pc[:, a:a + 1], t1T[:, bass.ds(i + 48 + a * KT, 1)])
                    if a < 4:
                        do(ins)
                do.tell(ins, d_exp, n)
                kkc, kac, rkc = (pc[:, b:b + 1] for b in range(2, 5))
                dve.wait_ge(proj_act, 20 + i * 6 + 2)
                do(ts(tmp, kf, kkc, None, ALU.mult))
                yield
                do.tell(tt(sq[:, 0], tmp, tmp, ALU.mult), head_sq, 8 + i * 2 + 1)
                yield
                dve.wait_ge(proj_act, 20 + i * 6 + 5)
                do(ts(S1, S1, -0.5 * DECAY, -0.5 * DECAY, ALU.mult, ALU.add))
                do(ts(S2, S2, 0.5, 0.5, ALU.mult, ALU.add))
                yield
                do(ts(th, S2, -1.0, kac, ALU.add, ALU.mult))
                yield
                do(stt(kf, th, 1.0, kf, ALU.add, ALU.mult))
                yield
                do.tell(stt(sq[:, 1], qf, rkc, kf, ALU.mult, ALU.mult), head_sq, 8 + i * 2 + 2)
                yield
                do(dve.tensor_tensor_scan(S3, reset, S1, 0.0, ALU.mult, ALU.add))
                yield
                do.tell(tt(S1, S3, S1, ALU.subtract), d_in, 12 + i + 1)
                yield
                dve.wait_ge(head_ss, 4 + i * 2 + 2)
                do.tell(tt(post, PS[:, 4, :], vf, ALU.mult), bonus_used, i + 1)
                yield
                dve.wait_ge(head_rs, 8 + i + 1)
                do(tt(tmp, tmp, rs[:, 0], ALU.mult))
                yield
                do(tt(th, tmp, S2, ALU.mult))
                yield
                dve.wait_ge(gates_ready, GDN_PAIRS + 2 + i + 1)
                do.tell(tt(S2, th, RT, ALU.mult), fm_ready, 12 + i * 3 + 1)
                yield
                do(tt(R1[:, :, 1], chunks(qf), chunks(S3), ALU.mult))
                yield
                do.tell(tt(S3, kf, RT, ALU.mult), fm_ready, 12 + i * 3 + 2)
                yield
                do.tell(stt(R1[:, :, 0], chunks(tmp), -1.0, chunks(S1), ALU.mult, ALU.mult),
                        fm_ready, 12 + i * 3 + 3)
                do.tell(ts(te[:, 1, 0:1], pc[:, 0:1], 1.0, None, ALU.mult), r1_ready, n)

            def rwkv_finish(i):
                n = i + GDN_PAIRS + 1
                do(dve.tensor_copy(pc[:, 8:9], t1T[:, bass.ds(i + T1["ln_g"], 1)]))
                do(dve.tensor_copy(pc[:, 9:10], t1T[:, bass.ds(i + T1["ln_b"], 1)]))
                dve.wait_ge(y_out, n)
                do.tell(dve.tensor_copy(sq[:, 0], PS[:, 4, :]), post_sq, 4 + i * 2 + 1)
                dve.wait_ge(post_ss, 4 + i * 2 + 1)
                do(stt(tmp, PS[:, 5, :], -1.0 / C, sq[:, 0], ALU.mult, ALU.add))
                do.tell(tt(sq[:, 1], tmp, tmp, ALU.mult), post_sq, 4 + i * 2 + 2)
                yield
                dve.wait_ge(post_rs, n)
                do(tt(tmp, tmp, rs[:, 1], ALU.mult))
                do(ts(tmp, tmp, pc[:, 8:9], pc[:, 9:10], ALU.mult, ALU.add))
                do(tt(tmp, tmp, bonus_k, ALU.add))
                do.tell(tt(hT[:, i], tmp, gate_k, ALU.mult), mix_ready, n)

            pairs(RWKV_PAIRS, GDN_PAIRS, True, RWKV_STEPS, rwkv_prepare, rwkv_finish)
            residual("o1", KT, GATE[0])
            norm(3)
            relu2("up1")
            residual("down1", KT, GATE[1])

        @block.scalar
        def _(act):
            do = Steps(act, act_)
            fn = act.activation
            act.wait_ge(tabs_ready, 1)
            do.tell(fn(cond_t[:, 1], cond_t[:, 0], ACT.Tanh), cond_tanh, 1)
            for k in range(KT):
                act.wait_ge(x_T, k + 1)
                do.tell(fn(xT[:, k], PS[:, 4 + k % 2, :], ACT.Copy), x_ready, k + 1)

            def rsqrt(o, ps, scale, eps, sem_, value):
                do(fn(o, ps, ACT.Ln, scale=scale, bias=eps))
                do.tell(fn(o, o, ACT.Exp, scale=-0.5), sem_, value)

            def norm(idx):
                for k in range(KT):
                    if idx:
                        act.wait_ge(tile_taken, X_DONE[idx] - KT + k + 1)
                    if k >= 2:
                        act.wait_ge(sq_used, idx * KT + k - 1)
                    do.tell(fn(sq[:, k % 2], xT[:, k], ACT.Square), sq_ready, idx * KT + k + 1)
                act.wait_ge(sq_used, idx * KT + KT)
                rsqrt(rs[:, 0], PS[:, 6, :], 1.0 / D, eps6, rstd_ready, idx + 1)
                for k in range(KT):
                    act.wait_ge(hx_ready, idx * KT + k + 1)
                    at = SHIFT[idx % 2] + k
                    do.tell(fn(hT[:, k], hT[:, k], ACT.Identity, bias=modT[:, at:at + 1]), h_ready, idx * KT + k + 1)

            norm(0)
            act.wait_ge(rows_e, 1)
            do(fn(rE, rE, ACT.Exp))
            do(fn(small8[:, 2:3], small8[:, 1:2], ACT.Exp))
            do.tell(fn(rE, rE, ACT.Ln, bias=one[0:8]), rows_l, 1)
            do.tell(fn(rB, PS[0:8, 1, :], ACT.Tanh, scale=0.5), rows_l, 2)
            for p in range(GDN_PAIRS):
                act.wait_ge(rows_bc, 2 if p == GDN_PAIRS - 1 else 1)
                ins = fn(Grow[:, p], PS[:, 2 * (p % 3), :], ACT.Copy)
                do(ins)
                ins = fn(Brow[:, p], PS[:, 2 * (p % 3) + 1, :], ACT.Copy)
                if p in (0, GDN_PAIRS - 1):
                    do.tell(ins, gates_ready, 1 if p == 0 else 2)
                else:
                    do(ins)

            def tokens_major(n, rw):
                q0 = n - GDN_PAIRS if rw else n
                first = 8 + q0 * 3 - 2 if rw else q0 * 2 - 1
                act.wait_ge(tok_out, first)
                do.tell(fn(btok, bank(2), ACT.Copy), tok_taken, 3 * n - 2)
                if rw:
                    act.wait_ge(tok_out, first + 1)
                    do.tell(fn(ktok, bank(3), ACT.Copy), tok_taken, 3 * n - 1)
                    act.wait_ge(vs_out, n)
                    do.tell(fn(Vs, bank(1), ACT.Copy), vs_ready, q0)

            def last_tokens(n, rw):
                act.wait_ge(tok_out, 8 + (n - GDN_PAIRS) * 3 if rw else 2 * n)
                if rw:
                    do.tell(fn(atok, bank(2), ACT.Copy), tok_taken, 3 * n)
                else:
                    do.tell(fn(atok[:, 0:4], bank(2)[:, 0:4], ACT.Copy), tok_taken, 3 * n - 1)
                    do.tell(fn(atok[:, 4:8], bank(2)[:, 4:8], ACT.Copy), tok_taken, 3 * n)

            def pair(i, base, rw, copies, prepare, finish, follow, nxt):
                n = i + base + 1
                if nxt:
                    for _ in prepare(i + 1, n):
                        pass
                act.wait_ge(wt_out, n)
                do(fn(WTs, bank(1), ACT.Copy))
                act.wait_ge(u0_out, n)
                do.tell(fn(U, bank(0), ACT.Copy), u0_ready, n)
                if follow:
                    copies(i + 2, 0)
                    copies(i + 2, 1)
                finishing = finish(i)
                next(finishing)
                if nxt:
                    tokens_major(n + 1, rw)
                for _ in finishing:
                    pass
                if nxt:
                    last_tokens(n + 1, rw)
                act.wait_ge(mix_ready, n)

            def pairs(count, base, rw, steps, copies, prepare, finish):
                for j in range(3):
                    copies(0, j)
                for _ in prepare(0, None):
                    pass
                for j in range(2):
                    copies(1, j)
                tokens_major(base + 1, rw)
                last_tokens(base + 1, rw)
                do.loop(count - 2, steps, lambda i: pair(i, base, rw, copies, prepare, finish, True, True))
                pair(count - 2, base, rw, copies, prepare, finish, False, True)
                pair(count - 1, base, rw, copies, prepare, finish, False, False)

            def gdn_copy(pair_, j):
                act.wait_ge(proj_out, pair_ * 4 + j + 5)
                do.tell(fn(cb[:, j, 3:3 + S], PS[:, 6 + j % 2, :], ACT.Copy), proj_act, pair_ * 5 + j + 1)

            def gdn_prepare(i, before):
                if before is not None:
                    gdn_copy(i, 2)
                    yield
                    act.wait_ge(kept, before)
                act.wait_ge(proj_out, i * 4 + 8)
                do.tell(fn(zf, PS[:, 7, :], ACT.Copy, scale=0.5), proj_act, i * 5 + 4)
                do.tell(fn(th, PS[:, 7, :], ACT.Tanh, scale=0.5), proj_act, i * 5 + 5)
                yield
                for j, (x, t) in enumerate(((qf, S1), (kf, S2), (vf, S3))):
                    act.wait_ge(proj_vec, i * 3 + j + 1)
                    do.tell(fn(t, x, ACT.Tanh), d_in, i * 3 + j + 1)
                    yield
                for j, x in enumerate((qf, kf)):
                    act.wait_ge(lat_taken, i * 3 + j + 1)
                    do.tell(fn(sq[:, j], x, ACT.Square), head_sq, i * 2 + j + 1)
                    yield
                act.wait_ge(head_ss, i + 1)
                for j in range(2):
                    do(fn(rs[:, j], PS[:, 4 + j, :], ACT.Ln, bias=eps12))
                yield
                for j in range(2):
                    do.tell(fn(rs[:, j], rs[:, j], ACT.Exp, scale=-0.5), head_rs, i * 2 + j + 1)
                yield
                act.wait_ge(d_exp, i + 1)
                do(fn(S1, S1, ACT.Exp))
                do(fn(S2, S2, ACT.Exp))
                do(fn(egC, glast, ACT.Exp))
                do.tell(fn(Gp, Gp, ACT.Exp), gates_ready, i + 3)

            def gdn_finish(i):
                act.wait_ge(y_out, i + 1)
                do.tell(fn(sq[:, 0], PS[:, 4, :], ACT.Square), post_sq, i + 1)
                yield
                act.wait_ge(post_ss, i + 1)
                rsqrt(rs[:, 0], PS[:, 5, :], 1.0 / C, eps6, post_rs, i + 1)

            act.wait_ge(cb_zeroed, 1)
            pairs(GDN_PAIRS, 0, False, GDN_ACT_STEPS, gdn_copy, gdn_prepare, gdn_finish)

            act.wait_ge(ang_ready, 1)
            do.tell(fn(trig, ang, ACT.Sin), trig_ready, 1)
            for j, x in enumerate((dq[:, 0], dq[:, 1], dkv)):
                act.wait_ge(lat_taken, 12 + j + 1)
                if j == 2:
                    act.wait_ge(lat_ss, 1)
                do.tell(fn(sq[:, j % 2], x, ACT.Square), lat_sq, j + 1)
            act.wait_ge(lat_ss, 2)
            rsqrt(rs[:, 0], PS[:, 5, :], 1.0 / 256, eps6, lat_rs, 1)
            act.wait_ge(lat_ss, 3)
            rsqrt(rs[:, 1], PS[:, 6, :], 1.0 / 128, eps6, lat_rs, 2)
            for t in range(TT):
                act.wait_ge(tok_proj, t + 1)
                for j in range(2):
                    do(fn(qall[:, t, j * 4:j * 4 + 4], PS[:, j, 0:384].rearrange("p (h d) -> p h d", h=4), ACT.Copy))
                kv = [PS[:, 2 + j, :].rearrange("p (h d) -> p h d", h=4) for j in range(2)]
                for j in range(2):
                    do(fn(kall[:, t, j * 4:j * 4 + 4, 0:NOPE], kv[j][:, :, 0:NOPE], ACT.Copy))
                    ins = fn(vall[:, t, j * 4:j * 4 + 4], kv[j][:, :, NOPE:P], ACT.Copy)
                    if j == 0:
                        do(ins)
                do.tell(ins, tok_copied, t + 1)
            act.wait_ge(ssh_ready, 1)
            do(fn(ssh, ssh, ACT.Ln, scale=1.0 / QK, bias=eps6))
            do.tell(fn(ssh, ssh, ACT.Exp, scale=-0.5), rsh_ready, 1)

            def copy_qk(hd):
                act.wait_ge(qkT_out, hd)
                do(fn(qhT[0:QK], PS[0:QK, 0, :], ACT.Copy))
                do.tell(fn(khT[0:QK], PS[0:QK, 1, :], ACT.Copy), qkT_ready, hd)

            def exponentials(at):
                for t in range(TT):
                    act.wait_ge(max_ready, at + t + 1)
                    do.tell(fn(prob[:, t, 0:(t + 1) * P], PS[:, 2 + t, 0:(t + 1) * P], ACT.Exp,
                               bias=negm[:, t:t + 1], scale=float(QK) ** -0.5, accum_out=den[:, t:t + 1]),
                            exp_ready, at + t + 1)

            def attend(i, last=False):
                for a in range(2):
                    hd = i * 2 + a + 1
                    follow = not (last and a == 1)
                    if follow:
                        copy_qk(hd + 1)
                    act.wait_ge(pT_out, hd)
                    for kt in range(TT):
                        ins = fn(probT[:, kt, kt * P:S], PS[:, 2 + kt, kt * P:S], ACT.Copy)
                        if kt < TT - 1:
                            do(ins)
                    do.tell(ins, pT_ready, hd)
                    if follow:
                        exponentials(i * 8 + a * 4 + 4)
            copy_qk(1)
            exponentials(0)
            do.loop(3, 8, attend)
            attend(3, True)
            norm(1)
            norm(2)

            for j, (m_, f) in enumerate(((64, ACT.Tanh), (64, ACT.Copy), (P, ACT.Tanh), (32, ACT.Tanh))):
                act.wait_ge(lora_out, j + 1)
                ins = fn(lora[0:m_, j], PS[0:m_, j, :], f, scale=0.5 if j >= 2 else 1.0)
                if j < 2:
                    do.tell(ins, lora_ready, j + 1)
                else:
                    do.tell(ins, proj_vec, 12 + j - 1)

            def rwkv_copy(pair_, j):
                act.wait_ge(proj_out, 20 + pair_ * 3 + j + 1)
                if not (isinstance(pair_, int) and pair_ == 0):
                    act.wait_ge(r1_ready, pair_ + GDN_PAIRS)
                do.tell(fn((qf, kf, vf)[j], PS[:, 6 + j % 2, :], ACT.Copy), proj_act, 20 + pair_ * 6 + j + 1)

            def rwkv_prepare(i, before):
                w0c, a0c = pc[:, 0:1], pc[:, 1:2]
                if before is not None:
                    rwkv_copy(i, 2)
                    yield
                act.wait_ge(d_exp, i + GDN_PAIRS + 1)
                act.wait_ge(low_out, i * 3 + 4)
                do.tell(fn(S1, PS[:, 4, :], ACT.Tanh, scale=0.5, bias=w0c), proj_act, 20 + i * 6 + 4)
                yield
                act.wait_ge(low_out, i * 3 + 5)
                do.tell(fn(S2, PS[:, 5, :], ACT.Tanh, scale=0.5, bias=a0c), proj_act, 20 + i * 6 + 5)
                yield
                if before is not None:
                    act.wait_ge(kept, before)
                act.wait_ge(low_out, i * 3 + 6)
                do.tell(fn(zf, PS[:, 4, :], ACT.Copy), proj_act, 20 + i * 6 + 6)
                yield
                act.wait_ge(head_ss, 4 + i * 2 + 1)
                rsqrt(rs[:, 0], PS[:, 5, :], 1.0, eps12, head_rs, 8 + i + 1)
                yield
                act.wait_ge(d_in, 12 + i + 1)
                do(fn(RT, S3, ACT.Exp, scale=-1.0))
                do(fn(egC, chunks(S3)[:, :, C - 1], ACT.Exp))
                yield
                do(fn(S3, S3, ACT.Exp))
                do.tell(fn(S1, S1, ACT.Exp), gates_ready, GDN_PAIRS + 2 + i + 1)

            def rwkv_finish(i):
                yield
                act.wait_ge(post_ss, 4 + i * 2 + 2)
                rsqrt(rs[:, 1], PS[:, 4, :], 1.0 / C, epsgn, post_rs, i + GDN_PAIRS + 1)

            pairs(RWKV_PAIRS, GDN_PAIRS, True, RWKV_ACT_STEPS, rwkv_copy, rwkv_prepare, rwkv_finish)
            norm(3)
            for q in range(2 * TT):
                t, hf = divmod(q, 2)
                act.wait_ge(xo_T, q + 1)
                if t >= 2:
                    act.wait_ge(out_landed[t % 2], 16)
                do.tell(fn(xout[:, t % 2, hf * S:(hf + 1) * S], PS[:, q % 2, :], ACT.Copy), xo_ready, q + 1)

        @block.gpsimd
        def _(pool):
            do = Steps(pool, pool_)

            def copy(dst, src):
                pool.wait_ge(cst_landed, 16)
                return pool.tensor_copy(dst, src)

            pool.wait_ge(gates_ready, 2)

            def modulation(wm, i, blocks, first, ring, acc, fills, width):
                step = blocks * width

                def fetch(b):
                    col = bass.ds(i * step + first + b * width, width)
                    pool.dma_start(ring[:, b % 2], wm[:, :, col]).then_inc(pmw_landed[b % 2], 16)
                fetch(0)
                fetch(1)
                for b in range(blocks):
                    pool.wait_ge(pmw_landed[b % 2], i * (8 * blocks) + 16 * (fills + b // 2 + 1))
                    w = ring[:, b % 2]
                    do(pool.tensor_tensor(w, w, cond[:].unsqueeze(2).broadcast_to([P, KT, width]), ALU.mult))
                    do(pool.tensor_tensor(w[:, 0:4], w[:, 0:4], w[:, 4:8], ALU.add))
                    do(pool.tensor_tensor(w[:, 0:2], w[:, 0:2], w[:, 2:4], ALU.add))
                    do(pool.tensor_tensor(acc[:, bass.ds(i * step + b * width, width)], w[:, 0], w[:, 1], ALU.add))
                    if b + 2 < blocks:
                        fetch(b + 2)

            def view(layer):
                return I["w_mod"][layer].rearrange("(k p) n -> p k n", p=P)

            do.loop(GDN_PAIRS, 32, lambda i: modulation(view(0), i, 8, 2048, mwring2, macc2, 0, P))
            do.tell(pool.memset(mwring2[:, 0, 0], 0.0), macc_ready, 2)

            pool.wait_ge(rsh_ready, 1)
            rotate(do, pool, 1, kall)
            pool.wait_ge(heads_ready, 1)

            def slices(hd, slot):
                do(copy(qh, qall[:, :, hd - 1]))
                do(copy(kh, kall[:, :, hd - 1]))
                do.tell(copy(vh[slot], vall[:, :, hd - 1]), hslice, hd)

            def next_slices(i, last=False):
                for a in range(2):
                    hd = i * 2 + a + 1
                    if not (last and a == 1):
                        pool.wait_ge(qkT_out, hd)
                        pool.wait_ge(o_out, hd)
                        slices(hd + 1, 1 - a)
            slices(1, 0)
            do.loop(3, 4, next_slices)
            next_slices(3, True)
            pool.wait_ge(mod_ready, 2)
            pool.wait_ge(tile_taken, 4 + 8)
            do.loop(6, 16, lambda i: modulation(view(1), i, 4, 0, mwring1, macc1, 16, 256))
            do.tell(pool.memset(mwring1[:, 0, 0], 0.0), macc_ready, 3)


def constants():
    import numpy as np

    t = np.zeros((P, NCONST), np.float32)

    def put(name, a):
        at, n = CONST_COLS[name]
        t[:a.shape[0], at:at + n] = a
    j, i = np.meshgrid(np.arange(P) % C, np.arange(C), indexing="ij")
    put("ident", np.eye(P))
    put("ones", np.ones((P, P)))
    put("blk", np.kron(np.eye(2), np.ones((C, C))))
    put("istack", j == i)
    put("strictT", j < i)
    put("inclT", j <= i)

    def doubling(r, c, n):
        return (r >> n == c >> n) & ((r >> (n - 1)) % 2 == 1) & ((c >> (n - 1)) % 2 == 0)
    put("level", np.concatenate([doubling(j, i, n) for n in range(1, LEVELS + 1)], 1))
    put("level1T", doubling(i, j, 1))
    a, b = np.meshgrid(np.arange(P), np.arange(P), indexing="ij")
    put("causal", np.where(b <= a, 0.0, -1e30))
    put("reset", np.tile((np.arange(S) % C != 0).astype(np.float32), (P, 1)))
    put("invfreq", np.tile(np.float32(10000.0) ** (-np.arange(0, ROPE, 2, dtype=np.float32) / ROPE), (P, 1)))
    heads = np.zeros((8, GDN_PAIRS * P))
    for h in range(8):
        heads[h, h * C:(h + 1) * C] = 1
    put("headsel", heads)
    put("eps", np.tile(np.array([EPS, L2_EPS, GN_EPS, 1.0]), (P, 1)))
    return t


def kernel(**inputs):
    import numpy as _np
    import concourse.bacc as _bacc
    from concourse import mybir as _mybir
    from concourse.bass_utils import run_bass_kernel_spmd as _run

    nc = _bacc.Bacc("TRN2", target_bir_lowering=False, num_devices=1)
    arrays, args = {}, {}
    for name, a in dict(inputs, const=constants()).items():
        a = _np.ascontiguousarray(a)
        arrays[f"in_{name}_dram"] = a
        args[name] = nc.dram_tensor(f"in_{name}_dram", a.shape, _mybir.dt.from_np(a.dtype), kind="ExternalInput").ap()
    out = nc.dram_tensor("out_0_dram", (1, S, D), F32, kind="ExternalOutput").ap()
    build(nc, args, out)
    r = _run(nc, [arrays], core_ids=[0])
    return r.results[0]["out_0_dram"]
```
